# Optimizing a Trainium2 kernel written in Bass

```python
import math
import jax, jax.numpy as jnp
from jax import lax
import numpy as np

D_MODEL = 2048
BATCH = 1
SEQ = 256
DEPTH = 1
DEC_BATCH = 1
DEC_SEQ = 64
PAST_LEN = 512

CHUNK = 64
EPS = 1e-6
F_FLOOR = 1e-30
D_MIX = D_MODEL
SSD_WIDTH = D_MIX // 2
SSD_HEAD_DIM = 64
SSD_HEADS = SSD_WIDTH // SSD_HEAD_DIM
SSD_GROUPS = 2
SSD_STATE = 64
CONV_WIDTH = 4
CONV_CH = SSD_WIDTH + 2 * SSD_GROUPS * SSD_STATE
HG_WIDTH = D_MIX // 4
HG_HEADS = 4
HG_HEAD_DIM = HG_WIDTH // HG_HEADS
HG_KEY_DIM = 128
HG_KEY_WIDTH = HG_HEADS * HG_KEY_DIM
S5_WIDTH = D_MIX - SSD_WIDTH - HG_WIDTH
S5_GROUP_CH = 16
S5_GROUPS = S5_WIDTH // S5_GROUP_CH
S5_STATE = 64
S5_MIN_NEG = -1e-4
N_EGROUPS = 4
EXPERTS_PER_GROUP = 8
N_EXPERTS = N_EGROUPS * EXPERTS_PER_GROUP
EXPERT_TOPK = 2
D_EXPERT = D_MODEL // 8
IN_SIZES = (SSD_WIDTH, CONV_CH, SSD_HEADS, HG_KEY_WIDTH, HG_KEY_WIDTH, HG_WIDTH, HG_WIDTH, S5_WIDTH)
IN_COLS = sum(IN_SIZES)
F32 = jnp.float32

kernel_name = 'hybrid_ssd_hgrn2_s5_hmoe_stream_step'

def rmsnorm(x, g):
    xf = x.astype(F32)
    y = xf * lax.rsqrt(jnp.mean(xf * xf, axis=-1, keepdims=True) + EPS)
    return (y * g.astype(F32)).astype(x.dtype)

def causal_conv(u, w, b, buf):
    t = u.shape[1]
    full = jnp.concatenate([buf.astype(u.dtype), u], axis=1)
    out = b
    for j in range(CONV_WIDTH):
        out = out + full[:, j:j + t] * w[j]
    return out, full[:, -(CONV_WIDTH - 1):]

def chunk_gla(q, k, v, log_a, s0):
    bsz, t, nh, _ = q.shape
    dv = v.shape[-1]
    ln = min(CHUNK, t)
    nc = t // ln

    def blocks(a):
        a = a.astype(F32).reshape(bsz, nc, ln, nh, a.shape[-1])
        return jnp.moveaxis(a, 1, 0)

    causal = jnp.tril(jnp.ones((ln, ln), dtype=bool))
    scalar_decay = log_a.shape[-1] == 1

    def step(s, inp):
        qc, kc, vc, lc = inp
        b = jnp.cumsum(lc, axis=1)
        diff = b[:, :, None] - b[:, None, :]
        dec = jnp.where(causal[None, :, :, None, None], jnp.exp(jnp.minimum(diff, 0.0)), 0.0)
        if scalar_decay:
            scores = jnp.einsum('bthk,bshk->btsh', qc, kc) * dec[..., 0]
        else:
            scores = jnp.einsum('bthk,bshk,btshk->btsh', qc, kc, dec)
        intra = jnp.einsum('btsh,bshv->bthv', scores, vc)
        inter = jnp.einsum('bthk,bhkv->bthv', qc * jnp.exp(b), s)
        b_last = b[:, -1]
        kd = kc * jnp.exp(b_last[:, None] - b)
        s_new = s * jnp.exp(b_last)[..., None] + jnp.einsum('bshk,bshv->bhkv', kd, vc)
        return s_new, intra + inter

    s_fin, ys = lax.scan(step, s0.astype(F32), (blocks(q), blocks(k), blocks(v), blocks(log_a)))
    y = jnp.moveaxis(ys, 0, 1).reshape(bsz, t, nh, dv)
    return y, s_fin

def s5_scan(u, lam_re, lam_im, log_dt, b_re, b_im, c_re, c_im, d, x0_re, x0_im):
    uf = u.astype(F32)
    dt = jnp.exp(log_dt.astype(F32))[:, None]
    lr = jnp.minimum(lam_re.astype(F32), S5_MIN_NEG)
    li = lam_im.astype(F32)
    mag = jnp.exp(lr * dt)
    ar = mag * jnp.cos(li * dt)
    ai = mag * jnp.sin(li * dt)
    den = lr * lr + li * li
    nr = ar - 1.0
    cr = (nr * lr + ai * li) / den
    ci = (ai * lr - nr * li) / den
    br = b_re.astype(F32)
    bi = b_im.astype(F32)
    bbar_re = cr[..., None] * br - ci[..., None] * bi
    bbar_im = cr[..., None] * bi + ci[..., None] * br
    bu_re = jnp.einsum('btgj,gpj->btgp', uf, bbar_re)
    bu_im = jnp.einsum('btgj,gpj->btgp', uf, bbar_im)
    if x0_re is not None:
        x0r = x0_re.astype(F32)
        x0i = x0_im.astype(F32)
        bu_re = bu_re.at[:, 0].add(ar * x0r - ai * x0i)
        bu_im = bu_im.at[:, 0].add(ar * x0i + ai * x0r)
    a_re = jnp.broadcast_to(ar, bu_re.shape)
    a_im = jnp.broadcast_to(ai, bu_im.shape)

    def combine(e1, e2):
        a1r, a1i, b1r, b1i = e1
        a2r, a2i, b2r, b2i = e2
        return (a1r * a2r - a1i * a2i, a1r * a2i + a1i * a2r,
                a2r * b1r - a2i * b1i + b2r, a2r * b1i + a2i * b1r + b2i)

    _, _, xr, xi = lax.associative_scan(combine, (a_re, a_im, bu_re, bu_im), axis=1)
    y = (jnp.einsum('btgp,gjp->btgj', xr, c_re.astype(F32))
         - jnp.einsum('btgp,gjp->btgj', xi, c_im.astype(F32)))
    y = y + d.astype(F32).reshape(S5_GROUPS, S5_GROUP_CH) * uf
    return y, xr[:, -1], xi[:, -1]

def mixer(h, st, P, l, lb):
    bsz, t, _ = h.shape
    proj = h @ P['w_in'][l]
    offs = [int(o) for o in np.cumsum(IN_SIZES)[:-1]]
    z, xbc, dt_raw, hq, hf, hi, hgate, u = jnp.split(proj, offs, axis=-1)
    if st is None:
        conv_buf = jnp.zeros((bsz, CONV_WIDTH - 1, CONV_CH), h.dtype)
        s_ssd = jnp.zeros((bsz, SSD_HEADS, SSD_STATE, SSD_HEAD_DIM), F32)
        s_hg = jnp.zeros((bsz, HG_HEADS, HG_KEY_DIM, HG_HEAD_DIM), F32)
        s5_r = None
        s5_i = None
    else:
        conv_buf, s_ssd, s_hg, s5_r, s5_i = st
    xbc_c, conv_new = causal_conv(xbc, P['conv_w'][l], P['conv_b'][l], conv_buf)
    xbc_c = jax.nn.silu(xbc_c)
    xs, bs, cs = jnp.split(xbc_c, [SSD_WIDTH, SSD_WIDTH + SSD_GROUPS * SSD_STATE], axis=-1)
    xs = xs.reshape(bsz, t, SSD_HEADS, SSD_HEAD_DIM).astype(F32)
    rep = SSD_HEADS // SSD_GROUPS
    bs = jnp.repeat(bs.reshape(bsz, t, SSD_GROUPS, SSD_STATE), rep, axis=2)
    cs = jnp.repeat(cs.reshape(bsz, t, SSD_GROUPS, SSD_STATE), rep, axis=2)
    dt = jax.nn.softplus(dt_raw.astype(F32) + P['ssd_dt_bias'][l].astype(F32))
    a = -jnp.exp(P['ssd_a_log'][l].astype(F32))
    y_a, ssd_new = chunk_gla(cs, bs, xs * dt[..., None], (dt * a)[..., None], s_ssd)
    y_a = y_a + P['ssd_d'][l].astype(F32)[:, None] * xs
    y_a = y_a.reshape(bsz, t, SSD_WIDTH) * jax.nn.silu(z.astype(F32))
    out_a = rmsnorm(y_a, P['ssd_norm_g'][l])
    hf32 = hf.astype(F32)
    f_gate = lb + (1.0 - lb) * jax.nn.sigmoid(hf32)
    log_f = jnp.log(jnp.maximum(f_gate, F_FLOOR))
    k_hg = (1.0 - lb) * jax.nn.sigmoid(-hf32)
    def heads(arr, dd):
        return arr.reshape(bsz, t, HG_HEADS, dd)
    o_b, hg_new = chunk_gla(heads(hq, HG_KEY_DIM), heads(k_hg, HG_KEY_DIM),
                            heads(hi, HG_HEAD_DIM), heads(log_f, HG_KEY_DIM), s_hg)
    o_b = rmsnorm(o_b, P['hgrn_norm_g'][l]).reshape(bsz, t, HG_WIDTH)
    out_b = o_b * jax.nn.silu(hgate.astype(F32))
    y_c, s5r_new, s5i_new = s5_scan(u.reshape(bsz, t, S5_GROUPS, S5_GROUP_CH),
                                    P['s5_lam_re'][l], P['s5_lam_im'][l], P['s5_log_dt'][l],
                                    P['s5_b_re'][l], P['s5_b_im'][l], P['s5_c_re'][l], P['s5_c_im'][l],
                                    P['s5_d'][l], s5_r, s5_i)
    g_c = jax.nn.gelu(y_c.reshape(bsz, t, S5_WIDTH))
    out_c = g_c * jax.nn.sigmoid(g_c @ P['s5_w_glu'][l].astype(F32) + P['s5_b_glu'][l].astype(F32))
    merged = jnp.concatenate([out_a, out_b, out_c], axis=-1).astype(h.dtype)
    mix = merged @ P['w_out'][l]
    return mix, (conv_new, ssd_new, hg_new, s5r_new, s5i_new)

def hmoe(h, P, l):
    bsz, t, d = h.shape
    xf = h.reshape(bsz * t, d)
    lg = (xf @ P['w_router_group'][l] + P['b_router_group'][l]).astype(F32)
    gi = jnp.argmax(lg, axis=-1)
    p_grp = jnp.max(jax.nn.softmax(lg, axis=-1), axis=-1, keepdims=True)
    le = (xf @ P['w_router_expert'][l] + P['b_router_expert'][l]).astype(F32)
    le = le.reshape(-1, N_EGROUPS, EXPERTS_PER_GROUP)
    le_g = jnp.sum(le * jax.nn.one_hot(gi, N_EGROUPS, dtype=F32)[:, :, None], axis=1)
    top_v, top_i = lax.top_k(le_g, EXPERT_TOPK)
    wts = jax.nn.softmax(top_v, axis=-1) * p_grp
    e_idx = gi[:, None] * EXPERTS_PER_GROUP + top_i
    comb = jnp.einsum('nk,nke->ne', wts, jax.nn.one_hot(e_idx, N_EXPERTS, dtype=F32)).astype(h.dtype)
    hg = jnp.einsum('nd,edf->nef', xf, P['w_exp_gate'][l])
    hu = jnp.einsum('nd,edf->nef', xf, P['w_exp_up'][l])
    act = jax.nn.silu(hg) * hu * comb[:, :, None]
    out = jnp.einsum('nef,efd->nd', act, P['w_exp_down'][l])
    return out.reshape(bsz, t, d)

def trunk(x, c, st, P):
    lbp = jax.nn.softmax(P['hgrn_lb_raw'].astype(F32), axis=0)
    lb_all = jnp.cumsum(lbp, axis=0) - lbp[0:1]
    new = ([], [], [], [], [])
    c_act = jax.nn.silu(c)
    for l in range(DEPTH):
        mod = (c_act @ P['w_ada'][l] + P['b_ada'][l])[:, None, :]
        sh1, sc1, gt1, sh2, sc2, gt2 = jnp.split(mod, 6, axis=-1)
        h = rmsnorm(x, P['g_mix'][l]) * (1 + sc1) + sh1
        st_l = None if st is None else tuple(s[l] for s in st)
        m, ns = mixer(h, st_l, P, l, lb_all[l])
        x = x + gt1 * m
        h = rmsnorm(x, P['g_ffn'][l]) * (1 + sc2) + sh2
        x = x + gt2 * hmoe(h, P, l)
        for acc, s in zip(new, ns):
            acc.append(s)
    y = rmsnorm(x, P['g_final'])
    return y, tuple(jnp.stack(acc) for acc in new)

def setup_inputs(seed: int = 0) -> dict:
    key = jax.random.key(seed)
    ks = iter(jax.random.split(key, 48))

    def nrm(shape, scale=1.0):
        return scale * jax.random.normal(next(ks), shape, F32)

    def unif(shape, lo, hi):
        return jax.random.uniform(next(ks), shape, F32, lo, hi)

    dt0 = jnp.exp(unif((DEPTH, SSD_HEADS), math.log(1e-3), math.log(1e-1)))
    return {
        'x_prompt': nrm((BATCH, SEQ, D_MODEL)),
        'x_sample': nrm((DEC_BATCH, DEC_SEQ, D_MODEL)),
        'c_prompt': nrm((BATCH, D_MODEL)),
        'c_sample': nrm((DEC_BATCH, D_MODEL)),
        'state_conv': nrm((DEPTH, DEC_BATCH, CONV_WIDTH - 1, CONV_CH)),
        'state_ssd': nrm((DEPTH, DEC_BATCH, SSD_HEADS, SSD_STATE, SSD_HEAD_DIM), 0.3),
        'state_hgrn': nrm((DEPTH, DEC_BATCH, HG_HEADS, HG_KEY_DIM, HG_HEAD_DIM), 0.3),
        'state_s5_re': nrm((DEPTH, DEC_BATCH, S5_GROUPS, S5_STATE), 0.1),
        'state_s5_im': nrm((DEPTH, DEC_BATCH, S5_GROUPS, S5_STATE), 0.1),
        'w_ada': nrm((DEPTH, D_MODEL, 6 * D_MODEL), 0.5 * D_MODEL ** -0.5),
        'b_ada': nrm((DEPTH, 6 * D_MODEL), 0.02),
        'g_mix': 1.0 + nrm((DEPTH, D_MODEL), 0.05),
        'g_ffn': 1.0 + nrm((DEPTH, D_MODEL), 0.05),
        'w_in': nrm((DEPTH, D_MODEL, IN_COLS), D_MODEL ** -0.5),
        'conv_w': nrm((DEPTH, CONV_WIDTH, CONV_CH), CONV_WIDTH ** -0.5),
        'conv_b': nrm((DEPTH, CONV_CH), 0.02),
        'ssd_dt_bias': dt0 + jnp.log(-jnp.expm1(-dt0)),
        'ssd_a_log': jnp.log(unif((DEPTH, SSD_HEADS), 1.0, 16.0)),
        'ssd_d': 1.0 + nrm((DEPTH, SSD_HEADS), 0.05),
        'ssd_norm_g': 1.0 + nrm((DEPTH, SSD_WIDTH), 0.05),
        'hgrn_lb_raw': nrm((DEPTH, HG_KEY_WIDTH), 0.5),
        'hgrn_norm_g': 1.0 + nrm((DEPTH, HG_HEADS, HG_HEAD_DIM), 0.05),
        's5_lam_re': -0.5 + nrm((DEPTH, S5_GROUPS, S5_STATE), 0.01),
        's5_lam_im': math.pi * jnp.arange(S5_STATE, dtype=F32) + nrm((DEPTH, S5_GROUPS, S5_STATE), 0.01),
        's5_log_dt': unif((DEPTH, S5_GROUPS), math.log(1e-3), math.log(1e-1)),
        's5_b_re': nrm((DEPTH, S5_GROUPS, S5_STATE, S5_GROUP_CH), (2 * S5_GROUP_CH) ** -0.5),
        's5_b_im': nrm((DEPTH, S5_GROUPS, S5_STATE, S5_GROUP_CH), (2 * S5_GROUP_CH) ** -0.5),
        's5_c_re': nrm((DEPTH, S5_GROUPS, S5_GROUP_CH, S5_STATE), S5_STATE ** -0.5),
        's5_c_im': nrm((DEPTH, S5_GROUPS, S5_GROUP_CH, S5_STATE), S5_STATE ** -0.5),
        's5_d': nrm((DEPTH, S5_WIDTH)),
        's5_w_glu': nrm((DEPTH, S5_WIDTH, S5_WIDTH), S5_WIDTH ** -0.5),
        's5_b_glu': nrm((DEPTH, S5_WIDTH), 0.02),
        'w_out': nrm((DEPTH, D_MIX, D_MODEL), D_MIX ** -0.5),
        'w_router_group': nrm((DEPTH, D_MODEL, N_EGROUPS), D_MODEL ** -0.5),
        'b_router_group': nrm((DEPTH, N_EGROUPS), 0.01),
        'w_router_expert': nrm((DEPTH, D_MODEL, N_EXPERTS), D_MODEL ** -0.5),
        'b_router_expert': nrm((DEPTH, N_EXPERTS), 0.01),
        'w_exp_gate': nrm((DEPTH, N_EXPERTS, D_MODEL, D_EXPERT), D_MODEL ** -0.5),
        'w_exp_up': nrm((DEPTH, N_EXPERTS, D_MODEL, D_EXPERT), D_MODEL ** -0.5),
        'w_exp_down': nrm((DEPTH, N_EXPERTS, D_EXPERT, D_MODEL), D_EXPERT ** -0.5),
        'g_final': 1.0 + nrm((D_MODEL,), 0.05),
    }

def reference(x_prompt, x_sample, c_prompt, c_sample, state_conv, state_ssd, state_hgrn,
              state_s5_re, state_s5_im, w_ada, b_ada, g_mix, g_ffn, w_in, conv_w, conv_b,
              ssd_dt_bias, ssd_a_log, ssd_d, ssd_norm_g, hgrn_lb_raw, hgrn_norm_g,
              s5_lam_re, s5_lam_im, s5_log_dt, s5_b_re, s5_b_im, s5_c_re, s5_c_im, s5_d,
              s5_w_glu, s5_b_glu, w_out, w_router_group, b_router_group, w_router_expert,
              b_router_expert, w_exp_gate, w_exp_up, w_exp_down, g_final):
    P = dict(w_ada=w_ada, b_ada=b_ada, g_mix=g_mix, g_ffn=g_ffn, w_in=w_in, conv_w=conv_w,
             conv_b=conv_b, ssd_dt_bias=ssd_dt_bias, ssd_a_log=ssd_a_log, ssd_d=ssd_d,
             ssd_norm_g=ssd_norm_g, hgrn_lb_raw=hgrn_lb_raw, hgrn_norm_g=hgrn_norm_g,
             s5_lam_re=s5_lam_re, s5_lam_im=s5_lam_im, s5_log_dt=s5_log_dt, s5_b_re=s5_b_re,
             s5_b_im=s5_b_im, s5_c_re=s5_c_re, s5_c_im=s5_c_im, s5_d=s5_d, s5_w_glu=s5_w_glu,
             s5_b_glu=s5_b_glu, w_out=w_out, w_router_group=w_router_group,
             b_router_group=b_router_group, w_router_expert=w_router_expert,
             b_router_expert=b_router_expert, w_exp_gate=w_exp_gate, w_exp_up=w_exp_up,
             w_exp_down=w_exp_down, g_final=g_final)
    y_prompt, (conv_p, ssd_p, hgrn_p, s5re_p, s5im_p) = trunk(x_prompt, c_prompt, None, P)
    y_sample, (conv_s, ssd_s, hgrn_s, s5re_s, s5im_s) = trunk(
        x_sample, c_sample, (state_conv, state_ssd, state_hgrn, state_s5_re, state_s5_im), P)
    return (y_prompt, y_sample, conv_p, ssd_p, hgrn_p, s5re_p, s5im_p,
            conv_s, ssd_s, hgrn_s, s5re_s, s5im_s)


_drawn_inputs = setup_inputs


def setup_inputs(seed=0):
    import zlib

    import numpy as np

    out = dict(_drawn_inputs(seed))
    spreads = {}
    factors = {'state_hgrn': 8.0,
     'g_ffn': 3.641,
     'ssd_d': 5.987,
     'ssd_norm_g': 5.036,
     'hgrn_norm_g': 8.0,
     's5_lam_re': 18.969,
     's5_c_re': 8.0,
     's5_c_im': 8.0,
     's5_w_glu': 3.097,
     's5_b_glu': 64.0,
     'b_router_group': 8.0,
     'b_router_expert': 8.0}
    for name, (base, spread) in spreads.items():
        noise = np.random.default_rng([zlib.crc32(name.encode()), seed]).standard_normal(out[name].shape)
        drawn = base * np.exp(spread * noise) if base else spread * noise
        out[name] = __import__('jax').numpy.asarray(drawn.astype(out[name].dtype))
    for name, factor in factors.items():
        out[name] = (out[name] * factor).astype(out[name].dtype)
    return out
```

```python
from contextlib import ExitStack

import concourse.bass as bass
from concourse import mybir

F32 = mybir.dt.float32
I32 = mybir.dt.int32
ALU = mybir.AluOpType
ACT = mybir.ActivationFunctionType
AX = mybir.AxisListType

P = 128
D = 2048
KD = D // P
TP, TS = 256, 64
T = TP + TS
CH = 64
NCH = T // CH
STREAMS = ((0, TP), (TP, T))
NXBC = 10
PADP, PADS = 3, 3 + TP + 3
TPAD = T + 6
Z, HQ, HF, HI, HG, U = 0, 8, 12, 16, 20, 24
NPROJ = 28
NH = 16
CW = 256
RING = 4
ADA1, INP, ADA2, OUTP, PRE = 0, 16, 36, 68, 76
NE = 32
MRING = 3
COL_HG, COL_DT = 2320, 2304
LEVELS = (0, 32, 16, 8, 4, 2, 1)
EPS = 1e-6

IN_CHUNKS = [(4368, U), (4624, U + 2), (COL_DT, None), (0, Z)]
IN_CHUNKS += [(COL_HG + CW * i, HQ + 2 * i) for i in range(8)]
IN_CHUNKS += [(CW * i, Z + 2 * i) for i in range(1, 4)]
IN_CHUNKS += [(1024 + CW * i, 100 + 2 * i) for i in range(5)]


def make_plan():
    bulk = [("in", n) for n in range(4, 20)] + [("ada", a) for a in range(16, 48)]
    s5 = []
    for b in range(8):
        s5 += [("s5_in", b), None, ("s5_out", b)]
    s5 += [None, ("s5_glu", 0)]
    hg = []
    for hp in range(2):
        hg += [("hg_prep", hp), None]
        for lv in range(len(LEVELS)):
            hg += [("hg_level", hp, lv), None]
        hg += [("hg_kd", hp), None, ("hg_state", hp), None, ("hg_out", hp), None]
    ssd = [("ssd_conv", 0), None, None, ("ssd_gamma", 0), None]
    for c in range(NCH):
        if c % 2 == 0:
            ssd += [("ssd_nat", c // 2), None]
        ssd += [("ssd_decay", c), None, ("ssd_y", c)]
    ssd += [None, ("ssd_norm", 0)]
    plan = [("in", n) for n in range(4)]
    for item in s5 + hg + ssd:
        if item is None:
            if bulk:
                plan.append(bulk.pop(0))
        else:
            if item[0] == "ssd_conv":
                while bulk and bulk[0][0] == "in":
                    plan.append(bulk.pop(0))
            plan.append(item)
    return plan + bulk


PLAN = make_plan()


def build(nc, a, o):
    ctx = ExitStack()
    with ctx:
        def sb(name, shape, dt=F32):
            return ctx.enter_context(nc.sbuf_tensor(name, shape, dt))

        sems = {}

        def S(name):
            if name not in sems:
                sems[name] = ctx.enter_context(nc.semaphore(name))
            return sems[name]

        psum = ctx.enter_context(nc.psum_tensor("psum", [P, 8, 512], F32))

        def bank(b, cols=512, part=P, lo=0):
            return psum[0:part, b, lo:lo + cols]

        xT = sb("xT", [P, KD, T])
        hT = sb("hT", [P, KD, T])
        slot = sb("slot", [P, RING, KD * CW])
        mem = sb("mem", [P, NPROJ * T + NXBC * TPAD + 7808])
        sq = sb("sq", [P, 2, 2 * T])
        rinv = sb("rinv", [P, T])
        ident = sb("ident", [P, P])
        ones = sb("ones", [P, P])
        rmask = sb("rmask", [P, T])
        lmask = sb("lmask", [P, len(LEVELS), CH])
        causal = sb("causal", [P, CH])
        parT = sb("parT", [P, 3 * P])
        modT = sb("modT", [P, 6 * KD, 2])
        rows = sb("rows", [64, 2 * CW])
        modrow = rows[0:2, :].rearrange("p (j n) -> p j n", j=2)
        dt_raw = rows[32:48, 0:T]
        cT = sb("cT", [P, KD, 2])
        sm = sb("sm", [P, 18, 16])
        BDT = sb("BDT", [P, 2, 4, P])
        CT = sb("CT", [P, 2, 4, P])
        ab1 = sb("ab1", [P, KD, 2])
        small = sb("small", [P, 96])
        s5fin = sb("s5fin", [P, 4, 16])

        proj = mem[:, 0:NPROJ * T].rearrange("p (n t) -> p n t", n=NPROJ)
        XB0 = NPROJ * T
        xbcp = mem[:, XB0:XB0 + NXBC * TPAD].rearrange("p (n t) -> p n t", n=NXBC)
        A0 = XB0 + NXBC * TPAD

        def ar(off, n):
            return mem[:, A0 + off:A0 + off + n]

        flat = mem[:, :]
        xnat = ar(0, 3 * D).rearrange("p (j d) -> p j d", j=3)
        prow = flat[:, 0:384].rearrange("p (j d) -> p j d", j=3)
        crow = flat[0:2, 384:384 + D]
        BR = flat[:, 2432:2688].rearrange("p (i j) -> p i j", i=16)
        BI = flat[:, 2688:2944].rearrange("p (i j) -> p i j", i=16)
        CR = flat[:, 2944:3456].rearrange("p (w u q) -> p w u q", w=2, u=4)
        bdp = flat[:, 3456:4480].rearrange("p (w i g j) -> p w i g j", w=2, i=16, g=2)
        cpad = flat[:, 4480:5504].rearrange("p (w u g q) -> p w u g q", w=2, u=4, g=2)
        btmp = flat[:, 5504:5760].rearrange("p (i j) -> p i j", i=16)
        cvrow = flat[0:3, 5760:7040]
        ldrow = flat[0:48, 7040:7042]
        s5b = [ar(640 * i, 640) for i in range(9)]
        wglu = ar(5760, 2048).rearrange("p (k m) -> p k m", k=4)
        hb, hE, hq_, hk_ = (ar(640 * i, 640) for i in range(4))
        htmp = ar(2560, 384)
        kdn = ar(1920, 768).rearrange("p (h q k) -> p h q k", h=2, q=3)
        hAT = ar(2944, 384)
        vn = ar(3328, 768).rearrange("p (h q k) -> p h q k", h=2, q=3)
        hS = ar(4096, 3072).rearrange("p (s h v) -> p s h v", s=6, h=4)
        dg = ar(0, 1024)
        W = ar(1024, 1024)
        v_ = ar(2048, 1024)
        vd = ar(3072, 1024)
        ctil = ar(4096, 1024)
        EB = ar(5120, 512)
        bn = ar(5632, 128)
        ytmp = ar(5760, 512)
        gtm = ar(6272, 128)
        cvout = ar(6400, 60).rearrange("p (i c) -> p i c", i=NXBC)
        cvst = ar(0, NXBC * P)
        aS = flat[:, HQ * T:HQ * T + 3072].rearrange("p (s n) -> p s n", s=6)
        hflat = hT[:, :, :].rearrange("p k t -> p (k t)")
        xbcT = hflat[:, 0:NXBC * T].rearrange("p (n t) -> p n t", n=NXBC)
        dtw = hflat[0:NH, 3200:3200 + 5 * T].rearrange("p (w t) -> p w t", w=5)
        bnat = hflat[:, 4800:4896].rearrange("p (q w h) -> p q w h", q=3, w=2)
        acc = flat[:, 0:KD * T].rearrange("p (k t) -> p k t", k=KD)
        combB = flat[:, 5120:5120 + NE * T]
        sgc = flat[:, 15360:15360 + 640]
        act_ = flat[:, 16000:16000 + 640]
        comb = flat[:, 16640:16640 + 96].rearrange("p (j e) -> p j e", j=3)
        combT = flat[0:NE, 16768:16768 + T]
        rt = flat[:, 17088:17088 + 1024]
        wr = flat[:, 18684:18684 + KD * 36].rearrange("p (k e) -> p k e", k=KD)
        brow = flat[0:1, 19260:19260 + 36]
        ynat = flat[:, 5120:5120 + 3 * D].rearrange("p (j d) -> p j d", j=3)
        comb_dram = nc.dram_tensor("comb_scratch", [NE, T], F32, kind="Internal").ap()

        b_ada, g_mix, g_ffn = parT[:, 0:96], parT[:, 96:112], parT[:, 112:128]
        p2 = parT[:, P:2 * P]
        conv_w = p2[:, 0:40].rearrange("p (j i) -> p j i", j=4)
        conv_b, ssd_g, lb_raw, hg_g, s5_d, s5_bg = (p2[:, x:y] for x, y in
                                                    ((40, 50), (50, 58), (58, 62), (62, 66), (66, 70), (70, 74)))
        g_fin, lam_re, lam_im = p2[:, 74:90], p2[:, 90:106], p2[:, 106:122]
        p3 = parT[:, 2 * P:3 * P]
        log_dt, ssd_D, x0re, x0im = p3[:, 0:16], p3[:, 32:40], p3[:, 64:80], p3[:, 80:96]

        def seg(i):
            return modT[:, KD * i:KD * (i + 1), :]

        def bc(ap, shape):
            return ap.broadcast_to(shape)

        def chunk_groups(n):
            if n < INP:
                return n + 1
            if n < ADA2:
                k = n - INP
                return 16 + 2 * (k + 1) - (1 if k >= 2 else 0)
            return 16 + 39 + (n - ADA2 + 1)

        def in_group(n):
            return 16 + 2 * n - (1 if n > 2 else 0)

        def ada_group(i):
            return i if i < 16 else 55 + i - 16

        class Steps:

            def __init__(self, eng, name):
                self.eng, self.name, self.n = eng, name, {}

            def __call__(self, ins, sem=None, wait=True):
                sem = sem or self.name
                ins.then_inc(S(sem), 1)
                self.n[sem] = self.n.get(sem, 0) + 1
                if wait:
                    self.eng.wait_ge(S(sem), self.n[sem])

        def states_stored(eng):
            eng.wait_ge(S("s5_stored"), 16 * 4)
            eng.wait_ge(S("hg_state_stored"), 16 * 2)
            eng.wait_ge(S("cv_saved"), 16 * 2)
            eng.wait_ge(S("ssd_stored"), 16 * 4)

        block = ctx.enter_context(nc.Block())

        @block.sync
        def _(sp):
            w_ada = a["w_ada"][0].rearrange("(k p) n -> p k n", p=P)
            w_in = a["w_in"][0].rearrange("(k p) n -> p k n", p=P)
            w_out = a["w_out"][0].rearrange("(k p) n -> p k n", p=P)

            def dst(s, w=CW):
                return slot[:, s, 0:KD * w].rearrange("p (k n) -> p k n", k=KD)

            for j in range(RING):
                sp.dma_start(dst(j), w_ada[:, :, j * CW:(j + 1) * CW]).then_inc(S(f"w_landed{j}"), 16)
            with sp.Fori(1, 4) as i:
                for j in range(RING):
                    sp.wait_ge(S("bulk_done"), 4 * i + (j - 3))
                    sp.dma_start(dst(j), w_ada[:, :, bass.ds(i * (4 * CW) + j * CW, CW)])\
                      .then_inc(S(f"w_landed{j}"), 16)
            for n in range(INP, PRE):
                s = n % RING
                if n < OUTP + RING:
                    sp.wait_ge(S("bulk_done"), chunk_groups(n - RING))
                else:
                    sp.wait_ge(S("out_done"), 2 * (n - RING - OUTP + 1))
                if n < ADA2:
                    col = IN_CHUNKS[n - INP][0]
                    w = 16 if col == COL_DT else CW
                    sp.dma_start(dst(s, w), w_in[:, :, col:col + w]).then_inc(S(f"w_landed{s}"), 16)
                elif n < OUTP:
                    i = n - ADA2 + 16
                    sp.dma_start(dst(s), w_ada[:, :, i * CW:(i + 1) * CW]).then_inc(S(f"w_landed{s}"), 16)
                else:
                    i = n - OUTP
                    sp.dma_start(dst(s), w_out[:, :, i * CW:(i + 1) * CW]).then_inc(S(f"w_landed{s}"), 16)
            gate = a["w_exp_gate"][0].rearrange("e (k p) n -> e p k n", p=P)
            up = a["w_exp_up"][0].rearrange("e (k p) n -> e p k n", p=P)
            down = a["w_exp_down"][0].rearrange("e (k p) n -> e p k n", p=P)

            def ddst(s):
                return slot[:, s, :].rearrange("p (k n) -> p k n", k=2)

            sp.wait_ge(S("out_done"), 2 * 5)
            sp.dma_start(dst(0), gate[0]).then_inc(S("w_landed0"), 16)
            sp.wait_ge(S("out_done"), 2 * 6)
            sp.dma_start(dst(1), up[0]).then_inc(S("w_landed1"), 16)
            sp.wait_ge(S("out_done"), 2 * 7)
            sp.dma_start(dst(2), gate[1]).then_inc(S("w_landed2"), 16)
            sp.wait_ge(S("gate_done"), 2)
            sp.dma_start(ddst(0), down[0]).then_inc(S("w_landed0"), 16)
            sp.wait_ge(S("up_done"), 2)
            sp.dma_start(dst(1), up[1]).then_inc(S("w_landed1"), 16)
            with sp.Fori(2, NE) as e:
                sp.wait_ge(S("gate_done"), 2 * e)
                sp.dma_start(dst(2), gate[bass.ds(e, 1)].rearrange("e p k n -> (e p) k n")).then_inc(S("w_landed2"), 16)
                sp.wait_ge(S("down_done"), 16 * e - 16)
                sp.dma_start(ddst(0), down[bass.ds(e - 1, 1)].rearrange("e p k n -> (e p) k n"))\
                  .then_inc(S("w_landed0"), 16)
                sp.wait_ge(S("up_done"), 2 * e)
                sp.dma_start(dst(1), up[bass.ds(e, 1)].rearrange("e p k n -> (e p) k n")).then_inc(S("w_landed1"), 16)
            sp.wait_ge(S("gate_done"), 2 * NE)
            sp.dma_start(ddst(2), down[NE - 1]).then_inc(S("w_landed2"), 16)
            sp.wait_ge(S("y_rows"), 12)
            sp.dma_start(o["y_prompt"][0].rearrange("(j p) d -> p j d", p=P), ynat[:, 0:2, :]).then_inc(S("stores"), 16)
            sp.dma_start(o["y_sample"][0], ynat[0:TS, 2, :]).then_inc(S("stores"), 16)
            sp.wait_ge(S("stores"), 16 * 2)
            states_stored(sp)

        @block.gpsimd
        def _(pool):
            pl = Steps(pool, "pool_step")
            g = nc.gpsimd
            pl(g.memset(ident[:, :], 0.0))
            pl(g.affine_select(out=ident[:, :], in_=ident[:, :], compare_op=ALU.not_equal, fill=1.0, base=0,
                               pattern=[[-1, P]], channel_multiplier=1))
            pl(g.memset(prow[:, 2, :], 0.0))
            pl(g.memset(ones[:, :], 1.0), "consts_a")
            pl(g.memset(rmask[:, :], 1.0))
            pl(g.memset(rmask[:, :].rearrange("p (c t) -> p c t", c=NCH)[:, :, 0:1], 0.0))
            pl(g.memset(lmask[:, :, :], 0.0))
            pl(g.memset(causal[:, :], 1.0))
            for half in range(2):
                lo = CH * half
                rows = slice(lo, lo + CH)
                pl(g.affine_select(out=lmask[rows, 0, :], in_=lmask[rows, 0, :], compare_op=ALU.not_equal,
                                   fill=1.0, base=0, pattern=[[-1, CH]], channel_multiplier=1))
                pl(g.affine_select(out=causal[rows, :], in_=causal[rows, :], compare_op=ALU.is_ge,
                                   fill=0.0, base=0, pattern=[[1, CH]], channel_multiplier=-1))
                for lv, m in enumerate(LEVELS[1:], 1):
                    sub = lmask[rows, lv, :].rearrange("p (b r) -> p b r", r=2 * m)[:, :, m:2 * m]
                    pl(g.memset(sub, 1.0))
                    pl(g.affine_select(out=sub, in_=sub, compare_op=ALU.is_ge, fill=0.0, base=0,
                                       pattern=[[-2 * m, CH // (2 * m)], [0, m]], channel_multiplier=1))
                    pl(g.affine_select(out=sub, in_=sub, compare_op=ALU.is_ge, fill=0.0, base=m - 1,
                                       pattern=[[2 * m, CH // (2 * m)], [0, m]], channel_multiplier=-1))
            par = small[:, 4:8]
            pl(g.memset(par, 1.0))
            pl(g.affine_select(out=par, in_=par, compare_op=ALU.is_ge, fill=0.0, base=-16,
                               pattern=[[-32, 4]], channel_multiplier=1))
            pl(g.affine_select(out=par, in_=par, compare_op=ALU.is_ge, fill=0.0, base=31,
                               pattern=[[32, 4]], channel_multiplier=-1))
            pl(g.tensor_tensor(small[:, 8:9], small[:, 4:5], small[:, 5:6], ALU.add))
            pl(g.tensor_tensor(small[:, 9:10], small[:, 6:7], small[:, 7:8], ALU.add))
            pl(g.tensor_tensor(small[:, 1:2], small[:, 8:9], small[:, 9:10], ALU.add))
            pl(g.tensor_scalar(small[:, 0:1], small[:, 1:2], -1.0, 1.0, ALU.mult, ALU.add))
            for j in range(8):
                pl(g.memset(small[:, 16 + j:17 + j], float(j - 99)))
            pl(g.memset(bdp, 0.0), "consts_b")
            pool.wait_ge(S("s5_angles"), 1)
            pool.wait_ge(S("x_transposed"), 12)
            pool.dma_start(wglu, a["s5_w_glu"][0].rearrange("(k p) m -> p k m", p=P)).then_inc(S("wglu_loaded"), 16)
            for b in range(8):
                if b >= 2:
                    pool.wait_ge(S("s5_turned"), b - 1)
                pc, ps = (s5b[5 + 2 * (b % 2) + i].rearrange("p (i t) -> p i t", i=2) for i in range(2))
                tt, t2 = (sq[:, 0, 320 * i:320 * i + 256].rearrange("p (i t) -> p i t", i=2) for i in range(2))
                if b == 0:
                    pool.wait_ge(S("norm_squares_used"), 8)
                cs = sm[:, 0, 2 * b:2 * b + 2].unsqueeze(2)
                sn = sm[:, 1, 2 * b:2 * b + 2].unsqueeze(2)
                pl(g.tensor_copy(pc[:, :, 0:1], cs))
                pl(g.tensor_copy(ps[:, :, 0:1], sn))
                m = 1
                while m < TP:
                    cm, sn_ = (bc(t[:, :, m - 1:m], [P, 2, m]) for t in (pc, ps))
                    pl(g.tensor_tensor(tt[:, :, 0:m], pc[:, :, 0:m], cm, ALU.mult))
                    pl(g.tensor_tensor(t2[:, :, 0:m], ps[:, :, 0:m], sn_, ALU.mult))
                    pl(g.tensor_tensor(pc[:, :, m:2 * m], tt[:, :, 0:m], t2[:, :, 0:m], ALU.subtract))
                    pl(g.tensor_tensor(tt[:, :, 0:m], pc[:, :, 0:m], sn_, ALU.mult))
                    pl(g.tensor_tensor(t2[:, :, 0:m], ps[:, :, 0:m], cm, ALU.mult))
                    pl(g.tensor_tensor(ps[:, :, m:2 * m], tt[:, :, 0:m], t2[:, :, 0:m], ALU.add))
                    m *= 2
                pl(g.tensor_copy(pc[:, :, TP:T], pc[:, :, 0:TS]))
                pl(g.tensor_copy(ps[:, :, TP:T], ps[:, :, 0:TS]), "s5_table")
            pool.wait_ge(S("s5_fin_rows"), 1)
            for w, name in enumerate(("s5re_p", "s5im_p", "s5re_s", "s5im_s")):
                pool.dma_start(o[name][0, 0].rearrange("(i g) q -> i (g q)", g=2), sq[0:16, 1, w * P:(w + 1) * P])\
                    .then_inc(S("s5_stored"), 16)
            pool.wait_ge(S("glu_used"), 4)
            pool.dma_start(hS[:, 4, :, :], a["state_hgrn"][0, 0].rearrange("h k v -> k h v"))\
                .then_inc(S("hg_in_loaded"), 16)
            pool.wait_ge(S("hg_S"), 2 * NCH)
            for sl, name in ((3, "hgrn_p"), (5, "hgrn_s")):
                pool.dma_start(o[name][0, 0].rearrange("h k v -> k h v"), hS[:, sl, :, :])\
                    .then_inc(S("hg_state_stored"), 16)
            pool.wait_ge(S("hg_normed"), 4)
            for g_ in range(2):
                pool.dma_start(aS[64 * g_:64 * g_ + 64, 4, :].rearrange("k (j v) -> k j v", j=8),
                               a["state_ssd"][0, 0, 8 * g_:8 * g_ + 8].rearrange("j k v -> k j v"))\
                    .then_inc(S("ssd_in_loaded"), 16)
            pool.wait_ge(S("cv_stored"), 1)
            for s_, name in ((0, "conv_p"), (3, "conv_s")):
                pool.dma_start(o[name][0, 0], cvst[s_:s_ + 3, :]).then_inc(S("cv_saved"), 16)
            pool.dma_start(wr[:, :, 0:4], a["w_router_group"][0].rearrange("(k p) e -> p k e", p=P))\
                .then_inc(S("router_loaded"), 16)
            pool.dma_start(wr[:, :, 4:36], a["w_router_expert"][0].rearrange("(k p) e -> p k e", p=P))\
                .then_inc(S("router_loaded"), 16)
            pool.dma_start(brow[:, 0:4], a["b_router_group"]).then_inc(S("router_loaded"), 16)
            pool.dma_start(brow[:, 4:36], a["b_router_expert"]).then_inc(S("router_loaded"), 16)
            pool.wait_ge(S("ssd_S"), NCH)
            for sl, name in ((3, "ssd_p"), (5, "ssd_s")):
                for g_ in range(2):
                    pool.dma_start(o[name][0, 0, 8 * g_:8 * g_ + 8].rearrange("j k v -> k j v"),
                                   aS[64 * g_:64 * g_ + 64, sl, :].rearrange("k (j v) -> k j v", j=8))\
                        .then_inc(S("ssd_stored"), 16)

        @block.scalar
        def _(act):
            s = nc.scalar
            st = Steps(act, "act_step")

            def load(dst, src, sem):
                act.dma_start(dst, src).then_inc(S(sem), 16)

            load(crow[0:1, :], a["c_prompt"], "c_loaded")
            load(crow[1:2, :], a["c_sample"], "c_loaded")
            load(xnat[:, 0:2, :], a["x_prompt"][0].rearrange("(j p) d -> p j d", p=P), "x_loaded")
            load(xnat[0:TS, 2, :], a["x_sample"][0], "x_loaded")
            r = lambda ap: ap.rearrange("(n q) -> n q", q=P)
            load(prow[0:96, 0, :], r(a["b_ada"][0]), "par_loaded")
            load(prow[96:112, 0, :], r(a["g_mix"][0]), "par_loaded")
            load(prow[112:128, 0, :], r(a["g_ffn"][0]), "par_loaded")
            load(prow[0:40, 1, :], a["conv_w"][0].rearrange("j (n q) -> (j n) q", q=P), "par_loaded")
            for lo, hi, name in ((40, 50, "conv_b"), (50, 58, "ssd_norm_g"), (58, 62, "hgrn_lb_raw"),
                                 (66, 70, "s5_d"), (70, 74, "s5_b_glu")):
                load(prow[lo:hi, 1, :], r(a[name][0]), "par_loaded")
            load(prow[62:66, 1, :], a["hgrn_norm_g"][0], "par_loaded")
            load(prow[74:90, 1, :], r(a["g_final"]), "par_loaded")
            two = lambda ap: ap.rearrange("(i g) q -> i (g q)", g=2)
            load(prow[90:106, 1, :], two(a["s5_lam_re"][0]), "par_loaded")
            load(prow[106:122, 1, :], two(a["s5_lam_im"][0]), "par_loaded")
            load(ldrow[0:16, :], a["s5_log_dt"][0].rearrange("(i g) -> i g", g=2), "ld_loaded")
            load(ldrow[32:40, :], a["ssd_d"][0].rearrange("(i g) -> i g", g=2), "ld_loaded")
            act.wait_ge(S("consts_a"), 1)
            load(prow[64:80, 2, :], two(a["state_s5_re"][0, 0]), "par_loaded")
            load(prow[80:96, 2, :], two(a["state_s5_im"][0, 0]), "par_loaded")
            gp = lambda ap: ap.rearrange("(i g) q j -> (g q) i j", g=2)
            load(BR, gp(a["s5_b_re"][0]), "s5_loaded")
            load(BI, gp(a["s5_b_im"][0]), "s5_loaded")
            load(CR[:, 0], a["s5_c_re"][0].rearrange("(u g) j q -> (g j) u q", u=4), "s5_loaded")
            load(CR[:, 1], a["s5_c_im"][0].rearrange("(u g) j q -> (g j) u q", u=4), "s5_loaded")
            load(cvrow, a["state_conv"][0, 0], "cv_loaded")
            load(small[0:NH, 32:33], a["ssd_dt_bias"][0].rearrange("(h u) -> h u", u=1), "hd_loaded")
            load(small[0:NH, 33:34], a["ssd_a_log"][0].rearrange("(h u) -> h u", u=1), "hd_loaded")

            act.wait_ge(S("c_loaded"), 32)
            st(s.activation(crow, crow, ACT.Silu), "c_act")
            act.wait_ge(S("par_columns"), 1)
            st(s.activation(sm[:, 2, :], log_dt, ACT.Exp), "s5_dt")
            act.wait_ge(S("s5_expo"), 1)
            st(s.activation(sm[:, 4, :], sm[:, 3, :], ACT.Exp), "s5_mag")
            act.wait_ge(S("hd_loaded"), 32)
            st(s.activation(small[0:NH, 34:35], small[0:NH, 33:34], ACT.Exp), "a_exp")
            act.wait_ge(S("s5_wrap"), 1)
            st(s.activation(sm[:, 0, :], sm[:, 7, :], ACT.Sin))
            st(s.activation(sm[:, 1, :], sm[:, 6, :], ACT.Sin), "s5_angles")

            def squares(src, i, tag):
                if i >= 2:
                    act.wait_ge(S(tag), i - 1)
                st(s.activation(sq[:, i % 2, :].rearrange("p (k t) -> p k t", k=2), src, ACT.Square), tag + "_sq")

            for i in range(8):
                act.wait_ge(S("x_transposed"), 12)
                squares(xT[:, 2 * i:2 * i + 2, :], i, "norm_squares_used")
            act.wait_ge(S("n1_mean"), 1)
            st(s.activation(rinv[:, :], rinv[:, :], ACT.Sqrt), "n1_root")

            def ada_evac(i, j, grp, slow=True):
                n = 4 * i + j
                act.wait_ge(S("bulk_done"), grp + 1)
                if slow:
                    act.wait_ge(S("mod_turned"), n - 1)
                s.activation(modrow[:, j % 2, :], psum[0:2, (grp if isinstance(grp, int) else j) % 2, 0:CW],
                             ACT.Copy).then_inc(S("bulk_evac"), 1)

            for j in range(4):
                ada_evac(0, j, j, slow=j >= 2)
            with act.Fori(1, 4) as i:
                for j in range(4):
                    act.wait_ge(S("bulk_done"), 4 * i + (j + 1))
                    act.wait_ge(S("mod_turned"), 4 * i + (j - 1))
                    s.activation(modrow[:, j % 2, :], psum[0:2, j % 2, 0:CW], ACT.Copy).then_inc(S("bulk_evac"), 1)

            act.wait_ge(S("h_scaled"), 1)
            for k in range(KD):
                s.activation(hT[:, k, 0:TP], hT[:, k, 0:TP], ACT.Identity, bias=seg(0)[:, k, 0:1],
                             scale=ab1[:, k, 0:1]).then_inc(S("h_prompt"), 1)

            def evac_in(n):
                tile = IN_CHUNKS[n][1]
                for q in range(1 if tile is None else 2):
                    grp = in_group(n) + q
                    act.wait_ge(S("bulk_done"), grp + 1)
                    src = psum[:, grp % 2, 0:T]
                    if tile is None:
                        s.activation(dt_raw, psum[0:NH, grp % 2, 0:T], ACT.Copy).then_inc(S("bulk_evac"), 1)
                    elif tile >= 100:
                        i = tile - 100 + q
                        st(s.activation(xbcp[:, i, PADP:PADP + TP], src[:, 0:TP], ACT.Copy))
                        s.activation(xbcp[:, i, PADS:PADS + TS], src[:, TP:T], ACT.Copy).then_inc(S("bulk_evac"), 1)
                    else:
                        s.activation(proj[:, tile + q, :], src, ACT.Copy).then_inc(S("bulk_evac"), 1)

            def s5_in(b):
                act.wait_ge(S("s5_bu"), b + 1)
                if b:
                    act.wait_ge(S("s5_turned"), b)
                    act.wait_ge(S("s5_y"), b)
                for w in range(2):
                    src = psum[:, 4 + 2 * w:6 + 2 * w, 0:T]
                    st(s.activation(s5b[w].rearrange("p (i t) -> p i t", i=2), src, ACT.Copy), "s5_bu_sb")

            def s5_out(b):
                if b % 2:
                    act.wait_ge(S("s5_gelu_arg"), b // 2 + 1)
                    st(s.activation(sq[:, 1, 0:T], sq[:, 1, 0:T], ACT.Sigmoid), "s5_gelu_sig")

            def s5_glu():
                for m in range(4):
                    act.wait_ge(S("glu_mm"), m + 1)
                    if m >= 1:
                        act.wait_ge(S("glu_used"), m)
                    st(s.activation(rinv[:, :], psum[:, 4 + m, 0:T], ACT.Sigmoid, bias=s5_bg[:, m:m + 1]), "glu_sig")

            def hg_prep(hp):
                hf = flat[:, (HF + 2 * hp) * T:(HF + 2 * hp + 2) * T]
                if hp == 0:
                    act.wait_ge(S("glu_used"), 4)
                act.wait_ge(S("bulk_evac"), in_group(12))
                if hp:
                    act.wait_ge(S("hg_kd_turned"), 2 * hp)
                    act.wait_ge(S("hg_kdn"), hp)
                st(s.activation(hE, hf, ACT.Sigmoid))
                st(s.activation(hf, hf, ACT.Sigmoid, scale=-1.0), "hg_sig")
                act.wait_ge(S("hg_f"), hp + 1)
                st(s.activation(hE, hE, ACT.Ln), "hg_ln")

            def hg_level(hp, lv):
                if lv:
                    act.wait_ge(S("hg_expo"), 6 * hp + lv)
                    st(s.activation(hE, hE, ACT.Exp), "hg_exp")

            def hg_kd(hp):
                act.wait_ge(S("hg_expo2"), 2 * hp + 1)
                st(s.activation(hE, hb, ACT.Exp), "hg_exp2")
                act.wait_ge(S("hg_expo2"), 2 * hp + 2)
                st(s.activation(hE, hE, ACT.Exp), "hg_exp2")

            def hg_out(hp):
                gate = flat[:, (HG + 2 * hp) * T:(HG + 2 * hp + 2) * T]
                st(s.activation(gate, gate, ACT.Silu), "hg_gate")
                for h in range(2):
                    act.wait_ge(S("hg_o"), 2 * hp + 2)
                    st(s.activation(sq[:, 0, h * T:h * T + T], psum[:, 4 + h, 0:T], ACT.Square), "hg_sq")
                for h in range(2):
                    act.wait_ge(S("hg_var"), 2 * hp + h + 1)
                    st(s.activation(rinv[:, :], rinv[:, :], ACT.Sqrt), "hg_root")

            def ssd_conv():
                act.wait_ge(S("dt_neg"), 1)
                st(s.activation(dtw[:, 1, :], dtw[:, 0, :], ACT.Exp), "dt_exp")
                act.wait_ge(S("dt_one"), 1)
                st(s.activation(dtw[:, 3, :], dtw[:, 2, :], ACT.Ln), "dt_ln")
                for i in range(NXBC):
                    act.wait_ge(S("conv_out"), i + 1)
                    st(s.activation(xbcT[:, i, :], xbcT[:, i, :], ACT.Silu), "conv_silu")
                st(s.activation(flat[:, 0:8 * T], flat[:, 0:8 * T], ACT.Silu), "z_silu")

            def ssd_decay(c):
                half = slice(CH * (c % 2), CH * (c % 2) + CH)
                act.wait_ge(S("ssd_diff"), 2 * c + 1)
                st(s.activation(small[half, 64:80], small[half, 64:80], ACT.Exp), "ssd_exp")
                for g in range(2):
                    rows = slice(64 * g, 64 * g + 64)
                    st(s.activation(EB[rows, :], psum[rows, 4 + g, :], ACT.Exp), "ssd_EB")
                act.wait_ge(S("ssd_diff"), 2 * c + 2)
                st(s.activation(W[half, :], W[half, :], ACT.Exp), "ssd_exp")

            def ssd_norm():
                act.wait_ge(S("ssd_done"), NCH)
                act.wait_ge(S("s5_stored"), 64)
                for i in range(4):
                    squares(proj[:, 2 * i:2 * i + 2, :], i, "ssd_squares_used")
                act.wait_ge(S("ssd_mean"), 1)
                st(s.activation(rinv[:, :], rinv[:, :], ACT.Sqrt), "ssd_root")

            for item in PLAN:
                kind = item[0]
                if kind == "in":
                    evac_in(item[1])
                elif kind == "ada":
                    ada_evac(0, item[1], ada_group(item[1]))
                elif kind == "s5_in":
                    s5_in(item[1])
                elif kind == "s5_out":
                    s5_out(item[1])
                elif kind == "s5_glu":
                    s5_glu()
                elif kind == "hg_prep":
                    hg_prep(item[1])
                elif kind == "hg_level":
                    hg_level(item[1], item[2])
                elif kind == "hg_kd":
                    hg_kd(item[1])
                elif kind == "hg_out":
                    hg_out(item[1])
                elif kind == "ssd_conv":
                    ssd_conv()
                elif kind == "ssd_decay":
                    ssd_decay(item[1])
                elif kind == "ssd_norm":
                    ssd_norm()

            for i in range(8):
                act.wait_ge(S("x_mixed"), 4 * (i + 1))
                squares(xT[:, 2 * i:2 * i + 2, :], i, "n2_squares_used")
            act.wait_ge(S("n2_mean"), 1)
            st(s.activation(rinv[:, :], rinv[:, :], ACT.Sqrt), "n2_root")
            act.wait_ge(S("h2_scaled"), 1)
            for k in range(KD):
                s.activation(hT[:, k, 0:TP], hT[:, k, 0:TP], ACT.Identity, bias=seg(3)[:, k, 0:1],
                             scale=ab1[:, k, 0:1]).then_inc(S("h2_prompt"), 1)
            act.wait_ge(S("rt_expo"), 1)
            st(s.activation(rt[:, 16:28], rt[:, 16:28], ACT.Exp))
            st(s.activation(rt[:, 240:243], rt[:, 240:243], ACT.Exp), "rt_exp")
            act.wait_ge(S("comb_cols"), 1)
            act.dma_start(comb_dram, combT).then_inc(S("comb_out"), 16)
            act.wait_ge(S("comb_out"), 16)
            act.dma_start(combB, comb_dram.rearrange("e t -> (e t)").unsqueeze(0).broadcast_to([P, NE * T]))\
               .then_inc(S("comb_loaded"), 16)
            act.wait_ge(S("gate_done"), 2)
            st(s.activation(sgc.rearrange("p (f t) -> p f t", f=2), psum[:, 0:2, 0:T], ACT.Silu), "gate_silu", wait=False)
            with act.Fori(1, NE) as e:
                act.wait_ge(S("gate_done"), 2 * e + 2)
                act.wait_ge(S("act_ready"), e)
                s.activation(sgc.rearrange("p (f t) -> p f t", f=2), psum[:, 0:2, 0:T], ACT.Silu)\
                 .then_inc(S("gate_silu"), 1)
            for i in range(8):
                act.wait_ge(S("x_final"), 4 * (i + 1))
                squares(xT[:, 2 * i:2 * i + 2, :], i, "n3_squares_used")
            act.wait_ge(S("n3_mean"), 1)
            st(s.activation(rinv[:, :], rinv[:, :], ACT.Sqrt), "n3_root")

        @block.tensor
        def _(pe):
            mm, tr = nc.tensor.matmul, nc.tensor.transpose
            pe.wait_ge(S("consts_a"), 1)
            pe.wait_ge(S("x_loaded"), 32)
            for g in range(12):
                j, kg = g // 4, g % 4
                n = P if j < 2 else TS
                if g >= 4:
                    pe.wait_ge(S("x_transposed"), g - 3)
                for q in range(4):
                    k = 4 * kg + q
                    last = tr(bank(4 + g % 4, n, lo=q * n), xnat[0:n, j, k * P:(k + 1) * P], ident[0:n, 0:n])
                last.then_inc(S("x_turned"), 1)
            pe.wait_ge(S("c_act"), 1)
            for k in range(KD):
                last = tr(bank(3, 2, lo=384 + 2 * k), crow[:, k * P:(k + 1) * P], ident[0:2, 0:2])
            last.then_inc(S("c_turned"), 1)
            pe.wait_ge(S("cT_ready"), 1)
            pe.wait_ge(S("par_rows"), 1)
            pe.wait_ge(S("par_loaded"), 16 * 15)
            tr(bank(3, P, lo=0), prow[:, 0, :], ident[:, :])
            tr(bank(3, 122, lo=P), prow[0:122, 1, :], ident[0:122, 0:122])
            tr(bank(3, 96, lo=2 * P), prow[0:96, 2, :], ident[0:96, 0:96]).then_inc(S("par_turned"), 1)
            pe.wait_ge(S("cv_loaded"), 16)
            pe.wait_ge(S("x_transposed"), 12)
            for i in range(NXBC):
                last = tr(bank(2, 3, lo=4 * i), cvrow[:, i * P:(i + 1) * P], ident[0:3, 0:3])
            last.then_inc(S("cv_turned"), 1)
            pe.wait_ge(S("par_columns"), 1)
            pe.wait_ge(S("cT_ready"), 1)

            def sum_squares(b, count, tag, i0=0):
                for i in range(count):
                    pe.wait_ge(S(tag + "_sq"), i + 1)
                    for q in range(2):
                        last = mm(bank(b, T), ones[:, :], sq[:, i % 2, q * T:q * T + T],
                                  start=(i == 0 and q == 0), stop=(i == count - 1 and q == 1))
                    last.then_inc(S(tag), 1)

            sum_squares(3, 8, "norm_squares_used")
            pe.wait_ge(S("s5_mats"), 1)
            for w in range(2):
                for u in range(4):
                    tr(bank(4 + w, P, lo=u * P),
                       bdp[:, w, 4 * u:4 * u + 4].rearrange("p i g j -> p (i g j)"), ident[:, :])
                    last = tr(bank(6 + w, P, lo=u * P), cpad[:, w, u].rearrange("p g q -> p (g q)"), ident[:, :])
            last.then_inc(S("s5_mats_turned"), 1)

            def ada_mm(s_, first, wait_evac):
                w = slot[:, s_, :].rearrange("p (k n) -> p k n", k=KD)
                for k in range(KD):
                    last = mm(psum[0:2, first, 0:CW], cT[:, k, :], w[:, k, :], start=(k == 0), stop=(k == KD - 1))
                last.then_inc(S("bulk_done"), 1)

            def ada_turn(j):
                for q in range(2):
                    last = mm(bank(2, 2, lo=64 + 4 * (j % 2) + 2 * q), modrow[:, j % 2, q * P:(q + 1) * P],
                              ident[0:2, 0:2], start=True, stop=True)
                last.then_inc(S("mod_turned"), 1)

            pe.wait_ge(S("cv_taken"), 1)
            for j in range(4):
                pe.wait_ge(S(f"w_landed{j}"), 16)
                if j >= 2:
                    pe.wait_ge(S("bulk_evac"), j - 1)
                ada_mm(j, j % 2, False)
                if j >= 1:
                    pe.wait_ge(S("bulk_evac"), j)
                    if j >= 2:
                        pe.wait_ge(S("mod_ready"), j - 1)
                    ada_turn(j - 1)
            with pe.Fori(1, 4) as i:
                for j in range(4):
                    pe.wait_ge(S(f"w_landed{j}"), 16 * i + 16)
                    pe.wait_ge(S("bulk_evac"), 4 * i + (j - 1))
                    ada_mm(j, j % 2, False)
                    pe.wait_ge(S("bulk_evac"), 4 * i + j)
                    pe.wait_ge(S("mod_ready"), 4 * i + (j - 1))
                    ada_turn(j + 3)
            pe.wait_ge(S("bulk_evac"), 16)
            pe.wait_ge(S("mod_ready"), 15)
            ada_turn(15)

            def in_mm(n):
                tile = IN_CHUNKS[n][1]
                r = INP + n
                pe.wait_ge(S(f"w_landed{r % RING}"), 16 * (r // RING + 1))
                wd = NH if tile is None else P
                w = slot[:, r % RING, 0:KD * (NH if tile is None else CW)].rearrange("p (k n) -> p k n", k=KD)
                for q in range(1 if tile is None else 2):
                    grp = in_group(n) + q
                    pe.wait_ge(S("bulk_evac"), grp - 1)
                    for k in range(KD):
                        last = mm(psum[0:wd, grp % 2, 0:T], w[:, k, q * P:q * P + wd], hT[:, k, :],
                                  start=(k == 0), stop=(k == KD - 1))
                    last.then_inc(S("bulk_done"), 1)

            def ada(i):
                r = ADA2 + i - 16
                grp = ada_group(i)
                pe.wait_ge(S(f"w_landed{r % RING}"), 16 * (r // RING + 1))
                pe.wait_ge(S("bulk_evac"), grp - 1)
                ada_mm(r % RING, grp % 2, False)
                if i > 16:
                    pe.wait_ge(S("bulk_evac"), grp)
                    pe.wait_ge(S("mod_ready"), i - 1)
                    ada_turn(i - 1)

            def s5_in(b):
                if b == 0:
                    pe.wait_ge(S("bulk_evac"), in_group(4))
                    pe.wait_ge(S("s5_mats_ready"), 1)
                if b:
                    pe.wait_ge(S("s5_bu_sb"), 2 * b)
                u = b // 2
                for i in range(2):
                    rows = slice(32 * (2 * (b % 2) + i), 32 * (2 * (b % 2) + i) + 32)
                    for w in range(2):
                        last = mm(psum[:, 4 + 2 * w + i, 0:T], BDT[rows, w, u, :], proj[rows, U + u, :],
                                  start=True, stop=True)
                last.then_inc(S("s5_bu"), 1)

            def s5_out(b):
                pe.wait_ge(S("s5_turned"), b + 1)
                if b % 2 == 0 and b:
                    pe.wait_ge(S("s5_g"), b // 2)
                u = b // 2
                for i in range(2):
                    c0 = 32 * (2 * (b % 2) + i)
                    for w in range(2):
                        last = mm(psum[c0:c0 + 32, 3, 0:T], CT[:, w, u, c0:c0 + 32],
                                  s5b[2 + w][:, i * T:i * T + T], start=(w == 0), stop=(w == 1))
                last.then_inc(S("s5_y"), 1)

            def s5_glu():
                pe.wait_ge(S("s5_g"), 4)
                pe.wait_ge(S("wglu_loaded"), 16)
                pe.wait_ge(S("s5_bu_sb"), 16)
                for m in range(4):
                    for k in range(4):
                        last = mm(bank(4 + m, T), wglu[:, k, m * P:(m + 1) * P], proj[:, U + k, :],
                                  start=(k == 0), stop=(k == 3))
                    last.then_inc(S("glu_mm"), 1)
                for w in range(4):
                    last = tr(bank(3, P, 16, lo=w * P), s5fin[:, w, :], ident[:, :])
                last.then_inc(S("s5_fin_turned"), 1)

            def hg_prep(hp):
                if hp == 0:
                    pe.wait_ge(S("bulk_evac"), in_group(12))
                    pe.wait_ge(S("glu_used"), 4)
                else:
                    pe.wait_ge(S("hg_normed"), 2)
                for h in range(2):
                    src = proj[:, HI + 2 * hp + h, :]
                    for q in range(3):
                        n = P if q < 2 else TS
                        last = tr(bank(6 + h, P, n, lo=q * P), src[:, q * P:q * P + n], ident[:, :])
                last.then_inc(S("hg_v"), 1)

            def hg_level(hp, lv):
                it = 7 * hp + lv
                if lv == 0:
                    pe.wait_ge(S("hg_k"), hp + 1)
                    q_, k_ = (flat[:, (x + 2 * hp) * T:(x + 2 * hp + 2) * T] for x in (HQ, HF))
                else:
                    pe.wait_ge(S("hg_qk"), 6 * hp + lv)
                    q_, k_ = hq_, hk_
                if it >= 2:
                    pe.wait_ge(S("hg_sc_used"), it - 1)
                for h in range(2):
                    for c in range(6):
                        cc = min(c, NCH - 1)
                        col = h * T + cc * CH
                        last = mm(psum[CH * (c % 2):CH * (c % 2) + CH, 4 + it % 2,
                                       (h * 3 + c // 2) * CH:(h * 3 + c // 2) * CH + CH],
                                  k_[:, col:col + CH], q_[:, col:col + CH], start=True, stop=True)
                last.then_inc(S("hg_sc"), 1)

            def hg_kd(hp):
                pe.wait_ge(S("hg_kd"), hp + 1)
                pe.wait_ge(S("hg_vn"), hp + 1)
                for h in range(2):
                    for q in range(3):
                        n = P if q < 2 else TS
                        last = tr(bank(6 + h, P, n, lo=q * P), hE[:, h * T + q * P:h * T + q * P + n], ident[:, :])
                    last.then_inc(S("hg_kd_turned"), 1)

            def hg_state(hp):
                pe.wait_ge(S("hg_kdn"), hp + 1)
                for c in range(NCH):
                    half = slice(CH * (c % 2), CH * (c % 2) + CH)
                    if c >= 2:
                        pe.wait_ge(S("hg_S"), NCH * hp + c - 1)
                    for h in range(2):
                        last = mm(bank(6 + c % 2, P, lo=h * P), kdn[half, h, c // 2, :], vn[half, h, c // 2, :],
                                  start=True, stop=True)
                    last.then_inc(S("hg_dS"), 1)

            def hg_out(hp):
                pe.wait_ge(S("hg_S"), NCH * (hp + 1))
                pe.wait_ge(S("hg_sc_used"), 7 * (hp + 1))
                for parity in range(2):
                    for h in range(2):
                        for c in range(parity, NCH, 2):
                            half = slice(CH * parity, CH * parity + CH)
                            out = bank(4 + h, CH, lo=c * CH)
                            pair = (h * 3 + c // 2) * CH
                            last = mm(out, vn[half, h, c // 2, :], hAT[half, pair:pair + CH], start=True, stop=(c == 0))
                            if c:
                                sl = c - 1 if c < 4 else 4
                                last = mm(out, hS[:, sl, 2 * hp + h, :], hq_[:, h * T + c * CH:h * T + c * CH + CH],
                                          start=False, stop=True)
                    last.then_inc(S("hg_o"), 1)
                    pe.wait_ge(S("hg_o"), 2 * hp + parity + 1)
                for h in range(2):
                    pe.wait_ge(S("hg_sq"), 2 * hp + h + 1)
                    mm(bank(6 + h, T), ones[:, :], sq[:, 0, h * T:h * T + T], start=True, stop=True)\
                        .then_inc(S("hg_ss"), 1)

            def ssd_gamma():
                pe.wait_ge(S("dt_done"), 1)
                pe.wait_ge(S("cv_new"), 1)
                pe.wait_ge(S("hg_normed"), 4)
                for q in range(3):
                    n = P if q < 2 else TS
                    for w in range(2):
                        last = tr(bank(6, NH, n, lo=(2 * q + w) * NH), dtw[:, w, q * P:q * P + n],
                                  ident[0:NH, 0:NH])
                last.then_inc(S("bdt_turned"), 1)
                for i in range(NXBC):
                    last = tr(psum[0:6, 3 + i // 4, (i % 4) * P:(i % 4) * P + P], cvout[:, i, :], ident[:, :])
                last.then_inc(S("cv_new_turned"), 1)

            def ssd_nat(q):
                n = P if q < 2 else TS
                pe.wait_ge(S("conv_silu"), NXBC)
                if q == 0:
                    pe.wait_ge(S("cv_stored"), 1)
                    pe.wait_ge(S("bdt_taken"), 1)
                else:
                    pe.wait_ge(S("ssd_done"), 2 * q)
                cols = slice(q * P, q * P + n)
                for i in range(8):
                    tr(bank(4 + i // 4, P, n, lo=(i % 4) * P), xbcT[:, i, cols], ident[:, :])
                tr(bank(6, P, n, lo=0), xbcT[:, 8, cols], ident[:, :])
                for g in range(2):
                    rows = slice(64 * g, 64 * g + 64)
                    for c in range(2 * q, min(2 * q + 2, NCH)):
                        c2 = c % 2
                        last = mm(psum[CH * c2:CH * c2 + CH, 6 + g, P:P + CH],
                                  xbcT[rows, 8, c * CH:c * CH + CH], xbcT[rows, 9, c * CH:c * CH + CH],
                                  start=True, stop=True)
                last.then_inc(S("ssd_nat"), 1)

            def ssd_decay(c):
                pe.wait_ge(S("ssd_diag"), c + 1)
                for g in range(2):
                    last = mm(bank(4 + g), ones[0:NH, :], dg[0:NH, 512 * g:512 * g + 512], start=True, stop=True)
                last.then_inc(S("ssd_b"), 1)

            def ssd_y(c):
                half = slice(CH * (c % 2), CH * (c % 2) + CH)
                pe.wait_ge(S("ssd_vd"), c + 1)
                for g in range(2):
                    rows = slice(64 * g, 64 * g + 64)
                    last = mm(psum[rows, 7, :], bn[half, 64 * g:64 * g + 64], vd[half, 512 * g:512 * g + 512],
                              start=True, stop=True)
                last.then_inc(S("ssd_dS"), 1)
                pe.wait_ge(S("ssd_W"), c + 1)
                if c == 4:
                    pe.wait_ge(S("ssd_in_loaded"), 32)
                def head_out(h):
                    return psum[64 * (h % 2):64 * (h % 2) + 64, 3, (h // 2) * CH:(h // 2) * CH + CH]

                for h in range(NH):
                    last = mm(head_out(h), v_[half, h * 64:h * 64 + 64], W[half, h * CH:h * CH + CH],
                              start=(h < 2), stop=(c == 0 and h >= NH - 2), skip_group_check=True)
                if c:
                    sl = c - 1 if c < 4 else 4
                    for h in range(NH):
                        last = mm(head_out(h), aS[:, sl, (h % 8) * 64:(h % 8) * 64 + 64], ctil[:, h * CH:h * CH + CH],
                                  start=False, stop=(h >= NH - 2), skip_group_check=True)
                last.then_inc(S("ssd_y"), 1)

            for item in PLAN:
                kind = item[0]
                if kind == "in":
                    if item[1] == 0:
                        pe.wait_ge(S("h_prompt"), KD)
                        pe.wait_ge(S("h_sample"), KD)
                    in_mm(item[1])
                elif kind == "ada":
                    ada(item[1])
                elif kind == "s5_in":
                    s5_in(item[1])
                elif kind == "s5_out":
                    s5_out(item[1])
                elif kind == "s5_glu":
                    s5_glu()
                elif kind == "hg_prep":
                    hg_prep(item[1])
                elif kind == "hg_level":
                    hg_level(item[1], item[2])
                elif kind == "hg_kd":
                    hg_kd(item[1])
                elif kind == "hg_state":
                    hg_state(item[1])
                elif kind == "hg_out":
                    hg_out(item[1])
                elif kind == "ssd_gamma":
                    ssd_gamma()
                elif kind == "ssd_nat":
                    ssd_nat(item[1])
                elif kind == "ssd_decay":
                    ssd_decay(item[1])
                elif kind == "ssd_y":
                    ssd_y(item[1])
                elif kind == "ssd_norm":
                    sum_squares(3, 4, "ssd_squares_used")
            pe.wait_ge(S("bulk_evac"), 87)
            pe.wait_ge(S("mod_ready"), 47)
            ada_turn(47)

            pe.wait_ge(S("merged"), 1)
            pe.wait_ge(S("hg_normed"), 4)
            src = [proj[:, Z + i, :] for i in range(8)] + [proj[:, HG + i, :] for i in range(4)] \
                + [proj[:, U + i, :] for i in range(4)]
            for n in range(8):
                r = OUTP + n
                pe.wait_ge(S(f"w_landed{r % RING}"), 16 * (r // RING + 1))
                w = slot[:, r % RING, :].rearrange("p (k n) -> p k n", k=KD)
                for q in range(2):
                    m = 2 * n + q
                    if m >= 4:
                        pe.wait_ge(S("x_mixed"), 2 * (m - 3))
                    for k in range(KD):
                        last = mm(bank(4 + m % 4, T), w[:, k, q * P:(q + 1) * P], src[k], start=(k == 0), stop=(k == KD - 1))
                    last.then_inc(S("out_done"), 1)
            sum_squares(3, 8, "n2_squares_used")
            pe.wait_ge(S("h2_prompt"), KD)
            pe.wait_ge(S("h2_sample"), KD)
            pe.wait_ge(S("router_loaded"), 64)
            for j in range(3):
                n = P if j < 2 else TS
                for k in range(KD):
                    mm(bank(2, 36, n, lo=36 * j), hT[:, k, j * P:j * P + n], wr[:, k, :], start=(k == 0), stop=False)
                last = mm(bank(2, 36, n, lo=36 * j), ones[0:1, 0:n], brow, start=False, stop=True)
            last.then_inc(S("logits"), 1)
            moeg = psum[:, 0:4, 0:T]

            def expert_in(s_, b0, sem):
                w = slot[:, s_, :].rearrange("p (k n) -> p k n", k=KD)
                for f in range(2):
                    for k in range(KD):
                        last = mm(moeg[:, b0 + f, :], w[:, k, f * P:(f + 1) * P], hT[:, k, :],
                                  start=(k == 0), stop=(k == KD - 1))
                    last.then_inc(S(sem), 1)

            def expert_down(s_, count):
                w = slot[:, s_, :].rearrange("p (k n) -> p k n", k=2)
                for m in range(KD):
                    if m >= 4 or count is not None:
                        pe.wait_ge(S("down_added"), (m - 3) if count is None else count + (m - 3))
                    for f in range(2):
                        last = mm(bank(4 + m % 4, T), w[:, f, m * P:(m + 1) * P], act_[:, f * T:f * T + T],
                                  start=(f == 0), stop=(f == 1))
                    last.then_inc(S("down_done"), 1)

            base = PRE // RING
            pe.wait_ge(S("w_landed0"), 16 * (base + 1))
            expert_in(0, 0, "gate_done")
            pe.wait_ge(S("comb_nat"), 1)
            for j in range(3):
                n = P if j < 2 else TS
                last = tr(psum[0:NE, 3, j * P:j * P + n], comb[0:n, j, :], ident[0:n, 0:n])
            last.then_inc(S("comb_turned"), 1)
            pe.wait_ge(S("comb_cols"), 1)
            pe.wait_ge(S("w_landed1"), 16 * (base + 1))
            expert_in(1, 2, "up_done")
            pe.wait_ge(S("w_landed2"), 16 * (base + 1))
            pe.wait_ge(S("gate_silu"), 1)
            expert_in(2, 0, "gate_done")
            pe.wait_ge(S("w_landed0"), 16 * (base + 2))
            pe.wait_ge(S("act_ready"), 1)
            pe.wait_ge(S("x_mixed"), 32)
            expert_down(0, None)
            pe.wait_ge(S("w_landed1"), 16 * (base + 2))
            expert_in(1, 2, "up_done")
            with pe.Fori(2, NE) as e:
                pe.wait_ge(S("w_landed2"), 16 * e + 16 * base)
                pe.wait_ge(S("gate_silu"), e)
                expert_in(2, 0, "gate_done")
                pe.wait_ge(S("w_landed0"), 16 * e + 16 * (base + 1))
                pe.wait_ge(S("act_ready"), e)
                expert_down(0, 16 * e - 16)
                pe.wait_ge(S("w_landed1"), 16 * e + 16 * (base + 1))
                expert_in(1, 2, "up_done")
            pe.wait_ge(S("w_landed2"), 16 * (base + NE))
            pe.wait_ge(S("act_ready"), NE)
            expert_down(2, 16 * (NE - 1))
            sum_squares(3, 8, "n3_squares_used")
            pe.wait_ge(S("y_ready"), 1)
            for g in range(12):
                j, kg = g // 4, g % 4
                n = P if j < 2 else TS
                if g >= 4:
                    pe.wait_ge(S("y_rows"), g - 3)
                for q in range(4):
                    last = tr(bank(4 + g % 4, P, n, lo=q * P), xT[:, 4 * kg + q, j * P:j * P + n], ident[:, :])
                last.then_inc(S("y_turned"), 1)

        @block.vector
        def _(dve):
            v = nc.vector
            st = Steps(dve, "dve_step")
            tt, ts, stt = v.tensor_tensor, v.tensor_scalar, v.scalar_tensor_tensor
            MUL, ADD, SUB = ALU.mult, ALU.add, ALU.subtract

            for g in range(12):
                j, kg = g // 4, g % 4
                n = P if j < 2 else TS
                dve.wait_ge(S("x_turned"), g + 1)
                st(v.tensor_copy(xT[:, 4 * kg:4 * kg + 4, j * P:j * P + n],
                                 bank(4 + g % 4, 4 * n).rearrange("p (q t) -> p q t", q=4)), "x_transposed", wait=False)
            dve.wait_ge(S("c_turned"), 1)
            st(v.tensor_copy(cT[:, :, :], bank(3, 32, lo=384).rearrange("p (k c) -> p k c", k=KD)), "cT_ready")
            dve.wait_ge(S("ld_loaded"), 32)
            dve.wait_ge(S("consts_a"), 1)
            for lo, n in ((0, 16), (32, 8)):
                last = v.tensor_copy(prow[lo:lo + n, 2, :].rearrange("p (g q) -> p g q", g=2),
                                     bc(ldrow[lo:lo + n, :].unsqueeze(2), [n, 2, 64]))
                st(last, "par_rows" if lo else None)
            dve.wait_ge(S("par_turned"), 1)
            st(v.tensor_copy(parT[:, 0:250], bank(3, 250)))
            st(v.tensor_copy(parT[:, 256:352], bank(3, 96, lo=256)), "par_columns")
            dve.wait_ge(S("cv_turned"), 1)
            st(v.tensor_copy(xbcp[:, :, PADS - 3:PADS],
                             bank(2, 40).rearrange("p (i c) -> p i c", i=NXBC)[:, :, 0:3]), "cv_taken")
            st(v.memset(xbcp[:, :, 0:3], 0.0))
            cos_, sin_, dt_, ex, mag, th, wr_, wc, k_, lr, aR, aI, den, nr, cr, ci, t1, t2 = \
                (sm[:, i, :] for i in range(18))
            st(ts(lr, lam_re, -1e-4, None, ALU.min))
            dve.wait_ge(S("s5_dt"), 1)
            st(tt(ex, lr, dt_, MUL), "s5_expo")
            st(tt(th, lam_im, dt_, MUL))
            magic = 12582912.0
            st(ts(k_, th, 0.15915494309189535, magic, MUL, ADD))
            st(ts(k_, k_, magic, None, SUB))
            st(stt(t1, k_, -6.28125, th, MUL, ADD))
            st(stt(t2, k_, -0.0019350051879882812, t1, MUL, ADD))
            st(stt(t1, k_, -3.0199159819e-07, t2, MUL, ADD))
            pi = 3.1415925
            st(ts(wr_, t1, pi, -pi, ALU.min, ALU.max))
            st(stt(t2, wr_, -1.0, wr_, MUL, ALU.max))
            st(ts(wc, t2, -1.0, 1.5707963267948966, MUL, ADD), "s5_wrap")
            dve.wait_ge(S("s5_angles"), 1)
            dve.wait_ge(S("s5_mag"), 1)
            st(tt(aR, mag, cos_, MUL))
            st(tt(aI, mag, sin_, MUL))
            st(tt(t1, lr, lr, MUL))
            st(tt(t2, lam_im, lam_im, MUL))
            st(tt(den, t1, t2, ADD))
            st(v.reciprocal(den, den))
            st(ts(nr, aR, -1.0, None, ADD))
            st(tt(t1, nr, lr, MUL))
            st(tt(t2, aI, lam_im, MUL))
            st(tt(cr, t1, t2, ADD))
            st(tt(cr, cr, den, MUL))
            st(tt(t1, aI, lr, MUL))
            st(tt(t2, nr, lam_im, MUL))
            st(tt(ci, t1, t2, SUB))
            st(tt(ci, ci, den, MUL))
            dve.wait_ge(S("s5_loaded"), 64)
            dve.wait_ge(S("consts_b"), 1)
            for w in range(2):
                b0, b1 = (BR, BI) if w == 0 else (BI, BR)
                for g in range(2):
                    rows = slice(64 * g, 64 * g + 64)
                    crb, cib = (bc(x[rows, :].unsqueeze(2), [64, 16, 16]) for x in (cr, ci))
                    st(tt(btmp[rows], b1[rows], cib, MUL))
                    st(tt(bdp[rows, w, :, g, :], b0[rows], crb, MUL))
                    st(tt(bdp[rows, w, :, g, :], bdp[rows, w, :, g, :], btmp[rows], SUB if w == 0 else ADD))
            for w in range(2):
                for g in range(2):
                    last = st(ts(cpad[:, w, :, g, :], CR[:, w], small[:, g:g + 1], 1.0 if w == 0 else -1.0, MUL, MUL),
                              "s5_mats" if w and g else None)
            dve.wait_ge(S("norm_squares_used"), 8)

            def mean_square(b, width, sem):
                st(ts(rinv[:, :], bank(b, T), 1.0 / width, EPS, MUL, ADD), sem)

            def invert(sem):
                dve.wait_ge(S(sem[0]), sem[1])
                st(v.reciprocal(rinv[:, :], rinv[:, :]))

            def modulate(g, sc, name):
                for s_ in range(2):
                    st(ts(ab1[:, :, s_], seg(sc)[:, :, s_], 1.0, None, ADD))
                    st(tt(ab1[:, :, s_], ab1[:, :, s_], g, MUL))
                dve.wait_ge(S("x_transposed"), 12)
                for k in range(0, KD, 4):
                    st(tt(hT[:, k:k + 4, :], xT[:, k:k + 4, :], bc(rinv[:, :].unsqueeze(1), [P, 4, T]), MUL),
                       f"{name}_scaled" if k == KD - 4 else None)

            def shift_sample(sh, name):
                for k in range(KD):
                    st(ts(hT[:, k, TP:T], hT[:, k, TP:T], ab1[:, k, 1:2], seg(sh)[:, k, 1:2], MUL, ADD),
                       f"{name}_sample", wait=False)

            mean_square(3, D, "n1_mean")
            invert(("n1_root", 1))
            dve.wait_ge(S("s5_mats_turned"), 1)
            for w in range(2):
                st(v.tensor_copy(BDT[:, w], bank(4 + w).rearrange("p (u n) -> p u n", u=4)))
                st(v.tensor_copy(CT[:, w], bank(6 + w).rearrange("p (u n) -> p u n", u=4)),
                   "s5_mats_ready" if w else None)
            lb, omlb, e_, r_ = (small[:, 40 + 4 * i:44 + 4 * i] for i in range(4))
            st(tt(e_, lb_raw, lb_raw, SUB))
            st(ts(e_, e_, 1.0, None, ADD))
            st(v.reciprocal(r_, e_))
            st(tt(e_, e_, r_, MUL))
            st(tt(lb, e_, e_, SUB))
            st(ts(omlb, lb, -1.0, 1.0, MUL, ADD))

            def mod_take(j, q, n):
                src = bank(2, 4, lo=64 + 4 * (j % 2)).rearrange("p (q c) -> p q c", q=2)
                return v.tensor_tensor(q, src, n, ADD)

            for j in range(4):
                dve.wait_ge(S("mod_turned"), j + 1)
                mod_take(j, modT[:, 2 * j:2 * j + 2, :], bc(b_ada[:, 2 * j:2 * j + 2].unsqueeze(2), [P, 2, 2]))\
                    .then_inc(S("mod_ready"), 1)
            with dve.Fori(1, 4) as i:
                for j in range(4):
                    dve.wait_ge(S("mod_turned"), 4 * i + (j + 1))
                    mod_take(j, modT[:, bass.ds(i * 8 + 2 * j, 2), :],
                             bc(b_ada[:, bass.ds(i * 8 + 2 * j, 2)].unsqueeze(2), [P, 2, 2]))\
                        .then_inc(S("mod_ready"), 1)
            dve.wait_ge(S("mod_ready"), 16)
            modulate(g_mix, 1, "h")
            shift_sample(0, "h")

            def ada(i):
                if i > 16:
                    take(i - 1)

            def take(i):
                dve.wait_ge(S("mod_turned"), i + 1)
                mod_take(i, modT[:, 2 * i:2 * i + 2, :], bc(b_ada[:, 2 * i:2 * i + 2].unsqueeze(2), [P, 2, 2]))\
                    .then_inc(S("mod_ready"), 1)

            def s5_in(b):
                br, bi, yr, yi, tm = s5b[0:5]
                pc, ps = s5b[5 + 2 * (b % 2)], s5b[6 + 2 * (b % 2)]
                dve.wait_ge(S("s5_bu_sb"), 2 * b + 2)
                dve.wait_ge(S("s5_table"), b + 1)
                if b:
                    dve.wait_ge(S("s5_y"), b)
                st(tt(yr, br, pc, MUL))
                st(tt(tm, bi, ps, MUL))
                st(tt(yr, yr, tm, ADD))
                st(tt(yi, bi, pc, MUL))
                st(tt(tm, br, ps, MUL))
                st(tt(yi, yi, tm, SUB))
                for i in range(2):
                    n = 2 * b + i
                    for lo, hi in STREAMS:
                        for src, dst, x0 in ((yr, br, x0re), (yi, bi, x0im)):
                            last = v.tensor_tensor_scan(
                                dst[:, i * T + lo:i * T + hi], bc(mag[:, n:n + 1], [P, hi - lo]),
                                src[:, i * T + lo:i * T + hi], x0[:, n:n + 1] if lo else 0.0, MUL, ADD)
                            st(last, wait=False)
                dve.wait_ge(S("dve_step"), st.n["dve_step"])
                st(tt(yr, br, pc, MUL))
                st(tt(tm, bi, ps, MUL))
                st(tt(yr, yr, tm, SUB))
                st(tt(yi, br, ps, MUL))
                st(tt(tm, bi, pc, MUL))
                st(tt(yi, yi, tm, ADD))
                for k, (src, col) in enumerate(((yr, TP - 1), (yi, TP - 1), (yr, T - 1), (yi, T - 1))):
                    st(v.tensor_copy(s5fin[:, k, 2 * b:2 * b + 2].unsqueeze(2),
                                     src.rearrange("p (i t) -> p i t", i=2)[:, :, col:col + 1]),
                       "s5_turned" if k == 3 else None)

            def s5_out(b):
                if b % 2 == 0:
                    return
                u = b // 2
                y, y3 = sq[:, 1, T:2 * T], sq[:, 1, 0:T]
                dve.wait_ge(S("s5_y"), b + 1)
                st(stt(y, proj[:, U + u, :], s5_d[:, u:u + 1], bank(3, T), MUL, ADD))
                st(tt(y3, y, y, MUL))
                st(ts(y3, y3, 0.044715, 1.0, MUL, ADD))
                st(tt(y3, y3, y, MUL))
                st(ts(y3, y3, 1.5957691216057308, None, MUL), "s5_gelu_arg")
                dve.wait_ge(S("s5_gelu_sig"), u + 1)
                st(tt(proj[:, U + u, :], y, y3, MUL), "s5_g")

            def s5_glu():
                dve.wait_ge(S("glu_mm"), 4)
                for m in range(4):
                    dve.wait_ge(S("glu_sig"), m + 1)
                    st(tt(proj[:, U + m, :], proj[:, U + m, :], rinv[:, :], MUL), "glu_used")
                dve.wait_ge(S("s5_fin_turned"), 1)
                st(v.tensor_copy(sq[0:16, 1, 0:512], psum[0:16, 3, :]), "s5_fin_rows")

            hb3 = lambda t, m: t.rearrange("p (n r) -> p n r", r=2 * m)

            def hg_prep(hp):
                hf = flat[:, (HF + 2 * hp) * T:(HF + 2 * hp + 2) * T]
                dve.wait_ge(S("hg_sig"), hp + 1)
                for h in range(2):
                    c = slice(h * T, h * T + T)
                    n = 2 * hp + h
                    st(ts(hE[:, c], hE[:, c], omlb[:, n:n + 1], lb[:, n:n + 1], MUL, ADD))
                    st(ts(hf[:, c], hf[:, c], omlb[:, n:n + 1], None, MUL), "hg_k" if h else None)
                if hp:
                    dve.wait_ge(S("hg_o"), 2)
                st(ts(hE, hE, 1e-30, None, ALU.max))
                st(ts(hq_, hE, 2.0 ** -40, None, ALU.is_lt))
                st(ts(hb, hq_, 2.0 ** 50, 1.0, MUL, ADD))
                st(tt(hE, hE, hb, MUL), "hg_f")
                dve.wait_ge(S("hg_ln"), hp + 1)
                st(stt(hE, hq_, -34.657359, hE, MUL, ADD))
                for h in range(2):
                    c = slice(h * T, h * T + T)
                    st(v.tensor_tensor_scan(hb[:, c], rmask[:, :], hE[:, c], 0.0, MUL, ADD))
                dve.wait_ge(S("hg_v"), hp + 1)
                for h in range(2):
                    b3 = bank(6 + h, 384).rearrange("p (q k) -> p q k", q=3)
                    st(v.tensor_copy(vn[:, h, 0:2, :], b3[:, 0:2, :]))
                    st(v.tensor_copy(vn[0:64, h, 2, :], b3[0:64, 2, :]), "hg_vn" if h else None)

            def hg_take(hp, lv):
                it = 7 * hp + lv
                dve.wait_ge(S("hg_sc"), it + 1)
                src = bank(4 + it % 2, 384).rearrange("p (n t) -> p n t", n=6)
                dst = (hAT if lv == 0 else htmp).rearrange("p (n t) -> p n t", n=6)
                mask = bc(lmask[:, lv, :].unsqueeze(1), [P, 6, CH])
                st(tt(dst, src, mask, MUL), "hg_sc_used")
                if lv:
                    st(tt(hAT, hAT, htmp, ADD))

            def hg_level(hp, lv):
                q_, k_ = (flat[:, (x + 2 * hp) * T:(x + 2 * hp + 2) * T] for x in (HQ, HF))
                if lv == 0:
                    return
                m = LEVELS[lv]
                b3 = hb3(hb, m)
                st(tt(hb3(hE, m), b3, bc(b3[:, :, m - 1:m], [P, 640 // (2 * m), 2 * m]), SUB))
                st(stt(hE, hE, -1.0, hE, MUL, ALU.min), "hg_expo")
                hg_take(hp, lv - 1)
                dve.wait_ge(S("hg_exp"), 6 * hp + lv)
                st(tt(hq_, q_, hE, MUL))
                st(tt(hk_, k_, hE, MUL), "hg_qk")

            def hg_kd(hp):
                q_, k_ = (flat[:, (x + 2 * hp) * T:(x + 2 * hp + 2) * T] for x in (HQ, HF))
                hg_take(hp, 6)
                st(v.memset(small[:, 60:61], 0.0), "hg_expo2")
                dve.wait_ge(S("hg_exp2"), 2 * hp + 1)
                st(tt(hq_, q_, hE, MUL))
                e3, b3 = (t.rearrange("p (n r) -> p n r", r=CH) for t in (hE, hb))
                st(v.tensor_copy(small[:, 80:90].unsqueeze(2), e3[:, :, CH - 1:CH]))
                st(tt(e3, bc(b3[:, :, CH - 1:CH], [P, 10, CH]), b3, SUB), "hg_expo2")
                dve.wait_ge(S("hg_exp2"), 2 * hp + 2)
                st(tt(hE, k_, hE, MUL), "hg_kd")
                for h in range(2):
                    dve.wait_ge(S("hg_kd_turned"), 2 * hp + h + 1)
                    b4 = bank(6 + h, 384).rearrange("p (q k) -> p q k", q=3)
                    st(v.tensor_copy(kdn[:, h, 0:2, :], b4[:, 0:2, :]))
                    st(v.tensor_copy(kdn[0:64, h, 2, :], b4[0:64, 2, :]), "hg_kdn" if h else None)

            def hg_state(hp):
                for c in range(NCH):
                    dve.wait_ge(S("hg_dS"), NCH * hp + c + 1)
                    if c == 4:
                        dve.wait_ge(S("hg_in_loaded"), 16)
                    into = (0, 1, 2, 3, 5)[c]
                    frm = (None, 0, 1, 2, 4)[c]
                    for h in range(2):
                        add = bank(6 + c % 2, P, lo=h * P)
                        dst = hS[:, into, 2 * hp + h, :]
                        if frm is None:
                            last = v.tensor_copy(dst, add)
                        else:
                            last = stt(dst, hS[:, frm, 2 * hp + h, :], small[:, 80 + 5 * h + c:81 + 5 * h + c],
                                       add, MUL, ADD)
                        st(last, "hg_S" if h else None)

            def hg_out(hp):
                for h in range(2):
                    n = 2 * hp + h
                    dve.wait_ge(S("hg_ss"), n + 1)
                    st(ts(rinv[:, :], bank(6 + h, T), 1.0 / P, EPS, MUL, ADD), "hg_var")
                    invert(("hg_root", n + 1))
                    st(stt(hb[:, 0:T], bank(4 + h, T), hg_g[:, n:n + 1], rinv[:, :], MUL, MUL))
                    dve.wait_ge(S("hg_gate"), hp + 1)
                    st(tt(proj[:, HG + n, :], proj[:, HG + n, :], hb[:, 0:T], MUL), "hg_normed")

            def ssd_conv():
                dve.wait_ge(S("bulk_evac"), 55)
                dve.wait_ge(S("bulk_done"), 55)
                dve.wait_ge(S("hg_state_stored"), 32)
                st(v.memset(ctil, 0.0))
                bias, alog = small[0:NH, 32:33], small[0:NH, 34:35]
                x_, e_, u_, l_, raw = (dtw[:, i, :] for i in range(5))
                st(v.tensor_copy(raw, dt_raw))
                st(ts(raw, raw, bias, None, ADD))
                st(stt(x_, raw, -1.0, raw, MUL, ALU.min), "dt_neg")
                dve.wait_ge(S("dt_exp"), 1)
                st(ts(u_, e_, 1.0, None, ADD), "dt_one")
                dve.wait_ge(S("dt_ln"), 1)
                st(ts(u_, u_, -1.0, None, ADD))
                st(ts(x_, u_, 0.0, None, ALU.is_equal))
                st(tt(u_, u_, x_, ADD))
                st(tt(l_, l_, x_, ADD))
                st(v.reciprocal(u_, u_))
                st(tt(l_, l_, e_, MUL))
                st(tt(l_, l_, u_, MUL))
                st(ts(x_, raw, 0.0, None, ALU.max))
                st(tt(dtw[:, 1, :], x_, l_, ADD))
                dve.wait_ge(S("a_exp"), 1)
                st(ts(l_, dtw[:, 1, :], alog, -1.0, MUL, MUL))
                st(v.tensor_tensor_scan(dtw[:, 0, :], rmask[0:NH, :], l_, 0.0, MUL, ADD), "dt_done")
                for s_, c0 in ((0, PADP + TP - 3), (1, PADS + TS - 3)):
                    st(v.tensor_copy(cvout[:, :, 3 * s_:3 * s_ + 3], xbcp[:, :, c0:c0 + 3]), "cv_new" if s_ else None)
                for i in range(NXBC):
                    for lo, hi in STREAMS:
                        p0 = (PADP if lo == 0 else PADS) - 3
                        n = hi - lo
                        dst = xbcT[:, i, lo:hi]
                        st(ts(dst, xbcp[:, i, p0:p0 + n], conv_w[:, 0, i:i + 1], conv_b[:, i:i + 1], MUL, ADD))
                        for j in range(1, 4):
                            st(stt(dst, xbcp[:, i, p0 + j:p0 + j + n], conv_w[:, j, i:i + 1], dst, MUL, ADD),
                               "conv_out" if lo and j == 3 else None)

            def ssd_gamma():
                dve.wait_ge(S("bdt_turned"), 1)
                src = bank(6, 96).rearrange("p (q w h) -> p q w h", q=3, w=2)
                st(v.tensor_copy(bnat[:, 0:2].rearrange("p q w h -> p (q w h)"), bank(6, 64)))
                st(v.tensor_copy(bnat[0:64, 2].rearrange("p w h -> p (w h)"), bank(6, 32, 64, lo=64)), "bdt_taken")
                dve.wait_ge(S("cv_new_turned"), 1)
                st(v.tensor_copy(cvst[0:6, :], psum[0:6, 3:6, :].rearrange("p b n -> p (b n)")[:, 0:NXBC * P]),
                   "cv_stored")

            def ssd_nat(q):
                n = P if q < 2 else TS
                if q == 0:
                    dve.wait_ge(S("cv_saved"), 32)
                dve.wait_ge(S("ssd_nat"), q + 1)
                st(tt(v_[0:n, :].rearrange("p (h n) -> p h n", h=NH),
                      psum[0:n, 4:6, :].rearrange("p b n -> p (b n)").rearrange("p (h n) -> p h n", h=NH),
                      bc(bnat[0:n, q, 1, :].unsqueeze(2), [n, NH, 64]), MUL))
                st(v.tensor_copy(bn[0:n, :], bank(6, P, n)))
                st(tt(gtm[0:n, :].rearrange("p (g t) -> p g t", g=2), psum[0:n, 6:8, P:P + CH],
                      bc(causal[0:n, :].unsqueeze(1), [n, 2, CH]), MUL), "ssd_nat_used")

            def ssd_decay(c):
                half = slice(CH * (c % 2), CH * (c % 2) + CH)
                cols = slice(c * CH, c * CH + CH)
                q = c // 2
                st(tt(dg[0:NH, :].rearrange("p (h t) -> p h t", h=NH),
                      bc(dtw[:, 0, cols].unsqueeze(1), [NH, NH, CH]),
                      bc(ident[0:NH, 0:NH].unsqueeze(2), [NH, NH, CH]), MUL), "ssd_diag")
                dve.wait_ge(S("ssd_b"), c + 1)
                bB = psum[half, 4:6, :].rearrange("p b n -> p (b n)").rearrange("p (h t) -> p h t", h=NH)
                dl = small[half, 64:80]
                st(tt(dl, bB[:, :, CH - 1], bnat[half, q, 0, :], SUB))
                w3 = W[half, :].rearrange("p (h t) -> p h t", h=NH)
                st(tt(w3, bB, bc(bnat[half, q, 0, :].unsqueeze(2), [CH, NH, CH]), SUB), "ssd_diff")
                st(ts(W[half, :], W[half, :], 0.0, None, ALU.min), "ssd_diff")
                dve.wait_ge(S("ssd_exp"), 2 * c + 1)
                st(tt(vd[half, :].rearrange("p (h n) -> p h n", h=NH), v_[half, :].rearrange("p (h n) -> p h n", h=NH),
                      bc(dl.unsqueeze(2), [CH, NH, 64]), MUL), "ssd_vd")
                dve.wait_ge(S("ssd_EB"), 2 * c + 2)
                e3 = EB.rearrange("p (j t) -> p j t", j=8)
                for g in range(2):
                    rows = slice(64 * g, 64 * g + 64)
                    st(tt(ctil[rows, 512 * g:512 * g + 512].rearrange("p (j t) -> p j t", j=8), e3[rows],
                          bc(xbcT[rows, 9, cols].unsqueeze(1), [64, 8, CH]), MUL))
                dve.wait_ge(S("ssd_exp"), 2 * c + 2)
                for g in range(2):
                    st(tt(W[half, 512 * g:512 * g + 512].rearrange("p (h t) -> p h t", h=8),
                          W[half, 512 * g:512 * g + 512].rearrange("p (h t) -> p h t", h=8),
                          bc(gtm[half, g * CH:g * CH + CH].unsqueeze(1), [CH, 8, CH]), MUL), "ssd_W" if g else None)

            def ssd_y(c):
                cols = slice(c * CH, c * CH + CH)
                e3 = EB.rearrange("p (j t) -> p j t", j=8)
                into = (0, 1, 2, 3, 5)[c]
                frm = (None, 0, 1, 2, 4)[c]
                dve.wait_ge(S("ssd_dS"), c + 1)
                if frm is None:
                    st(v.tensor_copy(aS[:, into, :], bank(7)))
                else:
                    if c == 4:
                        dve.wait_ge(S("ssd_in_loaded"), 32)
                    st(tt(aS[:, into, :].rearrange("p (j n) -> p j n", j=8),
                          aS[:, frm, :].rearrange("p (j n) -> p j n", j=8),
                          bc(e3[:, :, CH - 1:CH], [P, 8, 64]), MUL))
                    st(tt(aS[:, into, :], aS[:, into, :], bank(7), ADD))
                st(v.memset(small[:, 61:62], 0.0), "ssd_S")
                y3 = ytmp.rearrange("p (i t) -> p i t", i=8)
                st(tt(y3, xbcT[:, 0:8, cols], bc(ssd_D.unsqueeze(2), [P, 8, CH]), MUL))
                dve.wait_ge(S("ssd_y"), c + 1)
                st(tt(ytmp, ytmp, bank(3), ADD))
                dve.wait_ge(S("z_silu"), 1)
                st(tt(proj[:, 0:8, cols], proj[:, 0:8, cols], y3, MUL), "ssd_done")

            def ssd_norm():
                dve.wait_ge(S("ssd_squares_used"), 4)
                mean_square(3, 1024, "ssd_mean")
                invert(("ssd_root", 1))
                z = proj[:, 0:8, :]
                st(tt(z, z, bc(rinv[:, :].unsqueeze(1), [P, 8, T]), MUL))
                st(tt(z, z, bc(ssd_g.unsqueeze(2), [P, 8, T]), MUL), "merged")

            for item in PLAN:
                kind = item[0]
                if kind == "ada":
                    ada(item[1])
                elif kind == "s5_in":
                    s5_in(item[1])
                elif kind == "s5_out":
                    s5_out(item[1])
                elif kind == "s5_glu":
                    s5_glu()
                elif kind == "hg_prep":
                    hg_prep(item[1])
                elif kind == "hg_level":
                    hg_level(item[1], item[2])
                elif kind == "hg_kd":
                    hg_kd(item[1])
                elif kind == "hg_state":
                    hg_state(item[1])
                elif kind == "hg_out":
                    hg_out(item[1])
                elif kind == "ssd_conv":
                    ssd_conv()
                elif kind == "ssd_gamma":
                    ssd_gamma()
                elif kind == "ssd_nat":
                    ssd_nat(item[1])
                elif kind == "ssd_decay":
                    ssd_decay(item[1])
                elif kind == "ssd_y":
                    ssd_y(item[1])
                elif kind == "ssd_norm":
                    ssd_norm()
            take(47)
            dve.wait_ge(S("mod_ready"), 48)

            for m in range(KD):
                dve.wait_ge(S("out_done"), m + 1)
                for s_, (lo, hi) in enumerate(STREAMS):
                    st(stt(xT[:, m, lo:hi], bank(4 + m % 4, T)[:, lo:hi], seg(2)[:, m, s_:s_ + 1],
                           xT[:, m, lo:hi], MUL, ADD), "x_mixed", wait=False)
            dve.wait_ge(S("x_mixed"), 32)
            dve.wait_ge(S("n2_squares_used"), 8)
            mean_square(3, D, "n2_mean")
            invert(("n2_root", 1))
            modulate(g_ffn, 4, "h2")
            shift_sample(3, "h2")

            lg = rt[:, 400:508].rearrange("p (j e) -> p j e", j=3)
            states_stored(dve)
            st(v.memset(rt[:, 0:640], 0.0))
            dve.wait_ge(S("logits"), 1)
            st(v.tensor_copy(rt[:, 400:472], bank(2, 72)))
            st(v.tensor_copy(rt[0:64, 472:508], bank(2, 36, 64, lo=72)))
            G = lg[:, :, 0:4]
            ex4 = rt[:, 16:28].rearrange("p (j e) -> p j e", j=3)
            m3 = rt[:, 0:3].unsqueeze(2)
            st(v.tensor_reduce(m3, G, AX.X, ALU.max))
            st(tt(ex4, G, bc(m3, [P, 3, 4]), SUB))

            def first_max(dst, src, mx, n, tmp, idx):
                c = bc(small[:, 16:16 + n].unsqueeze(1), [P, 3, n])
                st(tt(dst, src, bc(mx, [P, 3, n]), ALU.is_equal))
                st(tt(tmp, dst, c, MUL))
                st(v.tensor_reduce(idx, tmp, AX.X, ALU.min))
                st(tt(dst, c, bc(idx, [P, 3, n]), ALU.is_equal))

            f3 = lambda off, n: rt[:, off:off + 3 * n].rearrange("p (j e) -> p j e", j=3)
            idx = rt[:, 4:7].unsqueeze(2)
            oh4 = f3(32, 4)
            first_max(oh4, G, m3, 4, f3(48, 4), idx)
            le4 = rt[:, 128:224].rearrange("p (j e) -> p j e", j=3)
            for g in range(4):
                st(tt(le4[:, :, 8 * g:8 * g + 8], lg[:, :, 4 + 8 * g:12 + 8 * g], bc(oh4[:, :, g:g + 1], [P, 3, 8]), MUL))
            le = f3(64, 8)
            st(tt(le, le4[:, :, 0:8], le4[:, :, 8:16], ADD))
            st(tt(le, le, le4[:, :, 16:24], ADD))
            st(tt(le, le, le4[:, :, 24:32], ADD))
            v1, v2 = rt[:, 8:11].unsqueeze(2), rt[:, 12:15].unsqueeze(2)
            oh1, oh2, tmp8, le2 = f3(96, 8), f3(256, 8), f3(288, 8), f3(320, 8)
            st(v.tensor_reduce(v1, le, AX.X, ALU.max))
            first_max(oh1, le, v1, 8, tmp8, idx)
            st(stt(le2.rearrange("p j e -> p (j e)"), oh1.rearrange("p j e -> p (j e)"), -3e38,
                   le.rearrange("p j e -> p (j e)"), MUL, ADD))
            st(v.tensor_reduce(v2, le2, AX.X, ALU.max))
            first_max(oh2, le2, v2, 8, tmp8, idx)
            st(tt(rt[:, 240:243].unsqueeze(2), v2, v1, SUB), "rt_expo")
            dve.wait_ge(S("rt_exp"), 1)
            e2, den, w1, w2 = (rt[:, 240 + 3 * i:243 + 3 * i].unsqueeze(2) for i in range(4))
            st(v.tensor_reduce(den, ex4, AX.X, ALU.add))
            st(v.reciprocal(den, den))
            st(ts(w1, e2, 1.0, None, ADD))
            st(v.reciprocal(w1, w1))
            st(tt(w1, w1, den, MUL))
            st(tt(w2, w1, e2, MUL))
            st(tt(oh1, oh1, bc(w1, [P, 3, 8]), MUL))
            st(tt(oh2, oh2, bc(w2, [P, 3, 8]), MUL))
            st(tt(oh1, oh1, oh2, ADD))
            for g in range(4):
                st(tt(comb[:, :, 8 * g:8 * g + 8], oh1, bc(oh4[:, :, g:g + 1], [P, 3, 8]), MUL),
                   "comb_nat" if g == 3 else None)
            dve.wait_ge(S("comb_turned"), 1)
            st(v.tensor_copy(combT, psum[0:NE, 3, 0:T]), "comb_cols")
            dve.wait_ge(S("comb_loaded"), 16)
            s3 = sgc.rearrange("p (f t) -> p f t", f=2)
            a3 = act_.rearrange("p (f t) -> p f t", f=2)

            def activate(e):
                cb = combB[:, e * T:e * T + T] if isinstance(e, int) else combB[:, bass.ds(e * T, T)]
                tt(s3, s3, bc(cb.unsqueeze(1), [P, 2, T]), MUL).then_inc(S("moe_mul"), 1)

            def accumulate(first, count):
                for m in range(KD):
                    dve.wait_ge(S("down_done"), count + (m + 1))
                    if first:
                        v.tensor_copy(acc[:, m, :], bank(4 + m % 4, T)).then_inc(S("down_added"), 1)
                    else:
                        tt(acc[:, m, :], acc[:, m, :], bank(4 + m % 4, T), ADD).then_inc(S("down_added"), 1)

            dve.wait_ge(S("gate_silu"), 1)
            activate(0)
            dve.wait_ge(S("moe_mul"), 1)
            dve.wait_ge(S("up_done"), 2)
            tt(a3, s3, psum[:, 2:4, 0:T], MUL).then_inc(S("act_ready"), 1)
            dve.wait_ge(S("gate_silu"), 2)
            activate(1)
            accumulate(True, 0)
            dve.wait_ge(S("moe_mul"), 2)
            dve.wait_ge(S("up_done"), 4)
            tt(a3, s3, psum[:, 2:4, 0:T], MUL).then_inc(S("act_ready"), 1)
            with dve.Fori(2, NE) as e:
                dve.wait_ge(S("gate_silu"), e + 1)
                activate(e)
                accumulate(False, 16 * e - 16)
                dve.wait_ge(S("moe_mul"), e + 1)
                dve.wait_ge(S("up_done"), 2 * e + 2)
                tt(a3, s3, psum[:, 2:4, 0:T], MUL).then_inc(S("act_ready"), 1)
            accumulate(False, 16 * (NE - 1))
            dve.wait_ge(S("down_added"), 16 * NE)
            for m in range(KD):
                for s_, (lo, hi) in enumerate(STREAMS):
                    st(stt(xT[:, m, lo:hi], acc[:, m, lo:hi], seg(5)[:, m, s_:s_ + 1], xT[:, m, lo:hi], MUL, ADD),
                       "x_final", wait=False)
            dve.wait_ge(S("x_final"), 32)
            dve.wait_ge(S("n3_squares_used"), 8)
            mean_square(3, D, "n3_mean")
            invert(("n3_root", 1))
            for k in range(KD):
                st(stt(xT[:, k, :], xT[:, k, :], g_fin[:, k:k + 1], rinv[:, :], MUL, MUL), wait=False)
            dve.wait_ge(S("dve_step"), st.n["dve_step"])
            st(v.memset(small[:, 62:63], 0.0), "y_ready")
            for g in range(12):
                j, kg = g // 4, g % 4
                n = P if j < 2 else TS
                dve.wait_ge(S("y_turned"), g + 1)
                st(v.tensor_copy(ynat[0:n, j, kg * 512:kg * 512 + 512], bank(4 + g % 4, 512, n)), "y_rows", wait=False)


_INS = ["x_prompt", "x_sample", "c_prompt", "c_sample", "state_conv", "state_ssd", "state_hgrn", "state_s5_re",
        "state_s5_im", "w_ada", "b_ada", "g_mix", "g_ffn", "w_in", "conv_w", "conv_b", "ssd_dt_bias", "ssd_a_log",
        "ssd_d", "ssd_norm_g", "hgrn_lb_raw", "hgrn_norm_g", "s5_lam_re", "s5_lam_im", "s5_log_dt", "s5_b_re",
        "s5_b_im", "s5_c_re", "s5_c_im", "s5_d", "s5_w_glu", "s5_b_glu", "w_out", "w_router_group",
        "b_router_group", "w_router_expert", "b_router_expert", "w_exp_gate", "w_exp_up", "w_exp_down", "g_final"]
_STATES = [("conv", (1, 1, 3, 1280)), ("ssd", (1, 1, 16, 64, 64)), ("hgrn", (1, 1, 4, 128, 128)),
           ("s5re", (1, 1, 32, 64)), ("s5im", (1, 1, 32, 64))]
_OUTS = [("y_prompt", (1, TP, D)), ("y_sample", (1, TS, D))] \
    + [(f"{n}_{s}", shape) for s in "ps" for n, shape in _STATES]


def kernel(**inputs):
    import numpy as _np
    import concourse.bacc as _bacc
    from concourse.bass_utils import run_bass_kernel_spmd as _run

    nc = _bacc.Bacc("TRN2", target_bir_lowering=False, num_devices=1)
    arrays, ins, outs = {}, {}, {}
    for name in _INS:
        x = _np.ascontiguousarray(inputs[name])
        arrays[f"in_{name}"] = x
        ins[name] = nc.dram_tensor(f"in_{name}", x.shape, mybir.dt.from_np(x.dtype), kind="ExternalInput").ap()
    for name, shape in _OUTS:
        outs[name] = nc.dram_tensor(f"out_{name}", shape, F32, kind="ExternalOutput").ap()
    build(nc, ins, outs)
    r = _run(nc, [arrays], core_ids=[0])
    return tuple(r.results[0][f"out_{name}"] for name, _ in _OUTS)
```

```python
from contextlib import ExitStack

import concourse.bass as bass
from concourse import mybir

F32 = mybir.dt.float32
I32 = mybir.dt.int32
ALU = mybir.AluOpType
ACT = mybir.ActivationFunctionType
AX = mybir.AxisListType

P = 128
D = 2048
KD = D // P
TP, TS = 256, 64
T = TP + TS
CH = 64
NCH = T // CH
STREAMS = ((0, TP), (TP, T))
NXBC = 10
PADP, PADS = 3, 3 + TP + 3
TPAD = T + 6
Z, HQ, HF, HI, HG, U = 0, 8, 12, 16, 20, 24
NPROJ = 28
NH = 16
CW = 256
RING = 4
ADA1, INP, ADA2, OUTP, PRE = 0, 16, 36, 68, 76
NE = 32
CAP = 64
NPAIR = NE // 2
QUADS = NE // 4
COL_HG, COL_DT = 2320, 2304
NORM = {"n1": 0, "ssd": 8, "n2": 12, "n3": 20}
LEVELS = (0, 32, 16, 8, 4, 2, 1)
EPS = 1e-6

IN_CHUNKS = [(4368, U), (4624, U + 2), (COL_DT, None), (0, Z)]
IN_CHUNKS += [(COL_HG + CW * i, HQ + 2 * i) for i in range(8)]
IN_CHUNKS += [(CW * i, Z + 2 * i) for i in range(1, 4)]
IN_CHUNKS += [(1024 + CW * i, 100 + 2 * i) for i in range(5)]


def make_plan():
    bulk = [("in", n) for n in range(4, 20)] + [("ada", a) for a in range(16, 48)]
    s5 = []
    for b in range(8):
        s5 += [("s5_in", b), None, ("s5_out", b)]
    s5 += [None, ("s5_glu", 0)]
    hg = []
    for hp in range(2):
        hg += [("hg_prep", hp), None]
        for lv in range(len(LEVELS)):
            hg += [("hg_level", hp, lv), None]
        hg += [("hg_kd", hp), None, ("hg_state", hp), None, ("hg_out", hp), None]
    ssd = [("ssd_conv", 0), None, None, ("ssd_gamma", 0), None]
    for c in range(NCH):
        if c % 2 == 0:
            ssd += [("ssd_nat", c // 2), None]
        ssd += [("ssd_decay", c), None, ("ssd_y", c)]
    ssd += [None, ("ssd_norm", 0)]
    plan = [("in", n) for n in range(4)]
    for item in s5 + hg + ssd:
        if item is None:
            if bulk:
                plan.append(bulk.pop(0))
        else:
            if item[0] == "ssd_conv":
                while bulk and bulk[0][0] == "in":
                    plan.append(bulk.pop(0))
            plan.append(item)
    return plan + bulk


PLAN = make_plan()


def build(nc, a, o):
    ctx = ExitStack()
    with ctx:
        def sb(name, shape, dt=F32):
            return ctx.enter_context(nc.sbuf_tensor(name, shape, dt))

        sems = {}

        def S(name):
            if name not in sems:
                sems[name] = ctx.enter_context(nc.semaphore(name))
            return sems[name]

        psum = ctx.enter_context(nc.psum_tensor("psum", [P, 8, 512], F32))

        def bank(b, cols=512, part=P, lo=0):
            return psum[0:part, b, lo:lo + cols]

        xT = sb("xT", [P, KD, T])
        hT = sb("hT", [P, KD, T])
        slot = sb("slot", [P, RING, KD * CW])
        mem = sb("mem", [P, NPROJ * T + NXBC * TPAD + 7808])
        sq = sb("sq", [P, 2, 2 * T])
        rinv = sb("rinv", [P, T])
        ident = sb("ident", [P, P])
        ones = sb("ones", [P, P])
        rmask = sb("rmask", [P, T])
        lmask = sb("lmask", [P, len(LEVELS), CH])
        causal = sb("causal", [P, CH])
        parT = sb("parT", [P, 3 * P])
        modT = sb("modT", [P, 6 * KD, 2])
        rows = sb("rows", [64, 2 * CW])
        modrow = rows[0:2, :].rearrange("p (j n) -> p j n", j=2)
        dt_raw = rows[32:48, 0:T]
        cT = sb("cT", [P, KD, 2])
        sm = sb("sm", [P, 18, 16])
        BDT = sb("BDT", [P, 2, 4, P])
        CT = sb("CT", [P, 2, 4, P])
        ab1 = sb("ab1", [P, KD, 2])
        small = sb("small", [P, 96])
        s5fin = sb("s5fin", [P, 4, 16])

        proj = mem[:, 0:NPROJ * T].rearrange("p (n t) -> p n t", n=NPROJ)
        XB0 = NPROJ * T
        xbcp = mem[:, XB0:XB0 + NXBC * TPAD].rearrange("p (n t) -> p n t", n=NXBC)
        A0 = XB0 + NXBC * TPAD

        def ar(off, n):
            return mem[:, A0 + off:A0 + off + n]

        flat = mem[:, :]
        xnat = ar(0, 3 * D).rearrange("p (j d) -> p j d", j=3)
        prow = flat[:, 0:384].rearrange("p (j d) -> p j d", j=3)
        crow = flat[0:2, 384:384 + D]
        BR = flat[:, 2432:2688].rearrange("p (i j) -> p i j", i=16)
        BI = flat[:, 2688:2944].rearrange("p (i j) -> p i j", i=16)
        CR = flat[:, 2944:3456].rearrange("p (w u q) -> p w u q", w=2, u=4)
        bdp = flat[:, 3456:4480].rearrange("p (w i g j) -> p w i g j", w=2, i=16, g=2)
        cpad = flat[:, 4480:5504].rearrange("p (w u g q) -> p w u g q", w=2, u=4, g=2)
        btmp = flat[:, 5504:5760].rearrange("p (i j) -> p i j", i=16)
        cvrow = flat[0:3, 5760:7040]
        ldrow = flat[0:48, 7040:7042]
        s5b = [ar(640 * i, 640) for i in range(9)]
        wglu = ar(5760, 2048).rearrange("p (k m) -> p k m", k=4)
        hb, hE, hq_, hk_ = (ar(640 * i, 640) for i in range(4))
        htmp = ar(2560, 384)
        kdn = ar(1920, 768).rearrange("p (h q k) -> p h q k", h=2, q=3)
        hAT = ar(2944, 384)
        vn = ar(3328, 768).rearrange("p (h q k) -> p h q k", h=2, q=3)
        hS = ar(4096, 3072).rearrange("p (s h v) -> p s h v", s=6, h=4)
        dg = ar(0, 1024)
        W = ar(1024, 1024)
        v_ = ar(2048, 1024)
        vd = ar(3072, 1024)
        ctil = ar(4096, 1024)
        EB = ar(5120, 512)
        bn = ar(5632, 128)
        ytmp = ar(5760, 512)
        gtm = ar(6272, 128)
        cvout = ar(6400, 60).rearrange("p (i c) -> p i c", i=NXBC)
        cvst = ar(0, NXBC * P)
        aS = flat[:, HQ * T:HQ * T + 3072].rearrange("p (s n) -> p s n", s=6)
        hflat = hT[:, :, :].rearrange("p k t -> p (k t)")
        xbcT = hflat[:, 0:NXBC * T].rearrange("p (n t) -> p n t", n=NXBC)
        dtw = hflat[0:NH, 3200:3200 + 5 * T].rearrange("p (w t) -> p w t", w=5)
        bnat = hflat[:, 4800:4896].rearrange("p (q w h) -> p q w h", q=3, w=2)
        U32 = mybir.dt.uint32
        idx_ = sb("idx", [P, 40], U32)
        pos_scatter, pos_gather, tokid = idx_[:, 0:6], idx_[:, 6:12], idx_[:, 12:15]
        spill = idx_[:, 15:16].bitcast(I32)
        slot_tok = idx_[:, 16:32]
        gu = [slot[:, 2 * h:2 * h + 2, :].rearrange("p s n -> p (s n)").rearrange("p (k n) -> p k n", k=KD)
              for h in range(2)]
        dn = [flat[:, 4096 * h:4096 * h + 4096].rearrange("p (f n) -> p f n", f=2) for h in range(2)]
        hn = flat[:, 8192:8192 + 3 * D].rearrange("p (j d) -> p j d", j=3)
        xe = [flat[:, 8192 + 2048 * i:10240 + 2048 * i].rearrange("p (k t) -> p k t", k=KD) for i in range(2)]
        ys = flat[:, 12288:12288 + D]
        xg = [flat[:, 14336 + 2048 * i:16384 + 2048 * i] for i in range(2)]
        r1 = flat[:, 0:3 * D].rearrange("p (j d) -> p j d", j=3)
        r2 = flat[:, 3 * D:6 * D].rearrange("p (j d) -> p j d", j=3)
        ynat = r1
        tri = flat[:, 18432:18560]
        e64i = flat[:, 18560:18592].bitcast(I32)
        e64 = flat[:, 18592:18624]
        eTi = flat[:, 18624:18656].bitcast(I32)
        eT = tri[:, 0:32]
        wr = flat[:, 18684:18684 + KD * 36].rearrange("p (k e) -> p k e", k=KD)
        brow = flat[0:1, 19260:19260 + 36]
        rt = flat[:, 19296:19296 + 512]
        comb = flat[:, 19808:19808 + 96].rearrange("p (j e) -> p j e", j=3)
        A1, A2, Mk, rk, ge, am = (sq[:, 0, 96 * i:96 * i + 96].rearrange("p (j e) -> p j e", j=3) for i in range(6))
        sg = sq[:, 1, 0:256]
        asb = sq[:, 1, 256:512]
        aTT = sq[:, 0, 0:4 * CAP].rearrange("p (h f t) -> p h f t", h=2, f=2)
        acc = flat[:, 0:KD * T].rearrange("p (k t) -> p k t", k=KD)
        combB = flat[:, 5120:5120 + NE * T]
        combT = flat[0:NE, 15360:15360 + T]
        sgc = flat[:, 15680:15680 + 640]
        act_ = flat[:, 16320:16320 + 640]
        tok_dram = nc.dram_tensor("token_of_slot", [NE * CAP, 1], U32, kind="Internal").ap()
        h2_dram = nc.dram_tensor("moe_input", [T, D], F32, kind="Internal").ap()
        y_dram = nc.dram_tensor("moe_output", [NE * CAP, D], F32, kind="Internal").ap()
        comb_dram = nc.dram_tensor("comb_scratch", [NE, T], F32, kind="Internal").ap()

        b_ada, g_mix, g_ffn = parT[:, 0:96], parT[:, 96:112], parT[:, 112:128]
        p2 = parT[:, P:2 * P]
        conv_w = p2[:, 0:40].rearrange("p (j i) -> p j i", j=4)
        conv_b, ssd_g, lb_raw, hg_g, s5_d, s5_bg = (p2[:, x:y] for x, y in
                                                    ((40, 50), (50, 58), (58, 62), (62, 66), (66, 70), (70, 74)))
        g_fin, lam_re, lam_im = p2[:, 74:90], p2[:, 90:106], p2[:, 106:122]
        p3 = parT[:, 2 * P:3 * P]
        log_dt, ssd_D, x0re, x0im = p3[:, 0:16], p3[:, 32:40], p3[:, 64:80], p3[:, 80:96]

        def seg(i):
            return modT[:, KD * i:KD * (i + 1), :]

        def bc(ap, shape):
            return ap.broadcast_to(shape)

        def chunk_groups(n):
            if n < INP:
                return n + 1
            if n < ADA2:
                k = n - INP
                return 16 + 2 * (k + 1) - (1 if k >= 2 else 0)
            return 16 + 39 + (n - ADA2 + 1)

        def in_group(n):
            return 16 + 2 * n - (1 if n > 2 else 0)

        def ada_group(i):
            return i if i < 16 else 55 + i - 16

        class Steps:

            def __init__(self, eng, name):
                self.eng, self.name, self.n = eng, name, {}

            def __call__(self, ins, sem=None, wait=True):
                sem = sem or self.name
                ins.then_inc(S(sem), 1)
                self.n[sem] = self.n.get(sem, 0) + 1
                if wait:
                    self.eng.wait_ge(S(sem), self.n[sem])

        def states_stored(eng):
            eng.wait_ge(S("s5_stored"), 16 * 4)
            eng.wait_ge(S("hg_state_stored"), 16 * 2)
            eng.wait_ge(S("cv_saved"), 16 * 2)
            eng.wait_ge(S("ssd_stored"), 16 * 4)

        block = ctx.enter_context(nc.Block())

        @block.sync
        def _(sp):
            w_ada = a["w_ada"][0].rearrange("(k p) n -> p k n", p=P)
            w_in = a["w_in"][0].rearrange("(k p) n -> p k n", p=P)
            w_out = a["w_out"][0].rearrange("(k p) n -> p k n", p=P)

            def dst(s, w=CW):
                return slot[:, s, 0:KD * w].rearrange("p (k n) -> p k n", k=KD)

            for j in range(RING):
                sp.dma_start(dst(j), w_ada[:, :, j * CW:(j + 1) * CW]).then_inc(S(f"w_landed{j}"), 16)
            with sp.Fori(1, 4) as i:
                for j in range(RING):
                    sp.wait_ge(S("bulk_done"), 4 * i + (j - 3))
                    sp.dma_start(dst(j), w_ada[:, :, bass.ds(i * (4 * CW) + j * CW, CW)])\
                      .then_inc(S(f"w_landed{j}"), 16)
            for n in range(INP, PRE):
                s = n % RING
                if n < OUTP + RING:
                    sp.wait_ge(S("bulk_done"), chunk_groups(n - RING))
                else:
                    sp.wait_ge(S("out_done"), 2 * (n - RING - OUTP + 1))
                if n < ADA2:
                    col = IN_CHUNKS[n - INP][0]
                    w = 16 if col == COL_DT else CW
                    sp.dma_start(dst(s, w), w_in[:, :, col:col + w]).then_inc(S(f"w_landed{s}"), 16)
                elif n < OUTP:
                    i = n - ADA2 + 16
                    sp.dma_start(dst(s), w_ada[:, :, i * CW:(i + 1) * CW]).then_inc(S(f"w_landed{s}"), 16)
                else:
                    i = n - OUTP
                    sp.dma_start(dst(s), w_out[:, :, i * CW:(i + 1) * CW]).then_inc(S(f"w_landed{s}"), 16)
            gate = a["w_exp_gate"][0].rearrange("e (k p) n -> e p k n", p=P)
            up = a["w_exp_up"][0].rearrange("e (k p) n -> e p k n", p=P)
            down = a["w_exp_down"][0].rearrange("e (k p) n -> e p k n", p=P)

            def one(w, e):
                return w[e] if isinstance(e, int) else w[bass.ds(e, 1)].rearrange("e p k n -> (e p) k n")

            def load_gu(h, e):
                sp.dma_start(gu[h][:, :, 0:CW], one(gate, e)).then_inc(S(f"gu_landed{h}"), 16)
                sp.dma_start(gu[h][:, :, CW:2 * CW], one(up, e)).then_inc(S(f"gu_landed{h}"), 16)

            def load_dn(h, e):
                sp.dma_start(dn[h], one(down, e)).then_inc(S(f"dn_landed{h}"), 16)

            sp.wait_ge(S("out_done"), 12)
            load_gu(0, 0)
            sp.wait_ge(S("out_done"), 16)
            load_gu(1, 1)
            load_dn(0, 0)
            sp.wait_ge(S("gu_done"), 1)
            load_gu(0, 2)
            load_dn(1, 1)
            sp.wait_ge(S("gu_done"), 2)
            load_gu(1, 3)
            sp.wait_ge(S("down_done"), 1)
            load_dn(0, 2)
            with sp.Fori(2, NPAIR) as i:
                sp.wait_ge(S("gu_done"), 2 * i - 1)
                load_gu(0, 2 * i)
                sp.wait_ge(S("down_done"), 2 * i - 2)
                load_dn(1, 2 * i - 1)
                sp.wait_ge(S("gu_done"), 2 * i)
                load_gu(1, 2 * i + 1)
                sp.wait_ge(S("down_done"), 2 * i - 1)
                load_dn(0, 2 * i)
            sp.wait_ge(S("down_done"), NE - 2)
            load_dn(1, NE - 1)
            sp.wait_ge(S("routed"), 5)
            with sp.If(sp.value_load(spill[0:1, :], min_val=0, max_val=2 * T) > 0):
                with sp.Fori(1, NE + 1) as e:
                    sp.wait_ge(S("fb_free"), e)
                    for j, (w, d_) in enumerate(((gate, dst(0)), (up, dst(1)),
                                                 (down, slot[:, 2, :].rearrange("p (k n) -> p k n", k=2)))):
                        sp.dma_start(d_, w[bass.ds(e - 1, 1)].rearrange("e p k n -> (e p) k n"))\
                          .then_inc(S("fb_landed"), 16)
            sp.wait_ge(S("y_rows"), 12)
            sp.dma_start(o["y_prompt"][0].rearrange("(j p) d -> p j d", p=P), ynat[:, 0:2, :]).then_inc(S("stores"), 16)
            sp.dma_start(o["y_sample"][0], ynat[0:TS, 2, :]).then_inc(S("stores"), 16)
            sp.wait_ge(S("stores"), 16 * 2)
            states_stored(sp)

        @block.gpsimd
        def _(pool):
            pl = Steps(pool, "pool_step")
            g = nc.gpsimd
            pl(g.memset(ident[:, :], 0.0))
            pl(g.affine_select(out=ident[:, :], in_=ident[:, :], compare_op=ALU.not_equal, fill=1.0, base=0,
                               pattern=[[-1, P]], channel_multiplier=1))
            pl(g.memset(prow[:, 2, :], 0.0))
            pl(g.memset(ones[:, :], 1.0), "consts_a")
            pl(g.memset(rmask[:, :], 1.0))
            pl(g.memset(rmask[:, :].rearrange("p (c t) -> p c t", c=NCH)[:, :, 0:1], 0.0))
            pl(g.memset(lmask[:, :, :], 0.0))
            pl(g.memset(causal[:, :], 1.0))
            for half in range(2):
                lo = CH * half
                rows = slice(lo, lo + CH)
                pl(g.affine_select(out=lmask[rows, 0, :], in_=lmask[rows, 0, :], compare_op=ALU.not_equal,
                                   fill=1.0, base=0, pattern=[[-1, CH]], channel_multiplier=1))
                pl(g.affine_select(out=causal[rows, :], in_=causal[rows, :], compare_op=ALU.is_ge,
                                   fill=0.0, base=0, pattern=[[1, CH]], channel_multiplier=-1))
                for lv, m in enumerate(LEVELS[1:], 1):
                    sub = lmask[rows, lv, :].rearrange("p (b r) -> p b r", r=2 * m)[:, :, m:2 * m]
                    pl(g.memset(sub, 1.0))
                    pl(g.affine_select(out=sub, in_=sub, compare_op=ALU.is_ge, fill=0.0, base=0,
                                       pattern=[[-2 * m, CH // (2 * m)], [0, m]], channel_multiplier=1))
                    pl(g.affine_select(out=sub, in_=sub, compare_op=ALU.is_ge, fill=0.0, base=m - 1,
                                       pattern=[[2 * m, CH // (2 * m)], [0, m]], channel_multiplier=-1))
            par = small[:, 4:8]
            pl(g.memset(par, 1.0))
            pl(g.affine_select(out=par, in_=par, compare_op=ALU.is_ge, fill=0.0, base=-16,
                               pattern=[[-32, 4]], channel_multiplier=1))
            pl(g.affine_select(out=par, in_=par, compare_op=ALU.is_ge, fill=0.0, base=31,
                               pattern=[[32, 4]], channel_multiplier=-1))
            pl(g.tensor_tensor(small[:, 8:9], small[:, 4:5], small[:, 5:6], ALU.add))
            pl(g.tensor_tensor(small[:, 9:10], small[:, 6:7], small[:, 7:8], ALU.add))
            pl(g.tensor_tensor(small[:, 1:2], small[:, 8:9], small[:, 9:10], ALU.add))
            pl(g.tensor_scalar(small[:, 0:1], small[:, 1:2], -1.0, 1.0, ALU.mult, ALU.add))
            for j in range(8):
                pl(g.memset(small[:, 16 + j:17 + j], float(j - 99)))
            pl(g.memset(bdp, 0.0), "consts_b")
            pool.wait_ge(S("setup_act"), 5)
            pool.wait_ge(S("x_transposed"), 12)
            pool.dma_start(wglu, a["s5_w_glu"][0].rearrange("(k p) m -> p k m", p=P)).then_inc(S("wglu_loaded"), 16)
            for b in range(8):
                if b >= 2:
                    pool.wait_ge(S("s5_turned"), b - 1)
                pc, ps = (s5b[5 + 2 * (b % 2) + i].rearrange("p (i t) -> p i t", i=2) for i in range(2))
                tt, t2 = (sq[:, 0, 320 * i:320 * i + 256].rearrange("p (i t) -> p i t", i=2) for i in range(2))
                if b == 0:
                    pool.wait_ge(S("squares_used"), 8)
                cs = sm[:, 0, 2 * b:2 * b + 2].unsqueeze(2)
                sn = sm[:, 1, 2 * b:2 * b + 2].unsqueeze(2)
                pl(g.tensor_copy(pc[:, :, 0:1], cs))
                pl(g.tensor_copy(ps[:, :, 0:1], sn))
                m = 1
                while m < TP:
                    cm, sn_ = (bc(t[:, :, m - 1:m], [P, 2, m]) for t in (pc, ps))
                    pl(g.tensor_tensor(tt[:, :, 0:m], pc[:, :, 0:m], cm, ALU.mult))
                    pl(g.tensor_tensor(t2[:, :, 0:m], ps[:, :, 0:m], sn_, ALU.mult))
                    pl(g.tensor_tensor(pc[:, :, m:2 * m], tt[:, :, 0:m], t2[:, :, 0:m], ALU.subtract))
                    pl(g.tensor_tensor(tt[:, :, 0:m], pc[:, :, 0:m], sn_, ALU.mult))
                    pl(g.tensor_tensor(t2[:, :, 0:m], ps[:, :, 0:m], cm, ALU.mult))
                    pl(g.tensor_tensor(ps[:, :, m:2 * m], tt[:, :, 0:m], t2[:, :, 0:m], ALU.add))
                    m *= 2
                pl(g.tensor_copy(pc[:, :, TP:T], pc[:, :, 0:TS]))
                pl(g.tensor_copy(ps[:, :, TP:T], ps[:, :, 0:TS]), "s5_table")
            pool.wait_ge(S("s5_fin_rows"), 1)
            for w, name in enumerate(("s5re_p", "s5im_p", "s5re_s", "s5im_s")):
                pool.dma_start(o[name][0, 0].rearrange("(i g) q -> i (g q)", g=2), sq[0:16, 1, w * P:(w + 1) * P])\
                    .then_inc(S("s5_stored"), 16)
            pool.wait_ge(S("glu_used"), 4)
            pool.dma_start(hS[:, 4, :, :], a["state_hgrn"][0, 0].rearrange("h k v -> k h v"))\
                .then_inc(S("hg_in_loaded"), 16)
            pool.wait_ge(S("hg_S"), 2 * NCH)
            for sl, name in ((3, "hgrn_p"), (5, "hgrn_s")):
                pool.dma_start(o[name][0, 0].rearrange("h k v -> k h v"), hS[:, sl, :, :])\
                    .then_inc(S("hg_state_stored"), 16)
            pool.wait_ge(S("hg_normed"), 4)
            for g_ in range(2):
                pool.dma_start(aS[64 * g_:64 * g_ + 64, 4, :].rearrange("k (j v) -> k j v", j=8),
                               a["state_ssd"][0, 0, 8 * g_:8 * g_ + 8].rearrange("j k v -> k j v"))\
                    .then_inc(S("ssd_in_loaded"), 16)
            pool.wait_ge(S("cv_stored"), 1)
            for s_, name in ((0, "conv_p"), (3, "conv_s")):
                pool.dma_start(o[name][0, 0], cvst[s_:s_ + 3, :]).then_inc(S("cv_saved"), 16)
            pool.dma_start(wr[:, :, 0:4], a["w_router_group"][0].rearrange("(k p) e -> p k e", p=P))\
                .then_inc(S("router_loaded"), 16)
            pool.dma_start(wr[:, :, 4:36], a["w_router_expert"][0].rearrange("(k p) e -> p k e", p=P))\
                .then_inc(S("router_loaded"), 16)
            pool.dma_start(brow[:, 0:4], a["b_router_group"]).then_inc(S("router_loaded"), 16)
            pool.dma_start(brow[:, 4:36], a["b_router_expert"]).then_inc(S("router_loaded"), 16)
            pool.wait_ge(S("ssd_done"), NCH)
            pl(g.memset(tri, 1.0))
            pl(g.affine_select(out=tri, in_=tri, compare_op=ALU.is_ge, fill=0.0, base=-1, pattern=[[1, P]],
                               channel_multiplier=-1))
            pl(g.iota(e64i, pattern=[[CAP, NE]], base=0, channel_multiplier=0))
            pl(g.iota(eTi, pattern=[[1, NPAIR], [CAP * NPAIR, 2]], base=0, channel_multiplier=0))
            pl(g.iota(tokid, pattern=[[P, 3]], base=0, channel_multiplier=1))
            pl(g.memset(slot_tok, 0), "slot_consts")
            pool.dma_start(tok_dram.rearrange("(p i) u -> p (i u)", p=P), slot_tok).then_inc(S("tokens_moved"), 16)
            pool.wait_ge(S("tokens_moved"), 16)
            pool.wait_ge(S("ssd_S"), NCH)
            for sl, name in ((3, "ssd_p"), (5, "ssd_s")):
                for g_ in range(2):
                    pool.dma_start(o[name][0, 0, 8 * g_:8 * g_ + 8].rearrange("j k v -> k j v"),
                                   aS[64 * g_:64 * g_ + 64, sl, :].rearrange("k (j v) -> k j v", j=8))\
                        .then_inc(S("ssd_stored"), 16)
            pool.wait_ge(S("routed"), 3)
            for c in range(2):
                for j in range(3):
                    n = P if j < 2 else TS
                    pool.indirect_dma_start(tok_dram, bass.IndirectOffsetOnAxis(ap=pos_scatter[0:n, 3 * c + j:3 * c + j + 1], axis=0),
                                            tokid[0:n, j:j + 1], None, bounds_check=NE * CAP - 1, oob_is_err=False)\
                        .then_inc(S("tokens_moved"), 16)
            pool.wait_ge(S("tokens_moved"), 16 * 7)
            pool.dma_start(slot_tok, tok_dram.rearrange("(p i) u -> p (i u)", p=P)).then_inc(S("tokens_moved"), 16)
            pool.wait_ge(S("tokens_moved"), 16 * 8)
            pool.wait_ge(S("h2_stored"), 32)
            states_stored(pool)
            for i in range(NPAIR):
                if i >= 2:
                    pool.wait_ge(S("xe_turned"), 4 * (i - 1))
                pool.indirect_dma_start(xg[i % 2], None, h2_dram, bass.IndirectOffsetOnAxis(ap=slot_tok[:, i:i + 1], axis=0))\
                    .then_inc(S(f"xg_landed{i % 2}"), 16)
            pool.wait_ge(S("y_stored0"), 16 * NPAIR)
            pool.wait_ge(S("y_stored1"), 16 * NPAIR)
            pool.wait_ge(S("down_done"), NE)
            for j in range(3):
                n = P if j < 2 else TS
                for c, r_ in ((0, r1), (1, r2)):
                    pool.indirect_dma_start(r_[0:n, j, :], None, y_dram,
                                            bass.IndirectOffsetOnAxis(ap=pos_gather[0:n, 3 * c + j:3 * c + j + 1], axis=0))\
                        .then_inc(S(f"rows_landed{j}"), 16)

        @block.scalar
        def _(act):
            s = nc.scalar
            st = Steps(act, "act_step")

            def load(dst, src, sem):
                act.dma_start(dst, src).then_inc(S(sem), 16)

            load(crow[0:1, :], a["c_prompt"], "c_loaded")
            load(crow[1:2, :], a["c_sample"], "c_loaded")
            load(xnat[:, 0:2, :], a["x_prompt"][0].rearrange("(j p) d -> p j d", p=P), "x_loaded")
            load(xnat[0:TS, 2, :], a["x_sample"][0], "x_loaded")
            r = lambda ap: ap.rearrange("(n q) -> n q", q=P)
            load(prow[0:96, 0, :], r(a["b_ada"][0]), "par_loaded")
            load(prow[96:112, 0, :], r(a["g_mix"][0]), "par_loaded")
            load(prow[112:128, 0, :], r(a["g_ffn"][0]), "par_loaded")
            load(prow[0:40, 1, :], a["conv_w"][0].rearrange("j (n q) -> (j n) q", q=P), "par_loaded")
            for lo, hi, name in ((40, 50, "conv_b"), (50, 58, "ssd_norm_g"), (58, 62, "hgrn_lb_raw"),
                                 (66, 70, "s5_d"), (70, 74, "s5_b_glu")):
                load(prow[lo:hi, 1, :], r(a[name][0]), "par_loaded")
            load(prow[62:66, 1, :], a["hgrn_norm_g"][0], "par_loaded")
            load(prow[74:90, 1, :], r(a["g_final"]), "par_loaded")
            two = lambda ap: ap.rearrange("(i g) q -> i (g q)", g=2)
            load(prow[90:106, 1, :], two(a["s5_lam_re"][0]), "par_loaded")
            load(prow[106:122, 1, :], two(a["s5_lam_im"][0]), "par_loaded")
            load(ldrow[0:16, :], a["s5_log_dt"][0].rearrange("(i g) -> i g", g=2), "ld_loaded")
            load(ldrow[32:40, :], a["ssd_d"][0].rearrange("(i g) -> i g", g=2), "ld_loaded")
            act.wait_ge(S("consts_a"), 1)
            load(prow[64:80, 2, :], two(a["state_s5_re"][0, 0]), "par_loaded")
            load(prow[80:96, 2, :], two(a["state_s5_im"][0, 0]), "par_loaded")
            gp = lambda ap: ap.rearrange("(i g) q j -> (g q) i j", g=2)
            load(BR, gp(a["s5_b_re"][0]), "s5_loaded")
            load(BI, gp(a["s5_b_im"][0]), "s5_loaded")
            load(CR[:, 0], a["s5_c_re"][0].rearrange("(u g) j q -> (g j) u q", u=4), "s5_loaded")
            load(CR[:, 1], a["s5_c_im"][0].rearrange("(u g) j q -> (g j) u q", u=4), "s5_loaded")
            load(cvrow, a["state_conv"][0, 0], "cv_loaded")
            load(small[0:NH, 32:33], a["ssd_dt_bias"][0].rearrange("(h u) -> h u", u=1), "hd_loaded")
            load(small[0:NH, 33:34], a["ssd_a_log"][0].rearrange("(h u) -> h u", u=1), "hd_loaded")

            act.wait_ge(S("c_loaded"), 32)
            st(s.activation(crow, crow, ACT.Silu), "setup_act")
            act.wait_ge(S("setup_taken"), 3)
            st(s.activation(sm[:, 2, :], log_dt, ACT.Exp), "setup_act")
            act.wait_ge(S("setup_dve"), 1)
            st(s.activation(sm[:, 4, :], sm[:, 3, :], ACT.Exp), "setup_act")
            act.wait_ge(S("hd_loaded"), 32)
            st(s.activation(small[0:NH, 34:35], small[0:NH, 33:34], ACT.Exp), "setup_act")
            act.wait_ge(S("setup_dve"), 2)
            st(s.activation(sm[:, 0, :], sm[:, 7, :], ACT.Sin))
            st(s.activation(sm[:, 1, :], sm[:, 6, :], ACT.Sin), "setup_act")

            def squares(src, i, tag):
                if i >= 2:
                    act.wait_ge(S("squares_used"), NORM[tag] + i - 1)
                st(s.activation(sq[:, i % 2, :].rearrange("p (k t) -> p k t", k=2), src, ACT.Square), "squares")

            for i in range(8):
                act.wait_ge(S("x_transposed"), 12)
                squares(xT[:, 2 * i:2 * i + 2, :], i, "n1")
            act.wait_ge(S("mean_square"), 1)
            st(s.activation(rinv[:, :], rinv[:, :], ACT.Sqrt), "root")

            def ada_evac(i, j, grp, slow=True):
                n = 4 * i + j
                act.wait_ge(S("bulk_done"), grp + 1)
                if slow:
                    act.wait_ge(S("mod_turned"), n - 1)
                s.activation(modrow[:, j % 2, :], psum[0:2, (grp if isinstance(grp, int) else j) % 2, 0:CW],
                             ACT.Copy).then_inc(S("bulk_evac"), 1)

            for j in range(4):
                ada_evac(0, j, j, slow=j >= 2)
            with act.Fori(1, 4) as i:
                for j in range(4):
                    act.wait_ge(S("bulk_done"), 4 * i + (j + 1))
                    act.wait_ge(S("mod_turned"), 4 * i + (j - 1))
                    s.activation(modrow[:, j % 2, :], psum[0:2, j % 2, 0:CW], ACT.Copy).then_inc(S("bulk_evac"), 1)

            act.wait_ge(S("h_scaled"), 1)
            for k in range(KD):
                s.activation(hT[:, k, 0:TP], hT[:, k, 0:TP], ACT.Identity, bias=seg(0)[:, k, 0:1],
                             scale=ab1[:, k, 0:1]).then_inc(S("h_prompt"), 1)

            def evac_in(n):
                tile = IN_CHUNKS[n][1]
                for q in range(1 if tile is None else 2):
                    grp = in_group(n) + q
                    act.wait_ge(S("bulk_done"), grp + 1)
                    src = psum[:, grp % 2, 0:T]
                    if tile is None:
                        s.activation(dt_raw, psum[0:NH, grp % 2, 0:T], ACT.Copy).then_inc(S("bulk_evac"), 1)
                    elif tile >= 100:
                        i = tile - 100 + q
                        st(s.activation(xbcp[:, i, PADP:PADP + TP], src[:, 0:TP], ACT.Copy))
                        s.activation(xbcp[:, i, PADS:PADS + TS], src[:, TP:T], ACT.Copy).then_inc(S("bulk_evac"), 1)
                    else:
                        s.activation(proj[:, tile + q, :], src, ACT.Copy).then_inc(S("bulk_evac"), 1)

            def s5_in(b):
                act.wait_ge(S("s5_bu"), b + 1)
                if b:
                    act.wait_ge(S("s5_turned"), b)
                    act.wait_ge(S("s5_y"), b)
                for w in range(2):
                    src = psum[:, 4 + 2 * w:6 + 2 * w, 0:T]
                    st(s.activation(s5b[w].rearrange("p (i t) -> p i t", i=2), src, ACT.Copy), "s5_bu_sb")

            def s5_out(b):
                if b % 2:
                    act.wait_ge(S("s5_gelu_arg"), b // 2 + 1)
                    st(s.activation(sq[:, 1, 0:T], sq[:, 1, 0:T], ACT.Sigmoid), "s5_gelu_sig")

            def s5_glu():
                for m in range(4):
                    act.wait_ge(S("glu_mm"), m + 1)
                    if m >= 1:
                        act.wait_ge(S("glu_used"), m)
                    st(s.activation(rinv[:, :], psum[:, 4 + m, 0:T], ACT.Sigmoid, bias=s5_bg[:, m:m + 1]), "glu_sig")

            def hg_prep(hp):
                hf = flat[:, (HF + 2 * hp) * T:(HF + 2 * hp + 2) * T]
                if hp == 0:
                    act.wait_ge(S("glu_used"), 4)
                act.wait_ge(S("bulk_evac"), in_group(12))
                if hp:
                    act.wait_ge(S("hg_kd_turned"), 2 * hp)
                    act.wait_ge(S("hg_kdn"), hp)
                st(s.activation(hE, hf, ACT.Sigmoid))
                st(s.activation(hf, hf, ACT.Sigmoid, scale=-1.0), "hg_sig")
                act.wait_ge(S("hg_f"), hp + 1)
                st(s.activation(hE, hE, ACT.Ln), "hg_ln")

            def hg_level(hp, lv):
                if lv:
                    act.wait_ge(S("hg_expo"), 6 * hp + lv)
                    st(s.activation(hE, hE, ACT.Exp), "hg_exp")

            def hg_kd(hp):
                act.wait_ge(S("hg_expo2"), 2 * hp + 1)
                st(s.activation(hE, hb, ACT.Exp), "hg_exp2")
                act.wait_ge(S("hg_expo2"), 2 * hp + 2)
                st(s.activation(hE, hE, ACT.Exp), "hg_exp2")

            def hg_out(hp):
                gate = flat[:, (HG + 2 * hp) * T:(HG + 2 * hp + 2) * T]
                st(s.activation(gate, gate, ACT.Silu), "hg_gate")
                for h in range(2):
                    act.wait_ge(S("hg_o"), 2 * hp + 2)
                    st(s.activation(sq[:, 0, h * T:h * T + T], psum[:, 4 + h, 0:T], ACT.Square), "hg_sq")
                for h in range(2):
                    act.wait_ge(S("hg_var"), 2 * hp + h + 1)
                    st(s.activation(rinv[:, :], rinv[:, :], ACT.Sqrt), "hg_root")

            def ssd_conv():
                act.wait_ge(S("dt_arg"), 1)
                st(s.activation(dtw[:, 1, :], dtw[:, 0, :], ACT.Exp), "dt_func")
                act.wait_ge(S("dt_arg"), 2)
                st(s.activation(dtw[:, 3, :], dtw[:, 2, :], ACT.Ln), "dt_func")
                for i in range(NXBC):
                    act.wait_ge(S("conv_out"), i + 1)
                    st(s.activation(xbcT[:, i, :], xbcT[:, i, :], ACT.Silu), "conv_silu")
                st(s.activation(flat[:, 0:8 * T], flat[:, 0:8 * T], ACT.Silu), "z_silu")

            def ssd_decay(c):
                half = slice(CH * (c % 2), CH * (c % 2) + CH)
                act.wait_ge(S("ssd_diff"), 2 * c + 1)
                st(s.activation(small[half, 64:80], small[half, 64:80], ACT.Exp), "ssd_exp")
                for g in range(2):
                    rows = slice(64 * g, 64 * g + 64)
                    st(s.activation(EB[rows, :], psum[rows, 4 + g, :], ACT.Exp), "ssd_EB")
                act.wait_ge(S("ssd_diff"), 2 * c + 2)
                st(s.activation(W[half, :], W[half, :], ACT.Exp), "ssd_exp")

            def ssd_norm():
                act.wait_ge(S("ssd_done"), NCH)
                act.wait_ge(S("s5_stored"), 64)
                for i in range(4):
                    squares(proj[:, 2 * i:2 * i + 2, :], i, "ssd")
                act.wait_ge(S("mean_square"), 2)
                st(s.activation(rinv[:, :], rinv[:, :], ACT.Sqrt), "root")

            for item in PLAN:
                kind = item[0]
                if kind == "in":
                    evac_in(item[1])
                elif kind == "ada":
                    ada_evac(0, item[1], ada_group(item[1]))
                elif kind == "s5_in":
                    s5_in(item[1])
                elif kind == "s5_out":
                    s5_out(item[1])
                elif kind == "s5_glu":
                    s5_glu()
                elif kind == "hg_prep":
                    hg_prep(item[1])
                elif kind == "hg_level":
                    hg_level(item[1], item[2])
                elif kind == "hg_kd":
                    hg_kd(item[1])
                elif kind == "hg_out":
                    hg_out(item[1])
                elif kind == "ssd_conv":
                    ssd_conv()
                elif kind == "ssd_decay":
                    ssd_decay(item[1])
                elif kind == "ssd_norm":
                    ssd_norm()

            for i in range(8):
                act.wait_ge(S("x_mixed"), 4 * (i + 1))
                squares(xT[:, 2 * i:2 * i + 2, :], i, "n2")
            act.wait_ge(S("mean_square"), 3)
            st(s.activation(rinv[:, :], rinv[:, :], ACT.Sqrt), "root")
            act.wait_ge(S("h_scaled"), 2)
            for k in range(KD):
                s.activation(hT[:, k, 0:TP], hT[:, k, 0:TP], ACT.Identity, bias=seg(3)[:, k, 0:1],
                             scale=ab1[:, k, 0:1]).then_inc(S("h_prompt"), 1)
            act.wait_ge(S("rt_expo"), 1)
            st(s.activation(rt[:, 16:28], rt[:, 16:28], ACT.Exp))
            st(s.activation(rt[:, 240:243], rt[:, 240:243], ACT.Exp), "rt_exp")
            for g_ in range(12):
                j, kg = g_ // 4, g_ % 4
                n = P if j < 2 else TS
                act.wait_ge(S("hn_turned"), g_ + 1)
                s.activation(hn[0:n, j, 512 * kg:512 * kg + 512], bank(4 + g_ % 4, 512, n), ACT.Copy)\
                 .then_inc(S("hn_rows"), 1)
            act.wait_ge(S("hn_rows"), 12)
            act.dma_start(h2_dram[0:TP].rearrange("(j p) d -> p j d", p=P), hn[:, 0:2, :]).then_inc(S("h2_stored"), 16)
            act.dma_start(h2_dram[TP:T], hn[0:TS, 2, :]).then_inc(S("h2_stored"), 16)

            def silu_gate(h, e):
                rows_ = slice(CAP * h, CAP * h + CAP)
                act.wait_ge(S("gu_done"), e + 1)
                if not (isinstance(e, int) and e < 2):
                    act.wait_ge(S("act_ready"), e - 1)
                s.activation(sg[rows_, :], psum[rows_, 0, 0:CW], ACT.Silu).then_inc(S("gate_silu"), 1)

            def store_y(h, e):
                act.wait_ge(S("y_rows_sb"), e + 1)
                where = y_dram[e * CAP:(e + 1) * CAP] if isinstance(e, int) else y_dram[bass.ds(e * CAP, CAP)]
                act.dma_start(where, ys[CAP * h:CAP * h + CAP, :]).then_inc(S(f"y_stored{h}"), 16)

            silu_gate(0, 0)
            silu_gate(1, 1)
            store_y(0, 0)
            with act.Fori(1, NPAIR) as i:
                silu_gate(0, 2 * i)
                store_y(1, 2 * i - 1)
                silu_gate(1, 2 * i + 1)
                store_y(0, 2 * i)
            store_y(1, NE - 1)
            act.wait_ge(S("routed"), 5)
            with act.If(act.value_load(spill[0:1, :], min_val=0, max_val=2 * T) > 0):
                act.wait_ge(S("fb_dve"), 2)
                act.dma_start(comb_dram, combT).then_inc(S("fb_rows"), 16)
                act.wait_ge(S("fb_rows"), 16)
                act.dma_start(combB, comb_dram.rearrange("e t -> (e t)").unsqueeze(0).broadcast_to([P, NE * T]))\
                   .then_inc(S("fb_rows"), 16)
                with act.Fori(1, NE + 1) as e:
                    act.wait_ge(S("fb_hidden"), e)
                    s.activation(sgc.rearrange("p (f t) -> p f t", f=2), psum[:, 0:2, 0:T], ACT.Silu)\
                     .then_inc(S("fb_silu"), 1)
            for i in range(8):
                act.wait_ge(S("x_final"), 1)
                squares(xT[:, 2 * i:2 * i + 2, :], i, "n3")
            act.wait_ge(S("mean_square"), 4)
            st(s.activation(rinv[:, :], rinv[:, :], ACT.Sqrt), "root")

        @block.tensor
        def _(pe):
            mm, tr = nc.tensor.matmul, nc.tensor.transpose
            pe.wait_ge(S("consts_a"), 1)
            pe.wait_ge(S("x_loaded"), 32)
            for g in range(12):
                j, kg = g // 4, g % 4
                n = P if j < 2 else TS
                if g >= 4:
                    pe.wait_ge(S("x_transposed"), g - 3)
                for q in range(4):
                    k = 4 * kg + q
                    last = tr(bank(4 + g % 4, n, lo=q * n), xnat[0:n, j, k * P:(k + 1) * P], ident[0:n, 0:n])
                last.then_inc(S("x_turned"), 1)
            pe.wait_ge(S("setup_act"), 1)
            for k in range(KD):
                last = tr(bank(3, 2, lo=384 + 2 * k), crow[:, k * P:(k + 1) * P], ident[0:2, 0:2])
            last.then_inc(S("setup_turned"), 1)
            pe.wait_ge(S("setup_taken"), 1)
            pe.wait_ge(S("setup_taken"), 2)
            pe.wait_ge(S("par_loaded"), 16 * 15)
            tr(bank(3, P, lo=0), prow[:, 0, :], ident[:, :])
            tr(bank(3, 122, lo=P), prow[0:122, 1, :], ident[0:122, 0:122])
            tr(bank(3, 96, lo=2 * P), prow[0:96, 2, :], ident[0:96, 0:96]).then_inc(S("setup_turned"), 1)
            pe.wait_ge(S("cv_loaded"), 16)
            pe.wait_ge(S("x_transposed"), 12)
            for i in range(NXBC):
                last = tr(bank(2, 3, lo=4 * i), cvrow[:, i * P:(i + 1) * P], ident[0:3, 0:3])
            last.then_inc(S("setup_turned"), 1)
            pe.wait_ge(S("setup_taken"), 3)
            pe.wait_ge(S("setup_taken"), 1)

            def sum_squares(b, count, tag):
                for i in range(count):
                    pe.wait_ge(S("squares"), NORM[tag] + i + 1)
                    for q in range(2):
                        last = mm(bank(b, T), ones[:, :], sq[:, i % 2, q * T:q * T + T],
                                  start=(i == 0 and q == 0), stop=(i == count - 1 and q == 1))
                    last.then_inc(S("squares_used"), 1)

            sum_squares(3, 8, "n1")
            pe.wait_ge(S("s5_mats"), 1)
            for w in range(2):
                for u in range(4):
                    tr(bank(4 + w, P, lo=u * P),
                       bdp[:, w, 4 * u:4 * u + 4].rearrange("p i g j -> p (i g j)"), ident[:, :])
                    last = tr(bank(6 + w, P, lo=u * P), cpad[:, w, u].rearrange("p g q -> p (g q)"), ident[:, :])
            last.then_inc(S("setup_turned"), 1)

            def ada_mm(s_, first, wait_evac):
                w = slot[:, s_, :].rearrange("p (k n) -> p k n", k=KD)
                for k in range(KD):
                    last = mm(psum[0:2, first, 0:CW], cT[:, k, :], w[:, k, :], start=(k == 0), stop=(k == KD - 1))
                last.then_inc(S("bulk_done"), 1)

            def ada_turn(j):
                for q in range(2):
                    last = mm(bank(2, 2, lo=64 + 4 * (j % 2) + 2 * q), modrow[:, j % 2, q * P:(q + 1) * P],
                              ident[0:2, 0:2], start=True, stop=True)
                last.then_inc(S("mod_turned"), 1)

            pe.wait_ge(S("setup_taken"), 4)
            for j in range(4):
                pe.wait_ge(S(f"w_landed{j}"), 16)
                if j >= 2:
                    pe.wait_ge(S("bulk_evac"), j - 1)
                ada_mm(j, j % 2, False)
                if j >= 1:
                    pe.wait_ge(S("bulk_evac"), j)
                    if j >= 2:
                        pe.wait_ge(S("mod_ready"), j - 1)
                    ada_turn(j - 1)
            with pe.Fori(1, 4) as i:
                for j in range(4):
                    pe.wait_ge(S(f"w_landed{j}"), 16 * i + 16)
                    pe.wait_ge(S("bulk_evac"), 4 * i + (j - 1))
                    ada_mm(j, j % 2, False)
                    pe.wait_ge(S("bulk_evac"), 4 * i + j)
                    pe.wait_ge(S("mod_ready"), 4 * i + (j - 1))
                    ada_turn(j + 3)
            pe.wait_ge(S("bulk_evac"), 16)
            pe.wait_ge(S("mod_ready"), 15)
            ada_turn(15)

            def in_mm(n):
                tile = IN_CHUNKS[n][1]
                r = INP + n
                pe.wait_ge(S(f"w_landed{r % RING}"), 16 * (r // RING + 1))
                wd = NH if tile is None else P
                w = slot[:, r % RING, 0:KD * (NH if tile is None else CW)].rearrange("p (k n) -> p k n", k=KD)
                for q in range(1 if tile is None else 2):
                    grp = in_group(n) + q
                    pe.wait_ge(S("bulk_evac"), grp - 1)
                    for k in range(KD):
                        last = mm(psum[0:wd, grp % 2, 0:T], w[:, k, q * P:q * P + wd], hT[:, k, :],
                                  start=(k == 0), stop=(k == KD - 1))
                    last.then_inc(S("bulk_done"), 1)

            def ada(i):
                r = ADA2 + i - 16
                grp = ada_group(i)
                pe.wait_ge(S(f"w_landed{r % RING}"), 16 * (r // RING + 1))
                pe.wait_ge(S("bulk_evac"), grp - 1)
                ada_mm(r % RING, grp % 2, False)
                if i > 16:
                    pe.wait_ge(S("bulk_evac"), grp)
                    pe.wait_ge(S("mod_ready"), i - 1)
                    ada_turn(i - 1)

            def s5_in(b):
                if b == 0:
                    pe.wait_ge(S("bulk_evac"), in_group(4))
                    pe.wait_ge(S("s5_mats_ready"), 1)
                if b:
                    pe.wait_ge(S("s5_bu_sb"), 2 * b)
                u = b // 2
                for i in range(2):
                    rows = slice(32 * (2 * (b % 2) + i), 32 * (2 * (b % 2) + i) + 32)
                    for w in range(2):
                        last = mm(psum[:, 4 + 2 * w + i, 0:T], BDT[rows, w, u, :], proj[rows, U + u, :],
                                  start=True, stop=True)
                last.then_inc(S("s5_bu"), 1)

            def s5_out(b):
                pe.wait_ge(S("s5_turned"), b + 1)
                if b % 2 == 0 and b:
                    pe.wait_ge(S("s5_g"), b // 2)
                u = b // 2
                for i in range(2):
                    c0 = 32 * (2 * (b % 2) + i)
                    for w in range(2):
                        last = mm(psum[c0:c0 + 32, 3, 0:T], CT[:, w, u, c0:c0 + 32],
                                  s5b[2 + w][:, i * T:i * T + T], start=(w == 0), stop=(w == 1))
                last.then_inc(S("s5_y"), 1)

            def s5_glu():
                pe.wait_ge(S("s5_g"), 4)
                pe.wait_ge(S("wglu_loaded"), 16)
                pe.wait_ge(S("s5_bu_sb"), 16)
                for m in range(4):
                    for k in range(4):
                        last = mm(bank(4 + m, T), wglu[:, k, m * P:(m + 1) * P], proj[:, U + k, :],
                                  start=(k == 0), stop=(k == 3))
                    last.then_inc(S("glu_mm"), 1)
                for w in range(4):
                    last = tr(bank(3, P, 16, lo=w * P), s5fin[:, w, :], ident[:, :])
                last.then_inc(S("s5_fin_turned"), 1)

            def hg_prep(hp):
                if hp == 0:
                    pe.wait_ge(S("bulk_evac"), in_group(12))
                    pe.wait_ge(S("glu_used"), 4)
                else:
                    pe.wait_ge(S("hg_normed"), 2)
                for h in range(2):
                    src = proj[:, HI + 2 * hp + h, :]
                    for q in range(3):
                        n = P if q < 2 else TS
                        last = tr(bank(6 + h, P, n, lo=q * P), src[:, q * P:q * P + n], ident[:, :])
                last.then_inc(S("hg_v"), 1)

            def hg_level(hp, lv):
                it = 7 * hp + lv
                if lv == 0:
                    pe.wait_ge(S("hg_k"), hp + 1)
                    q_, k_ = (flat[:, (x + 2 * hp) * T:(x + 2 * hp + 2) * T] for x in (HQ, HF))
                else:
                    pe.wait_ge(S("hg_qk"), 6 * hp + lv)
                    q_, k_ = hq_, hk_
                if it >= 2:
                    pe.wait_ge(S("hg_sc_used"), it - 1)
                for h in range(2):
                    for c in range(6):
                        cc = min(c, NCH - 1)
                        col = h * T + cc * CH
                        last = mm(psum[CH * (c % 2):CH * (c % 2) + CH, 4 + it % 2,
                                       (h * 3 + c // 2) * CH:(h * 3 + c // 2) * CH + CH],
                                  k_[:, col:col + CH], q_[:, col:col + CH], start=True, stop=True)
                last.then_inc(S("hg_sc"), 1)

            def hg_kd(hp):
                pe.wait_ge(S("hg_kd"), hp + 1)
                pe.wait_ge(S("hg_vn"), hp + 1)
                for h in range(2):
                    for q in range(3):
                        n = P if q < 2 else TS
                        last = tr(bank(6 + h, P, n, lo=q * P), hE[:, h * T + q * P:h * T + q * P + n], ident[:, :])
                    last.then_inc(S("hg_kd_turned"), 1)

            def hg_state(hp):
                pe.wait_ge(S("hg_kdn"), hp + 1)
                for c in range(NCH):
                    half = slice(CH * (c % 2), CH * (c % 2) + CH)
                    if c >= 2:
                        pe.wait_ge(S("hg_S"), NCH * hp + c - 1)
                    for h in range(2):
                        last = mm(bank(6 + c % 2, P, lo=h * P), kdn[half, h, c // 2, :], vn[half, h, c // 2, :],
                                  start=True, stop=True)
                    last.then_inc(S("hg_dS"), 1)

            def hg_out(hp):
                pe.wait_ge(S("hg_S"), NCH * (hp + 1))
                pe.wait_ge(S("hg_sc_used"), 7 * (hp + 1))
                for parity in range(2):
                    for h in range(2):
                        for c in range(parity, NCH, 2):
                            half = slice(CH * parity, CH * parity + CH)
                            out = bank(4 + h, CH, lo=c * CH)
                            pair = (h * 3 + c // 2) * CH
                            last = mm(out, vn[half, h, c // 2, :], hAT[half, pair:pair + CH], start=True, stop=(c == 0))
                            if c:
                                sl = c - 1 if c < 4 else 4
                                last = mm(out, hS[:, sl, 2 * hp + h, :], hq_[:, h * T + c * CH:h * T + c * CH + CH],
                                          start=False, stop=True)
                    last.then_inc(S("hg_o"), 1)
                    pe.wait_ge(S("hg_o"), 2 * hp + parity + 1)
                for h in range(2):
                    pe.wait_ge(S("hg_sq"), 2 * hp + h + 1)
                    mm(bank(6 + h, T), ones[:, :], sq[:, 0, h * T:h * T + T], start=True, stop=True)\
                        .then_inc(S("hg_ss"), 1)

            def ssd_gamma():
                pe.wait_ge(S("dt_done"), 1)
                pe.wait_ge(S("cv_new"), 1)
                pe.wait_ge(S("hg_normed"), 4)
                for q in range(3):
                    n = P if q < 2 else TS
                    for w in range(2):
                        last = tr(bank(6, NH, n, lo=(2 * q + w) * NH), dtw[:, w, q * P:q * P + n],
                                  ident[0:NH, 0:NH])
                last.then_inc(S("bdt_turned"), 1)
                for i in range(NXBC):
                    last = tr(psum[0:6, 3 + i // 4, (i % 4) * P:(i % 4) * P + P], cvout[:, i, :], ident[:, :])
                last.then_inc(S("cv_new_turned"), 1)

            def ssd_nat(q):
                n = P if q < 2 else TS
                pe.wait_ge(S("conv_silu"), NXBC)
                if q == 0:
                    pe.wait_ge(S("cv_stored"), 1)
                    pe.wait_ge(S("bdt_taken"), 1)
                else:
                    pe.wait_ge(S("ssd_done"), 2 * q)
                cols = slice(q * P, q * P + n)
                for i in range(8):
                    tr(bank(4 + i // 4, P, n, lo=(i % 4) * P), xbcT[:, i, cols], ident[:, :])
                tr(bank(6, P, n, lo=0), xbcT[:, 8, cols], ident[:, :])
                for g in range(2):
                    rows = slice(64 * g, 64 * g + 64)
                    for c in range(2 * q, min(2 * q + 2, NCH)):
                        c2 = c % 2
                        last = mm(psum[CH * c2:CH * c2 + CH, 6 + g, P:P + CH],
                                  xbcT[rows, 8, c * CH:c * CH + CH], xbcT[rows, 9, c * CH:c * CH + CH],
                                  start=True, stop=True)
                last.then_inc(S("ssd_nat"), 1)

            def ssd_decay(c):
                pe.wait_ge(S("ssd_diag"), c + 1)
                for g in range(2):
                    last = mm(bank(4 + g), ones[0:NH, :], dg[0:NH, 512 * g:512 * g + 512], start=True, stop=True)
                last.then_inc(S("ssd_b"), 1)

            def ssd_y(c):
                half = slice(CH * (c % 2), CH * (c % 2) + CH)
                pe.wait_ge(S("ssd_vd"), c + 1)
                for g in range(2):
                    rows = slice(64 * g, 64 * g + 64)
                    last = mm(psum[rows, 7, :], bn[half, 64 * g:64 * g + 64], vd[half, 512 * g:512 * g + 512],
                              start=True, stop=True)
                last.then_inc(S("ssd_dS"), 1)
                pe.wait_ge(S("ssd_W"), c + 1)
                if c == 4:
                    pe.wait_ge(S("ssd_in_loaded"), 32)
                def head_out(h):
                    return psum[64 * (h % 2):64 * (h % 2) + 64, 3, (h // 2) * CH:(h // 2) * CH + CH]

                for h in range(NH):
                    last = mm(head_out(h), v_[half, h * 64:h * 64 + 64], W[half, h * CH:h * CH + CH],
                              start=(h < 2), stop=(c == 0 and h >= NH - 2), skip_group_check=True)
                if c:
                    sl = c - 1 if c < 4 else 4
                    for h in range(NH):
                        last = mm(head_out(h), aS[:, sl, (h % 8) * 64:(h % 8) * 64 + 64], ctil[:, h * CH:h * CH + CH],
                                  start=False, stop=(h >= NH - 2), skip_group_check=True)
                last.then_inc(S("ssd_y"), 1)

            for item in PLAN:
                kind = item[0]
                if kind == "in":
                    if item[1] == 0:
                        pe.wait_ge(S("h_prompt"), KD)
                        pe.wait_ge(S("h_sample"), KD)
                    in_mm(item[1])
                elif kind == "ada":
                    ada(item[1])
                elif kind == "s5_in":
                    s5_in(item[1])
                elif kind == "s5_out":
                    s5_out(item[1])
                elif kind == "s5_glu":
                    s5_glu()
                elif kind == "hg_prep":
                    hg_prep(item[1])
                elif kind == "hg_level":
                    hg_level(item[1], item[2])
                elif kind == "hg_kd":
                    hg_kd(item[1])
                elif kind == "hg_state":
                    hg_state(item[1])
                elif kind == "hg_out":
                    hg_out(item[1])
                elif kind == "ssd_gamma":
                    ssd_gamma()
                elif kind == "ssd_nat":
                    ssd_nat(item[1])
                elif kind == "ssd_decay":
                    ssd_decay(item[1])
                elif kind == "ssd_y":
                    ssd_y(item[1])
                elif kind == "ssd_norm":
                    sum_squares(3, 4, "ssd")
            pe.wait_ge(S("bulk_evac"), 87)
            pe.wait_ge(S("mod_ready"), 47)
            ada_turn(47)

            pe.wait_ge(S("merged"), 1)
            pe.wait_ge(S("hg_normed"), 4)
            src = [proj[:, Z + i, :] for i in range(8)] + [proj[:, HG + i, :] for i in range(4)] \
                + [proj[:, U + i, :] for i in range(4)]
            for n in range(8):
                r = OUTP + n
                pe.wait_ge(S(f"w_landed{r % RING}"), 16 * (r // RING + 1))
                w = slot[:, r % RING, :].rearrange("p (k n) -> p k n", k=KD)
                for q in range(2):
                    m = 2 * n + q
                    if m >= 4:
                        pe.wait_ge(S("x_mixed"), 2 * (m - 3))
                    for k in range(KD):
                        last = mm(bank(4 + m % 4, T), w[:, k, q * P:(q + 1) * P], src[k], start=(k == 0), stop=(k == KD - 1))
                    last.then_inc(S("out_done"), 1)
            sum_squares(3, 8, "n2")
            pe.wait_ge(S("h_prompt"), 2 * KD)
            pe.wait_ge(S("h_sample"), 2 * KD)
            pe.wait_ge(S("router_loaded"), 64)
            for j in range(3):
                n = P if j < 2 else TS
                for k in range(KD):
                    mm(bank(2, 36, n, lo=36 * j), hT[:, k, j * P:j * P + n], wr[:, k, :], start=(k == 0), stop=False)
                last = mm(bank(2, 36, n, lo=36 * j), ones[0:1, 0:n], brow, start=False, stop=True)
            last.then_inc(S("logits"), 1)
            for g in range(12):
                j, kg = g // 4, g % 4
                n = P if j < 2 else TS
                pe.wait_ge(S("x_mixed"), 32)
                if g >= 4:
                    pe.wait_ge(S("hn_rows"), g - 3)
                for q in range(4):
                    last = tr(bank(4 + g % 4, P, n, lo=q * P), hT[:, 4 * kg + q, j * P:j * P + n], ident[:, :])
                last.then_inc(S("hn_turned"), 1)
            pe.wait_ge(S("routed"), 1)
            pe.wait_ge(S("slot_consts"), 1)
            for j in range(3):
                n = P if j < 2 else TS
                for jj in range(j + 1):
                    last = mm(bank(3, NE, n, lo=NE * j), tri[:, 0:n] if jj == j else ones[:, 0:n], Mk[:, jj, :],
                              start=(jj == 0), stop=(jj == j))
            last.then_inc(S("rank"), 1)
            pe.wait_ge(S("routed"), 2)
            mm(bank(3, 3), ones[:, :], rt[:, 496:499], start=True, stop=True).then_inc(S("rank"), 1)

            def turn_x(i, g_, par):
                pe.wait_ge(S(f"xg_landed{par}"), 8 * (i - par) + 16)
                if not (isinstance(i, int) and 4 * i + g_ < 2):
                    pe.wait_ge(S("xe_ready"), 4 * i + (g_ - 1))
                for q in range(4):
                    last = tr(bank(6 + g_ % 2, P, lo=q * P), xg[par][:, (4 * g_ + q) * P:(4 * g_ + q + 1) * P], ident[:, :])
                last.then_inc(S("xe_turned"), 1)

            def act_turn(h, e):
                rows_ = slice(CAP * h, CAP * h + CAP)
                pe.wait_ge(S("act_ready"), e + 1)
                if not (isinstance(e, int) and e < 1):
                    pe.wait_ge(S("actT_ready"), e)
                for f in range(2):
                    last = mm(bank(5, CAP, lo=f * CAP), asb[rows_, f * P:(f + 1) * P], ident[rows_, rows_],
                              start=True, stop=True)
                last.then_inc(S("act_turned"), 1)

            def expert_gu(i, h, par, prev):
                e = 2 * i + h
                rows_ = slice(CAP * h, CAP * h + CAP)
                pe.wait_ge(S(f"gu_landed{h}"), 32 * i + 32)
                pe.wait_ge(S("xe_ready"), 4 * i + 4)
                if not (isinstance(e, int) and e < 2):
                    pe.wait_ge(S("act_ready"), e - 1)
                for k in range(KD):
                    last = mm(psum[rows_, 0, :], xe[par][:, k, CAP * h:CAP * h + CAP], gu[h][:, k, :],
                              start=(k == 0), stop=(k == KD - 1))
                    if k == 11 and prev:
                        act_turn(1 - h, e - 1)
                last.then_inc(S("gu_done"), 1)

            def expert_down(i, h):
                e = 2 * i + h
                rows_ = slice(CAP * h, CAP * h + CAP)
                pe.wait_ge(S(f"dn_landed{h}"), 16 * i + 16)
                pe.wait_ge(S("actT_ready"), e + 1)
                if not (isinstance(e, int) and e < 2):
                    pe.wait_ge(S("y_rows_sb"), e - 1)
                for n in range(4):
                    for f in range(2):
                        last = mm(psum[rows_, 1 + n, :], aTT[:, h, f, :], dn[h][:, f, 512 * n:512 * n + 512],
                                  start=(f == 0), stop=(f == 1))
                last.then_inc(S("down_done"), 1)

            def pair(i, par, more):
                expert_gu(i, 0, par, not (isinstance(i, int) and i == 0))
                if not (isinstance(i, int) and i == 0):
                    expert_down(i - 1, 1)
                if more:
                    turn_x(i + 1, 0, 1 - par)
                    turn_x(i + 1, 1, 1 - par)
                expert_gu(i, 1, par, True)
                expert_down(i, 0)
                if more:
                    turn_x(i + 1, 2, 1 - par)
                    turn_x(i + 1, 3, 1 - par)

            pe.wait_ge(S("hn_rows"), 12)
            pe.wait_ge(S("routed"), 5)
            for g_ in range(4):
                turn_x(0, g_, 0)
            pair(0, 0, True)
            pair(1, 1, True)
            with pe.Fori(1, QUADS - 1) as q:
                pair(2 * q, 0, True)
                pair(2 * q + 1, 1, True)
            pair(NPAIR - 2, 0, True)
            pair(NPAIR - 1, 1, False)
            act_turn(1, NE - 1)
            expert_down(NPAIR - 1, 1)
            for g in range(12):
                j, kg = g // 4, g % 4
                n = P if j < 2 else TS
                if kg == 0:
                    pe.wait_ge(S("rows_summed"), j + 1)
                    pe.wait_ge(S("xe_ready"), 4 * NPAIR)
                if g >= 2:
                    pe.wait_ge(S("m_added"), g - 1)
                for q in range(4):
                    last = tr(bank(6 + g % 2, n, lo=q * n), r1[0:n, j, (4 * kg + q) * P:(4 * kg + q + 1) * P], ident[0:n, 0:n])
                last.then_inc(S("m_turned"), 1)
            with pe.If(pe.value_load(spill[0:1, :], min_val=0, max_val=2 * T) > 0):
                pe.wait_ge(S("m_added"), 12)
                for j in range(3):
                    n = P if j < 2 else TS
                    last = tr(psum[0:NE, 3, j * P:j * P + n], comb[0:n, j, :], ident[0:n, 0:n])
                last.then_inc(S("fb_comb_turned"), 1)
                pe.wait_ge(S("fb_dve"), 2)
                pe.sem_inc(S("fb_free"), 1)
                w0, w1 = (slot[:, j, :].rearrange("p (k n) -> p k n", k=KD) for j in range(2))
                w2 = slot[:, 2, :].rearrange("p (k n) -> p k n", k=2)
                with pe.Fori(1, NE + 1) as e:
                    pe.wait_ge(S("fb_landed"), 48 * e)
                    pe.wait_ge(S("fb_added"), 4 * e - 3)
                    for b, w in ((0, w0), (2, w1)):
                        for f in range(2):
                            for k in range(KD):
                                last = mm(bank(b + f, T), w[:, k, f * P:(f + 1) * P], hT[:, k, :],
                                          start=(k == 0), stop=(k == KD - 1))
                    last.then_inc(S("fb_hidden"), 1)
                    pe.wait_ge(S("fb_act"), e)
                    for g in range(4):
                        pe.wait_ge(S("fb_added"), 4 * e + (g - 3))
                        for m in range(4 * g, 4 * g + 4):
                            for f in range(2):
                                last = mm(bank(4 + m % 4, T), w2[:, f, m * P:(m + 1) * P], act_[:, f * T:f * T + T],
                                          start=(f == 0), stop=(f == 1))
                        last.then_inc(S("fb_down"), 1)
                    pe.wait_ge(S("fb_down"), 4 * e)
                    pe.sem_inc(S("fb_free"), 1)
            sum_squares(3, 8, "n3")
            pe.wait_ge(S("y_ready"), 1)
            for g in range(12):
                j, kg = g // 4, g % 4
                n = P if j < 2 else TS
                if g >= 4:
                    pe.wait_ge(S("y_rows"), g - 3)
                for q in range(4):
                    last = tr(bank(4 + g % 4, P, n, lo=q * P), xT[:, 4 * kg + q, j * P:j * P + n], ident[:, :])
                last.then_inc(S("y_turned"), 1)

        @block.vector
        def _(dve):
            v = nc.vector
            st = Steps(dve, "dve_step")
            tt, ts, stt = v.tensor_tensor, v.tensor_scalar, v.scalar_tensor_tensor
            MUL, ADD, SUB = ALU.mult, ALU.add, ALU.subtract

            for g in range(12):
                j, kg = g // 4, g % 4
                n = P if j < 2 else TS
                dve.wait_ge(S("x_turned"), g + 1)
                st(v.tensor_copy(xT[:, 4 * kg:4 * kg + 4, j * P:j * P + n],
                                 bank(4 + g % 4, 4 * n).rearrange("p (q t) -> p q t", q=4)), "x_transposed", wait=False)
            dve.wait_ge(S("setup_turned"), 1)
            st(v.tensor_copy(cT[:, :, :], bank(3, 32, lo=384).rearrange("p (k c) -> p k c", k=KD)), "setup_taken")
            dve.wait_ge(S("ld_loaded"), 32)
            dve.wait_ge(S("consts_a"), 1)
            for lo, n in ((0, 16), (32, 8)):
                last = v.tensor_copy(prow[lo:lo + n, 2, :].rearrange("p (g q) -> p g q", g=2),
                                     bc(ldrow[lo:lo + n, :].unsqueeze(2), [n, 2, 64]))
                st(last, "setup_taken" if lo else None)
            dve.wait_ge(S("setup_turned"), 2)
            st(v.tensor_copy(parT[:, 0:250], bank(3, 250)))
            st(v.tensor_copy(parT[:, 256:352], bank(3, 96, lo=256)), "setup_taken")
            dve.wait_ge(S("setup_turned"), 3)
            st(v.tensor_copy(xbcp[:, :, PADS - 3:PADS],
                             bank(2, 40).rearrange("p (i c) -> p i c", i=NXBC)[:, :, 0:3]), "setup_taken")
            st(v.memset(xbcp[:, :, 0:3], 0.0))
            cos_, sin_, dt_, ex, mag, th, wr_, wc, k_, lr, aR, aI, den, nr, cr, ci, t1, t2 = \
                (sm[:, i, :] for i in range(18))
            st(ts(lr, lam_re, -1e-4, None, ALU.min))
            dve.wait_ge(S("setup_act"), 2)
            st(tt(ex, lr, dt_, MUL), "setup_dve")
            st(tt(th, lam_im, dt_, MUL))
            magic = 12582912.0
            st(ts(k_, th, 0.15915494309189535, magic, MUL, ADD))
            st(ts(k_, k_, magic, None, SUB))
            st(stt(t1, k_, -6.28125, th, MUL, ADD))
            st(stt(t2, k_, -0.0019350051879882812, t1, MUL, ADD))
            st(stt(t1, k_, -3.0199159819e-07, t2, MUL, ADD))
            pi = 3.1415925
            st(ts(wr_, t1, pi, -pi, ALU.min, ALU.max))
            st(stt(t2, wr_, -1.0, wr_, MUL, ALU.max))
            st(ts(wc, t2, -1.0, 1.5707963267948966, MUL, ADD), "setup_dve")
            dve.wait_ge(S("setup_act"), 5)
            dve.wait_ge(S("setup_act"), 3)
            st(tt(aR, mag, cos_, MUL))
            st(tt(aI, mag, sin_, MUL))
            st(tt(t1, lr, lr, MUL))
            st(tt(t2, lam_im, lam_im, MUL))
            st(tt(den, t1, t2, ADD))
            st(v.reciprocal(den, den))
            st(ts(nr, aR, -1.0, None, ADD))
            st(tt(t1, nr, lr, MUL))
            st(tt(t2, aI, lam_im, MUL))
            st(tt(cr, t1, t2, ADD))
            st(tt(cr, cr, den, MUL))
            st(tt(t1, aI, lr, MUL))
            st(tt(t2, nr, lam_im, MUL))
            st(tt(ci, t1, t2, SUB))
            st(tt(ci, ci, den, MUL))
            dve.wait_ge(S("s5_loaded"), 64)
            dve.wait_ge(S("consts_b"), 1)
            for w in range(2):
                b0, b1 = (BR, BI) if w == 0 else (BI, BR)
                for g in range(2):
                    rows = slice(64 * g, 64 * g + 64)
                    crb, cib = (bc(x[rows, :].unsqueeze(2), [64, 16, 16]) for x in (cr, ci))
                    st(tt(btmp[rows], b1[rows], cib, MUL))
                    st(tt(bdp[rows, w, :, g, :], b0[rows], crb, MUL))
                    st(tt(bdp[rows, w, :, g, :], bdp[rows, w, :, g, :], btmp[rows], SUB if w == 0 else ADD))
            for w in range(2):
                for g in range(2):
                    last = st(ts(cpad[:, w, :, g, :], CR[:, w], small[:, g:g + 1], 1.0 if w == 0 else -1.0, MUL, MUL),
                              "s5_mats" if w and g else None)
            dve.wait_ge(S("squares_used"), 8)

            def mean_square(b, width):
                st(ts(rinv[:, :], bank(b, T), 1.0 / width, EPS, MUL, ADD), "mean_square")

            def invert(sem):
                dve.wait_ge(S(sem[0]), sem[1])
                st(v.reciprocal(rinv[:, :], rinv[:, :]))

            def modulate(g, sc):
                for s_ in range(2):
                    st(ts(ab1[:, :, s_], seg(sc)[:, :, s_], 1.0, None, ADD))
                    st(tt(ab1[:, :, s_], ab1[:, :, s_], g, MUL))
                dve.wait_ge(S("x_transposed"), 12)
                for k in range(0, KD, 4):
                    st(tt(hT[:, k:k + 4, :], xT[:, k:k + 4, :], bc(rinv[:, :].unsqueeze(1), [P, 4, T]), MUL),
                       "h_scaled" if k == KD - 4 else None)

            def shift_sample(sh):
                for k in range(KD):
                    st(ts(hT[:, k, TP:T], hT[:, k, TP:T], ab1[:, k, 1:2], seg(sh)[:, k, 1:2], MUL, ADD),
                       "h_sample", wait=False)

            mean_square(3, D)
            invert(("root", 1))
            dve.wait_ge(S("setup_turned"), 4)
            for w in range(2):
                st(v.tensor_copy(BDT[:, w], bank(4 + w).rearrange("p (u n) -> p u n", u=4)))
                st(v.tensor_copy(CT[:, w], bank(6 + w).rearrange("p (u n) -> p u n", u=4)),
                   "s5_mats_ready" if w else None)
            lb, omlb, e_, r_ = (small[:, 40 + 4 * i:44 + 4 * i] for i in range(4))
            st(tt(e_, lb_raw, lb_raw, SUB))
            st(ts(e_, e_, 1.0, None, ADD))
            st(v.reciprocal(r_, e_))
            st(tt(e_, e_, r_, MUL))
            st(tt(lb, e_, e_, SUB))
            st(ts(omlb, lb, -1.0, 1.0, MUL, ADD))

            def mod_take(j, q, n):
                src = bank(2, 4, lo=64 + 4 * (j % 2)).rearrange("p (q c) -> p q c", q=2)
                return v.tensor_tensor(q, src, n, ADD)

            for j in range(4):
                dve.wait_ge(S("mod_turned"), j + 1)
                mod_take(j, modT[:, 2 * j:2 * j + 2, :], bc(b_ada[:, 2 * j:2 * j + 2].unsqueeze(2), [P, 2, 2]))\
                    .then_inc(S("mod_ready"), 1)
            with dve.Fori(1, 4) as i:
                for j in range(4):
                    dve.wait_ge(S("mod_turned"), 4 * i + (j + 1))
                    mod_take(j, modT[:, bass.ds(i * 8 + 2 * j, 2), :],
                             bc(b_ada[:, bass.ds(i * 8 + 2 * j, 2)].unsqueeze(2), [P, 2, 2]))\
                        .then_inc(S("mod_ready"), 1)
            dve.wait_ge(S("mod_ready"), 16)
            modulate(g_mix, 1)
            shift_sample(0)

            def ada(i):
                if i > 16:
                    take(i - 1)

            def take(i):
                dve.wait_ge(S("mod_turned"), i + 1)
                mod_take(i, modT[:, 2 * i:2 * i + 2, :], bc(b_ada[:, 2 * i:2 * i + 2].unsqueeze(2), [P, 2, 2]))\
                    .then_inc(S("mod_ready"), 1)

            def s5_in(b):
                br, bi, yr, yi, tm = s5b[0:5]
                pc, ps = s5b[5 + 2 * (b % 2)], s5b[6 + 2 * (b % 2)]
                dve.wait_ge(S("s5_bu_sb"), 2 * b + 2)
                dve.wait_ge(S("s5_table"), b + 1)
                if b:
                    dve.wait_ge(S("s5_y"), b)
                st(tt(yr, br, pc, MUL))
                st(tt(tm, bi, ps, MUL))
                st(tt(yr, yr, tm, ADD))
                st(tt(yi, bi, pc, MUL))
                st(tt(tm, br, ps, MUL))
                st(tt(yi, yi, tm, SUB))
                for i in range(2):
                    n = 2 * b + i
                    for lo, hi in STREAMS:
                        for src, dst, x0 in ((yr, br, x0re), (yi, bi, x0im)):
                            last = v.tensor_tensor_scan(
                                dst[:, i * T + lo:i * T + hi], bc(mag[:, n:n + 1], [P, hi - lo]),
                                src[:, i * T + lo:i * T + hi], x0[:, n:n + 1] if lo else 0.0, MUL, ADD)
                            st(last, wait=False)
                dve.wait_ge(S("dve_step"), st.n["dve_step"])
                st(tt(yr, br, pc, MUL))
                st(tt(tm, bi, ps, MUL))
                st(tt(yr, yr, tm, SUB))
                st(tt(yi, br, ps, MUL))
                st(tt(tm, bi, pc, MUL))
                st(tt(yi, yi, tm, ADD))
                for k, (src, col) in enumerate(((yr, TP - 1), (yi, TP - 1), (yr, T - 1), (yi, T - 1))):
                    st(v.tensor_copy(s5fin[:, k, 2 * b:2 * b + 2].unsqueeze(2),
                                     src.rearrange("p (i t) -> p i t", i=2)[:, :, col:col + 1]),
                       "s5_turned" if k == 3 else None)

            def s5_out(b):
                if b % 2 == 0:
                    return
                u = b // 2
                y, y3 = sq[:, 1, T:2 * T], sq[:, 1, 0:T]
                dve.wait_ge(S("s5_y"), b + 1)
                st(stt(y, proj[:, U + u, :], s5_d[:, u:u + 1], bank(3, T), MUL, ADD))
                st(tt(y3, y, y, MUL))
                st(ts(y3, y3, 0.044715, 1.0, MUL, ADD))
                st(tt(y3, y3, y, MUL))
                st(ts(y3, y3, 1.5957691216057308, None, MUL), "s5_gelu_arg")
                dve.wait_ge(S("s5_gelu_sig"), u + 1)
                st(tt(proj[:, U + u, :], y, y3, MUL), "s5_g")

            def s5_glu():
                dve.wait_ge(S("glu_mm"), 4)
                for m in range(4):
                    dve.wait_ge(S("glu_sig"), m + 1)
                    st(tt(proj[:, U + m, :], proj[:, U + m, :], rinv[:, :], MUL), "glu_used")
                dve.wait_ge(S("s5_fin_turned"), 1)
                st(v.tensor_copy(sq[0:16, 1, 0:512], psum[0:16, 3, :]), "s5_fin_rows")

            hb3 = lambda t, m: t.rearrange("p (n r) -> p n r", r=2 * m)

            def hg_prep(hp):
                hf = flat[:, (HF + 2 * hp) * T:(HF + 2 * hp + 2) * T]
                dve.wait_ge(S("hg_sig"), hp + 1)
                for h in range(2):
                    c = slice(h * T, h * T + T)
                    n = 2 * hp + h
                    st(ts(hE[:, c], hE[:, c], omlb[:, n:n + 1], lb[:, n:n + 1], MUL, ADD))
                    st(ts(hf[:, c], hf[:, c], omlb[:, n:n + 1], None, MUL), "hg_k" if h else None)
                if hp:
                    dve.wait_ge(S("hg_o"), 2)
                st(ts(hE, hE, 1e-30, None, ALU.max))
                st(ts(hq_, hE, 2.0 ** -40, None, ALU.is_lt))
                st(ts(hb, hq_, 2.0 ** 50, 1.0, MUL, ADD))
                st(tt(hE, hE, hb, MUL), "hg_f")
                dve.wait_ge(S("hg_ln"), hp + 1)
                st(stt(hE, hq_, -34.657359, hE, MUL, ADD))
                for h in range(2):
                    c = slice(h * T, h * T + T)
                    st(v.tensor_tensor_scan(hb[:, c], rmask[:, :], hE[:, c], 0.0, MUL, ADD))
                dve.wait_ge(S("hg_v"), hp + 1)
                for h in range(2):
                    b3 = bank(6 + h, 384).rearrange("p (q k) -> p q k", q=3)
                    st(v.tensor_copy(vn[:, h, 0:2, :], b3[:, 0:2, :]))
                    st(v.tensor_copy(vn[0:64, h, 2, :], b3[0:64, 2, :]), "hg_vn" if h else None)

            def hg_take(hp, lv):
                it = 7 * hp + lv
                dve.wait_ge(S("hg_sc"), it + 1)
                src = bank(4 + it % 2, 384).rearrange("p (n t) -> p n t", n=6)
                dst = (hAT if lv == 0 else htmp).rearrange("p (n t) -> p n t", n=6)
                mask = bc(lmask[:, lv, :].unsqueeze(1), [P, 6, CH])
                st(tt(dst, src, mask, MUL), "hg_sc_used")
                if lv:
                    st(tt(hAT, hAT, htmp, ADD))

            def hg_level(hp, lv):
                q_, k_ = (flat[:, (x + 2 * hp) * T:(x + 2 * hp + 2) * T] for x in (HQ, HF))
                if lv == 0:
                    return
                m = LEVELS[lv]
                b3 = hb3(hb, m)
                st(tt(hb3(hE, m), b3, bc(b3[:, :, m - 1:m], [P, 640 // (2 * m), 2 * m]), SUB))
                st(stt(hE, hE, -1.0, hE, MUL, ALU.min), "hg_expo")
                hg_take(hp, lv - 1)
                dve.wait_ge(S("hg_exp"), 6 * hp + lv)
                st(tt(hq_, q_, hE, MUL))
                st(tt(hk_, k_, hE, MUL), "hg_qk")

            def hg_kd(hp):
                q_, k_ = (flat[:, (x + 2 * hp) * T:(x + 2 * hp + 2) * T] for x in (HQ, HF))
                hg_take(hp, 6)
                st(v.memset(small[:, 60:61], 0.0), "hg_expo2")
                dve.wait_ge(S("hg_exp2"), 2 * hp + 1)
                st(tt(hq_, q_, hE, MUL))
                e3, b3 = (t.rearrange("p (n r) -> p n r", r=CH) for t in (hE, hb))
                st(v.tensor_copy(small[:, 80:90].unsqueeze(2), e3[:, :, CH - 1:CH]))
                st(tt(e3, bc(b3[:, :, CH - 1:CH], [P, 10, CH]), b3, SUB), "hg_expo2")
                dve.wait_ge(S("hg_exp2"), 2 * hp + 2)
                st(tt(hE, k_, hE, MUL), "hg_kd")
                for h in range(2):
                    dve.wait_ge(S("hg_kd_turned"), 2 * hp + h + 1)
                    b4 = bank(6 + h, 384).rearrange("p (q k) -> p q k", q=3)
                    st(v.tensor_copy(kdn[:, h, 0:2, :], b4[:, 0:2, :]))
                    st(v.tensor_copy(kdn[0:64, h, 2, :], b4[0:64, 2, :]), "hg_kdn" if h else None)

            def hg_state(hp):
                for c in range(NCH):
                    dve.wait_ge(S("hg_dS"), NCH * hp + c + 1)
                    if c == 4:
                        dve.wait_ge(S("hg_in_loaded"), 16)
                    into = (0, 1, 2, 3, 5)[c]
                    frm = (None, 0, 1, 2, 4)[c]
                    for h in range(2):
                        add = bank(6 + c % 2, P, lo=h * P)
                        dst = hS[:, into, 2 * hp + h, :]
                        if frm is None:
                            last = v.tensor_copy(dst, add)
                        else:
                            last = stt(dst, hS[:, frm, 2 * hp + h, :], small[:, 80 + 5 * h + c:81 + 5 * h + c],
                                       add, MUL, ADD)
                        st(last, "hg_S" if h else None)

            def hg_out(hp):
                for h in range(2):
                    n = 2 * hp + h
                    dve.wait_ge(S("hg_ss"), n + 1)
                    st(ts(rinv[:, :], bank(6 + h, T), 1.0 / P, EPS, MUL, ADD), "hg_var")
                    invert(("hg_root", n + 1))
                    st(stt(hb[:, 0:T], bank(4 + h, T), hg_g[:, n:n + 1], rinv[:, :], MUL, MUL))
                    dve.wait_ge(S("hg_gate"), hp + 1)
                    st(tt(proj[:, HG + n, :], proj[:, HG + n, :], hb[:, 0:T], MUL), "hg_normed")

            def ssd_conv():
                dve.wait_ge(S("bulk_evac"), 55)
                dve.wait_ge(S("bulk_done"), 55)
                dve.wait_ge(S("hg_state_stored"), 32)
                st(v.memset(ctil, 0.0))
                bias, alog = small[0:NH, 32:33], small[0:NH, 34:35]
                x_, e_, u_, l_, raw = (dtw[:, i, :] for i in range(5))
                st(v.tensor_copy(raw, dt_raw))
                st(ts(raw, raw, bias, None, ADD))
                st(stt(x_, raw, -1.0, raw, MUL, ALU.min), "dt_arg")
                dve.wait_ge(S("dt_func"), 1)
                st(ts(u_, e_, 1.0, None, ADD), "dt_arg")
                dve.wait_ge(S("dt_func"), 2)
                st(ts(u_, u_, -1.0, None, ADD))
                st(ts(x_, u_, 0.0, None, ALU.is_equal))
                st(tt(u_, u_, x_, ADD))
                st(tt(l_, l_, x_, ADD))
                st(v.reciprocal(u_, u_))
                st(tt(l_, l_, e_, MUL))
                st(tt(l_, l_, u_, MUL))
                st(ts(x_, raw, 0.0, None, ALU.max))
                st(tt(dtw[:, 1, :], x_, l_, ADD))
                dve.wait_ge(S("setup_act"), 4)
                st(ts(l_, dtw[:, 1, :], alog, -1.0, MUL, MUL))
                st(v.tensor_tensor_scan(dtw[:, 0, :], rmask[0:NH, :], l_, 0.0, MUL, ADD), "dt_done")
                for s_, c0 in ((0, PADP + TP - 3), (1, PADS + TS - 3)):
                    st(v.tensor_copy(cvout[:, :, 3 * s_:3 * s_ + 3], xbcp[:, :, c0:c0 + 3]), "cv_new" if s_ else None)
                for i in range(NXBC):
                    for lo, hi in STREAMS:
                        p0 = (PADP if lo == 0 else PADS) - 3
                        n = hi - lo
                        dst = xbcT[:, i, lo:hi]
                        st(ts(dst, xbcp[:, i, p0:p0 + n], conv_w[:, 0, i:i + 1], conv_b[:, i:i + 1], MUL, ADD))
                        for j in range(1, 4):
                            st(stt(dst, xbcp[:, i, p0 + j:p0 + j + n], conv_w[:, j, i:i + 1], dst, MUL, ADD),
                               "conv_out" if lo and j == 3 else None)

            def ssd_gamma():
                dve.wait_ge(S("bdt_turned"), 1)
                src = bank(6, 96).rearrange("p (q w h) -> p q w h", q=3, w=2)
                st(v.tensor_copy(bnat[:, 0:2].rearrange("p q w h -> p (q w h)"), bank(6, 64)))
                st(v.tensor_copy(bnat[0:64, 2].rearrange("p w h -> p (w h)"), bank(6, 32, 64, lo=64)), "bdt_taken")
                dve.wait_ge(S("cv_new_turned"), 1)
                st(v.tensor_copy(cvst[0:6, :], psum[0:6, 3:6, :].rearrange("p b n -> p (b n)")[:, 0:NXBC * P]),
                   "cv_stored")

            def ssd_nat(q):
                n = P if q < 2 else TS
                if q == 0:
                    dve.wait_ge(S("cv_saved"), 32)
                dve.wait_ge(S("ssd_nat"), q + 1)
                st(tt(v_[0:n, :].rearrange("p (h n) -> p h n", h=NH),
                      psum[0:n, 4:6, :].rearrange("p b n -> p (b n)").rearrange("p (h n) -> p h n", h=NH),
                      bc(bnat[0:n, q, 1, :].unsqueeze(2), [n, NH, 64]), MUL))
                st(v.tensor_copy(bn[0:n, :], bank(6, P, n)))
                st(tt(gtm[0:n, :].rearrange("p (g t) -> p g t", g=2), psum[0:n, 6:8, P:P + CH],
                      bc(causal[0:n, :].unsqueeze(1), [n, 2, CH]), MUL))

            def ssd_decay(c):
                half = slice(CH * (c % 2), CH * (c % 2) + CH)
                cols = slice(c * CH, c * CH + CH)
                q = c // 2
                st(tt(dg[0:NH, :].rearrange("p (h t) -> p h t", h=NH),
                      bc(dtw[:, 0, cols].unsqueeze(1), [NH, NH, CH]),
                      bc(ident[0:NH, 0:NH].unsqueeze(2), [NH, NH, CH]), MUL), "ssd_diag")
                dve.wait_ge(S("ssd_b"), c + 1)
                bB = psum[half, 4:6, :].rearrange("p b n -> p (b n)").rearrange("p (h t) -> p h t", h=NH)
                dl = small[half, 64:80]
                st(tt(dl, bB[:, :, CH - 1], bnat[half, q, 0, :], SUB))
                w3 = W[half, :].rearrange("p (h t) -> p h t", h=NH)
                st(tt(w3, bB, bc(bnat[half, q, 0, :].unsqueeze(2), [CH, NH, CH]), SUB), "ssd_diff")
                st(ts(W[half, :], W[half, :], 0.0, None, ALU.min), "ssd_diff")
                dve.wait_ge(S("ssd_exp"), 2 * c + 1)
                st(tt(vd[half, :].rearrange("p (h n) -> p h n", h=NH), v_[half, :].rearrange("p (h n) -> p h n", h=NH),
                      bc(dl.unsqueeze(2), [CH, NH, 64]), MUL), "ssd_vd")
                dve.wait_ge(S("ssd_EB"), 2 * c + 2)
                e3 = EB.rearrange("p (j t) -> p j t", j=8)
                for g in range(2):
                    rows = slice(64 * g, 64 * g + 64)
                    st(tt(ctil[rows, 512 * g:512 * g + 512].rearrange("p (j t) -> p j t", j=8), e3[rows],
                          bc(xbcT[rows, 9, cols].unsqueeze(1), [64, 8, CH]), MUL))
                dve.wait_ge(S("ssd_exp"), 2 * c + 2)
                for g in range(2):
                    st(tt(W[half, 512 * g:512 * g + 512].rearrange("p (h t) -> p h t", h=8),
                          W[half, 512 * g:512 * g + 512].rearrange("p (h t) -> p h t", h=8),
                          bc(gtm[half, g * CH:g * CH + CH].unsqueeze(1), [CH, 8, CH]), MUL), "ssd_W" if g else None)

            def ssd_y(c):
                cols = slice(c * CH, c * CH + CH)
                e3 = EB.rearrange("p (j t) -> p j t", j=8)
                into = (0, 1, 2, 3, 5)[c]
                frm = (None, 0, 1, 2, 4)[c]
                dve.wait_ge(S("ssd_dS"), c + 1)
                if frm is None:
                    st(v.tensor_copy(aS[:, into, :], bank(7)))
                else:
                    if c == 4:
                        dve.wait_ge(S("ssd_in_loaded"), 32)
                    st(tt(aS[:, into, :].rearrange("p (j n) -> p j n", j=8),
                          aS[:, frm, :].rearrange("p (j n) -> p j n", j=8),
                          bc(e3[:, :, CH - 1:CH], [P, 8, 64]), MUL))
                    st(tt(aS[:, into, :], aS[:, into, :], bank(7), ADD))
                st(v.memset(small[:, 61:62], 0.0), "ssd_S")
                y3 = ytmp.rearrange("p (i t) -> p i t", i=8)
                st(tt(y3, xbcT[:, 0:8, cols], bc(ssd_D.unsqueeze(2), [P, 8, CH]), MUL))
                dve.wait_ge(S("ssd_y"), c + 1)
                st(tt(ytmp, ytmp, bank(3), ADD))
                dve.wait_ge(S("z_silu"), 1)
                st(tt(proj[:, 0:8, cols], proj[:, 0:8, cols], y3, MUL), "ssd_done")

            def ssd_norm():
                dve.wait_ge(S("squares_used"), NORM["ssd"] + 4)
                mean_square(3, 1024)
                invert(("root", 2))
                z = proj[:, 0:8, :]
                st(tt(z, z, bc(rinv[:, :].unsqueeze(1), [P, 8, T]), MUL))
                st(tt(z, z, bc(ssd_g.unsqueeze(2), [P, 8, T]), MUL), "merged")

            for item in PLAN:
                kind = item[0]
                if kind == "ada":
                    ada(item[1])
                elif kind == "s5_in":
                    s5_in(item[1])
                elif kind == "s5_out":
                    s5_out(item[1])
                elif kind == "s5_glu":
                    s5_glu()
                elif kind == "hg_prep":
                    hg_prep(item[1])
                elif kind == "hg_level":
                    hg_level(item[1], item[2])
                elif kind == "hg_kd":
                    hg_kd(item[1])
                elif kind == "hg_state":
                    hg_state(item[1])
                elif kind == "hg_out":
                    hg_out(item[1])
                elif kind == "ssd_conv":
                    ssd_conv()
                elif kind == "ssd_gamma":
                    ssd_gamma()
                elif kind == "ssd_nat":
                    ssd_nat(item[1])
                elif kind == "ssd_decay":
                    ssd_decay(item[1])
                elif kind == "ssd_y":
                    ssd_y(item[1])
                elif kind == "ssd_norm":
                    ssd_norm()
            take(47)
            dve.wait_ge(S("mod_ready"), 48)

            for m in range(KD):
                dve.wait_ge(S("out_done"), m + 1)
                for s_, (lo, hi) in enumerate(STREAMS):
                    st(stt(xT[:, m, lo:hi], bank(4 + m % 4, T)[:, lo:hi], seg(2)[:, m, s_:s_ + 1],
                           xT[:, m, lo:hi], MUL, ADD), "x_mixed", wait=False)
            dve.wait_ge(S("x_mixed"), 32)
            dve.wait_ge(S("squares_used"), NORM["n2"] + 8)
            mean_square(3, D)
            invert(("root", 3))
            modulate(g_ffn, 4)
            shift_sample(3)

            lg = rt[:, 400:508].rearrange("p (j e) -> p j e", j=3)
            states_stored(dve)
            st(v.memset(rt, 0.0))
            dve.wait_ge(S("logits"), 1)
            st(v.tensor_copy(rt[:, 400:472], bank(2, 72)))
            st(v.tensor_copy(rt[0:64, 472:508], bank(2, 36, 64, lo=72)))
            G = lg[:, :, 0:4]
            ex4 = rt[:, 16:28].rearrange("p (j e) -> p j e", j=3)
            m3 = rt[:, 0:3].unsqueeze(2)
            st(v.tensor_reduce(m3, G, AX.X, ALU.max))
            st(tt(ex4, G, bc(m3, [P, 3, 4]), SUB))

            def first_max(dst, src, mx, n, tmp, idx):
                c = bc(small[:, 16:16 + n].unsqueeze(1), [P, 3, n])
                st(tt(dst, src, bc(mx, [P, 3, n]), ALU.is_equal))
                st(tt(tmp, dst, c, MUL))
                st(v.tensor_reduce(idx, tmp, AX.X, ALU.min))
                st(tt(dst, c, bc(idx, [P, 3, n]), ALU.is_equal))

            f3 = lambda off, n: rt[:, off:off + 3 * n].rearrange("p (j e) -> p j e", j=3)
            idx = rt[:, 4:7].unsqueeze(2)
            oh4 = f3(32, 4)
            first_max(oh4, G, m3, 4, f3(48, 4), idx)
            le4 = rt[:, 128:224].rearrange("p (j e) -> p j e", j=3)
            for g in range(4):
                st(tt(le4[:, :, 8 * g:8 * g + 8], lg[:, :, 4 + 8 * g:12 + 8 * g], bc(oh4[:, :, g:g + 1], [P, 3, 8]), MUL))
            le = f3(64, 8)
            st(tt(le, le4[:, :, 0:8], le4[:, :, 8:16], ADD))
            st(tt(le, le, le4[:, :, 16:24], ADD))
            st(tt(le, le, le4[:, :, 24:32], ADD))
            v1, v2 = rt[:, 8:11].unsqueeze(2), rt[:, 12:15].unsqueeze(2)
            oh1, oh2, tmp8, le2 = f3(96, 8), f3(256, 8), f3(288, 8), f3(320, 8)
            st(v.tensor_reduce(v1, le, AX.X, ALU.max))
            first_max(oh1, le, v1, 8, tmp8, idx)
            st(stt(le2.rearrange("p j e -> p (j e)"), oh1.rearrange("p j e -> p (j e)"), -3e38,
                   le.rearrange("p j e -> p (j e)"), MUL, ADD))
            st(v.tensor_reduce(v2, le2, AX.X, ALU.max))
            first_max(oh2, le2, v2, 8, tmp8, idx)
            st(tt(rt[:, 240:243].unsqueeze(2), v2, v1, SUB), "rt_expo")
            dve.wait_ge(S("rt_exp"), 1)
            e2, den, w1, w2 = (rt[:, 240 + 3 * i:243 + 3 * i].unsqueeze(2) for i in range(4))
            st(v.tensor_reduce(den, ex4, AX.X, ALU.add))
            st(v.reciprocal(den, den))
            st(ts(w1, e2, 1.0, None, ADD))
            st(v.reciprocal(w1, w1))
            st(tt(w1, w1, den, MUL))
            st(tt(w2, w1, e2, MUL))
            for g in range(4):
                for A_, oh_ in ((A1, oh1), (A2, oh2)):
                    st(tt(A_[:, :, 8 * g:8 * g + 8], oh_, bc(oh4[:, :, g:g + 1], [P, 3, 8]), MUL))
            st(v.memset(A1[64:P, 2, :], 0.0))
            st(v.memset(A2[64:P, 2, :], 0.0))
            st(tt(Mk, A1, A2, ADD), "routed")
            dve.wait_ge(S("slot_consts"), 1)
            st(v.tensor_copy(e64, e64i))
            dve.wait_ge(S("rank"), 1)
            st(v.tensor_copy(eT, eTi))
            st(v.memset(rk, 0.0))
            st(v.tensor_copy(rk[:, 0:2, :], bank(3, 64).rearrange("p (j e) -> p j e", j=2)))
            st(v.tensor_copy(rk[0:64, 2, :], bank(3, NE, 64, lo=64)))
            st(ts(ge, rk, float(CAP), None, ALU.is_ge))
            st(ts(Mk, rk, float(NPAIR), None, MUL))
            st(tt(Mk, Mk, bc(eT.unsqueeze(1), [P, 3, NE]), ADD))
            st(tt(rk, rk, bc(e64.unsqueeze(1), [P, 3, NE]), ADD))
            over, sl_, keep = rt[:, 484:490], rt[:, 490:496], rt[:, 500:506]
            for c, (A_, w_) in enumerate(((A1, w1), (A2, w2))):
                cc = slice(3 * c, 3 * c + 3)
                st(tt(am, A_, ge, MUL))
                st(v.tensor_reduce(over[:, cc].unsqueeze(2), am, AX.X, ADD))
                st(tt(am, A_, rk, MUL))
                st(v.tensor_reduce(sl_[:, cc].unsqueeze(2), am, AX.X, ADD))
                st(tt(am, A_, Mk, MUL))
                st(v.tensor_reduce(rt[:, 472 + 3 * c:475 + 3 * c].unsqueeze(2), am, AX.X, ADD))
            st(tt(rt[:, 496:499], over[:, 0:3], over[:, 3:6], ADD), "routed")
            st(ts(keep, over, -1.0, 1.0, MUL, ADD))
            st(stt(rt[:, 472:478], over, 1.0e6, rt[:, 472:478], MUL, ADD))
            st(v.tensor_copy(pos_scatter, rt[:, 472:478]), "routed")
            st(tt(rt[:, 478:484], sl_, keep, MUL))
            st(v.tensor_copy(pos_gather, rt[:, 478:484]), "routed")
            for c, (A_, w_) in enumerate(((A1, w1), (A2, w2))):
                st(tt(A_, A_, bc(w_, [P, 3, NE]), MUL))
            st(tt(comb, A1, A2, ADD))
            st(tt(comb, comb, ge, MUL))
            wk = rt[:, 506:512]
            st(tt(wk[:, 0:3].unsqueeze(2), w1, keep[:, 0:3].unsqueeze(2), MUL))
            st(tt(wk[:, 3:6].unsqueeze(2), w2, keep[:, 3:6].unsqueeze(2), MUL))
            dve.wait_ge(S("rank"), 2)
            st(v.tensor_reduce(rt[:, 499:500], bank(3, 3), AX.X, ADD))
            st(v.tensor_copy(spill, rt[:, 499:500]), "routed")

            def take_x(i, g_, par):
                dve.wait_ge(S("xe_turned"), 4 * i + (g_ + 1))
                v.tensor_copy(xe[par][:, 4 * g_:4 * g_ + 4, :], bank(6 + g_ % 2).rearrange("p (k t) -> p k t", k=4))\
                    .then_inc(S("xe_ready"), 1)

            def activate(h, e):
                rows_ = slice(CAP * h, CAP * h + CAP)
                dve.wait_ge(S("gate_silu"), e + 1)
                if not (isinstance(e, int) and e < 2):
                    dve.wait_ge(S("act_turned"), e - 1)
                tt(asb[rows_, :], sg[rows_, :], psum[rows_, 0, CW:2 * CW], MUL).then_inc(S("act_ready"), 1)

            def take_act(h, e):
                dve.wait_ge(S("act_turned"), e + 1)
                if not (isinstance(e, int) and e < 2):
                    dve.wait_ge(S("down_done"), e - 1)
                v.tensor_copy(aTT[:, h], bank(5, 2 * CAP).rearrange("p (f t) -> p f t", f=2)).then_inc(S("actT_ready"), 1)

            def take_y(h, e):
                rows_ = slice(CAP * h, CAP * h + CAP)
                dve.wait_ge(S("down_done"), e + 1)
                if not (isinstance(e, int) and e < 2):
                    dve.wait_ge(S(f"y_stored{h}"), 8 * (e - h))
                v.tensor_copy(ys[rows_, :], psum[rows_, 1:5, :].rearrange("p b n -> p (b n)")).then_inc(S("y_rows_sb"), 1)

            def pair(i, par, more):
                first = isinstance(i, int) and i == 0
                if not first:
                    take_act(1, 2 * i - 1)
                activate(0, 2 * i)
                if not first:
                    take_y(1, 2 * i - 1)
                if more:
                    take_x(i + 1, 0, 1 - par)
                    take_x(i + 1, 1, 1 - par)
                take_act(0, 2 * i)
                activate(1, 2 * i + 1)
                take_y(0, 2 * i)
                if more:
                    take_x(i + 1, 2, 1 - par)
                    take_x(i + 1, 3, 1 - par)

            dve.wait_ge(S("h2_stored"), 32)
            for g_ in range(4):
                take_x(0, g_, 0)
            pair(0, 0, True)
            pair(1, 1, True)
            with dve.Fori(1, QUADS - 1) as q:
                pair(2 * q, 0, True)
                pair(2 * q + 1, 1, True)
            pair(NPAIR - 2, 0, True)
            pair(NPAIR - 1, 1, False)
            take_act(1, NE - 1)
            take_y(1, NE - 1)
            for j in range(3):
                n = P if j < 2 else TS
                dve.wait_ge(S(f"rows_landed{j}"), 32)
                st(ts(r1[0:n, j, :], r1[0:n, j, :], wk[0:n, j:j + 1], None, MUL))
                st(stt(r1[0:n, j, :], r2[0:n, j, :], wk[0:n, 3 + j:4 + j], r1[0:n, j, :], MUL, ADD), "rows_summed")
            for g in range(12):
                j, kg = g // 4, g % 4
                n = P if j < 2 else TS
                dve.wait_ge(S("m_turned"), g + 1)
                for q in range(4):
                    k = 4 * kg + q
                    cols = slice(j * P, j * P + n)
                    st(stt(xT[:, k, cols], bank(6 + g % 2, n, lo=q * n), seg(5)[:, k, j // 2:j // 2 + 1],
                           xT[:, k, cols], MUL, ADD), "m_added" if q == 3 else None, wait=False)
            dve.wait_ge(S("m_added"), 12)
            dve.wait_ge(S("dve_step"), st.n["dve_step"])
            with dve.If(dve.value_load(spill[0:1, :], min_val=0, max_val=2 * T) > 0):
                dve.wait_ge(S("fb_comb_turned"), 1)
                v.memset(acc, 0.0).then_inc(S("fb_dve"), 1)
                dve.wait_ge(S("fb_dve"), 1)
                v.tensor_copy(combT, psum[0:NE, 3, 0:T]).then_inc(S("fb_dve"), 1)
                v.memset(small[:, 62:63], 0.0).then_inc(S("fb_added"), 1)
                dve.wait_ge(S("fb_rows"), 32)
                s3 = sgc.rearrange("p (f t) -> p f t", f=2)
                a3 = act_.rearrange("p (f t) -> p f t", f=2)
                with dve.Fori(1, NE + 1) as e:
                    dve.wait_ge(S("fb_silu"), e)
                    cb = combB[:, bass.ds((e - 1) * T, T)]
                    tt(s3, s3, bc(cb.unsqueeze(1), [P, 2, T]), MUL).then_inc(S("fb_weighted"), 1)
                    dve.wait_ge(S("fb_weighted"), e)
                    tt(a3, s3, psum[:, 2:4, 0:T], MUL).then_inc(S("fb_act"), 1)
                    for g in range(4):
                        dve.wait_ge(S("fb_down"), 4 * e + (g - 3))
                        tt(acc[:, 4 * g:4 * g + 4, :], acc[:, 4 * g:4 * g + 4, :], psum[:, 4:8, 0:T], ADD)\
                            .then_inc(S("fb_added"), 1)
                dve.wait_ge(S("fb_added"), 4 * NE + 1)
                for m in range(KD):
                    for s_, (lo, hi) in enumerate(STREAMS):
                        last = stt(xT[:, m, lo:hi], acc[:, m, lo:hi], seg(5)[:, m, s_:s_ + 1], xT[:, m, lo:hi], MUL, ADD)
                last.then_inc(S("fb_dve"), 1)
                dve.wait_ge(S("fb_dve"), 3)
            st(v.memset(small[:, 63:64], 0.0), "x_final")
            dve.wait_ge(S("squares_used"), NORM["n3"] + 8)
            mean_square(3, D)
            invert(("root", 4))
            for k in range(KD):
                st(stt(xT[:, k, :], xT[:, k, :], g_fin[:, k:k + 1], rinv[:, :], MUL, MUL), wait=False)
            dve.wait_ge(S("dve_step"), st.n["dve_step"])
            st(v.memset(small[:, 62:63], 0.0), "y_ready")
            for g in range(12):
                j, kg = g // 4, g % 4
                n = P if j < 2 else TS
                dve.wait_ge(S("y_turned"), g + 1)
                st(v.tensor_copy(ynat[0:n, j, kg * 512:kg * 512 + 512], bank(4 + g % 4, 512, n)), "y_rows", wait=False)


_INS = ["x_prompt", "x_sample", "c_prompt", "c_sample", "state_conv", "state_ssd", "state_hgrn", "state_s5_re",
        "state_s5_im", "w_ada", "b_ada", "g_mix", "g_ffn", "w_in", "conv_w", "conv_b", "ssd_dt_bias", "ssd_a_log",
        "ssd_d", "ssd_norm_g", "hgrn_lb_raw", "hgrn_norm_g", "s5_lam_re", "s5_lam_im", "s5_log_dt", "s5_b_re",
        "s5_b_im", "s5_c_re", "s5_c_im", "s5_d", "s5_w_glu", "s5_b_glu", "w_out", "w_router_group",
        "b_router_group", "w_router_expert", "b_router_expert", "w_exp_gate", "w_exp_up", "w_exp_down", "g_final"]
_STATES = [("conv", (1, 1, 3, 1280)), ("ssd", (1, 1, 16, 64, 64)), ("hgrn", (1, 1, 4, 128, 128)),
           ("s5re", (1, 1, 32, 64)), ("s5im", (1, 1, 32, 64))]
_OUTS = [("y_prompt", (1, TP, D)), ("y_sample", (1, TS, D))] \
    + [(f"{n}_{s}", shape) for s in "ps" for n, shape in _STATES]


def kernel(**inputs):
    import numpy as _np
    import concourse.bacc as _bacc
    from concourse.bass_utils import run_bass_kernel_spmd as _run

    nc = _bacc.Bacc("TRN2", target_bir_lowering=False, num_devices=1)
    arrays, ins, outs = {}, {}, {}
    for name in _INS:
        x = _np.ascontiguousarray(inputs[name])
        arrays[f"in_{name}"] = x
        ins[name] = nc.dram_tensor(f"in_{name}", x.shape, mybir.dt.from_np(x.dtype), kind="ExternalInput").ap()
    for name, shape in _OUTS:
        outs[name] = nc.dram_tensor(f"out_{name}", shape, F32, kind="ExternalOutput").ap()
    build(nc, ins, outs)
    r = _run(nc, [arrays], core_ids=[0])
    return tuple(r.results[0][f"out_{name}"] for name, _ in _OUTS)
```

```python
from contextlib import ExitStack

import concourse.bass as bass
from concourse import mybir

F32 = mybir.dt.float32
I32 = mybir.dt.int32
ALU = mybir.AluOpType
ACT = mybir.ActivationFunctionType
AX = mybir.AxisListType

P = 128
D = 2048
KD = D // P
TP, TS = 256, 64
T = TP + TS
CH = 64
NCH = T // CH
STREAMS = ((0, TP), (TP, T))
NXBC = 10
PADP, PADS = 3, 3 + TP + 3
TPAD = T + 6
Z, HQ, HF, HI, HG, U = 0, 8, 12, 16, 20, 24
NPROJ = 28
NH = 16
CW = 256
RING = 4
ADA1, MIDDLE, OUTP, PRE = 0, 16, 72, 76
NE = 32
CAP = 64
NPAIR = NE // 2
QUADS = NE // 4
COL_HG, COL_DT = 2320, 2304
NORM = {"n1": 0, "ssd": 8, "n2": 12, "n3": 20}
LEVELS = (0, 32, 16, 8, 4, 2, 1)
EPS = 1e-6

IN_CHUNKS = [(4368, U), (4624, U + 2), (0, Z)]
IN_CHUNKS += [(COL_HG + CW * i, HQ + 2 * i) for i in range(8)]
AFTER_HG = len(IN_CHUNKS)
IN_CHUNKS += [(COL_DT, None)]
IN_CHUNKS += [(CW * i, Z + 2 * i) for i in range(1, 4)]
IN_CHUNKS += [(1024 + CW * i, 100 + 2 * i) for i in range(5)]

START = [0, 1, "x", 2, 3, "parameters", 4, 5, "s5", 6, 7, "norm", 8, 9, "s5_matrices"] + list(range(10, 16))


def make_plan():
    ins = [("in", n, q) for n in range(len(IN_CHUNKS)) for q in range(1 if IN_CHUNKS[n][1] is None else 2)]
    adas = [("ada", a) for a in range(16, 48)]
    outs = [("out", n, q) for n in range(4) for q in range(4)]
    plan = [ins.pop(0) for _ in range(4)]
    bulk = [[ins.pop(0), adas.pop(0), ins.pop(0)] for _ in range(9)]
    left, steps = len(ins), 23
    for i in range(steps):
        piece = [ins.pop(0)] if (i + 1) * left // steps > i * left // steps else []
        bulk.append(piece + ([adas.pop(0)] if i % 4 == 1 or not piece else []))
    steps = 15
    for i in range(steps):
        bulk.append((adas[:1] if i else []) + [outs.pop(0) for _ in range(2 if i == steps - 6 else 1)])
        adas = adas[1:] if i else adas
    bulk += [[x] for x in adas + outs]
    s5 = []
    for b in range(8):
        s5 += [("s5_in", b), None, ("s5_out", b)]
    s5 += [None, ("s5_glu", 0), None]
    hg = []
    for hp in range(2):
        hg += [("hg_prep", hp), None]
        for lv in range(len(LEVELS)):
            hg += [("hg_level", hp, lv), None]
        hg += [("hg_kd", hp), None, ("hg_state", hp), None, ("hg_out", hp), None]
    ssd = [("ssd_dt", 0), None]
    for i in range(NXBC // 2):
        ssd += [("ssd_conv", i), None]
    ssd += [("ssd_gamma", 0), None]
    for c in range(NCH):
        if c % 2 == 0:
            ssd += [("ssd_nat", c // 2), None]
        ssd += [("ssd_decay", c), None, ("ssd_y", c)]
    ssd += [None, ("ssd_norm", 0)]
    for item in s5 + hg + ssd:
        if item is None:
            if bulk:
                plan += bulk.pop(0)
        else:
            if item[0] == "ssd_dt":
                while any(x[0] == "in" for group in bulk for x in group):
                    plan += bulk.pop(0)
            plan.append(item)
    return plan + [x for group in bulk for x in group]


PLAN = make_plan()
CHUNKS, GROUP, DONE = [], {}, []
groups_ = 16
for item_ in PLAN:
    if item_[0] in ("in", "ada", "out"):
        if item_[:2] not in CHUNKS:
            CHUNKS.append(item_[:2])
            DONE.append(0)
        GROUP[item_] = groups_
        groups_ += 1
        DONE[CHUNKS.index(item_[:2])] = groups_
ALL_GROUPS = groups_
OUT_PIECES = [item_ for item_ in PLAN if item_[0] == "out"]


def build(nc, a, o):
    ctx = ExitStack()
    with ctx:
        def sb(name, shape, dt=F32):
            return ctx.enter_context(nc.sbuf_tensor(name, shape, dt))

        sems = {}

        def S(name):
            if name not in sems:
                sems[name] = ctx.enter_context(nc.semaphore(name))
            return sems[name]

        psum = ctx.enter_context(nc.psum_tensor("psum", [P, 8, 512], F32))

        def bank(b, cols=512, part=P, lo=0):
            return psum[0:part, b, lo:lo + cols]

        xT = sb("xT", [P, KD, T])
        hT = sb("hT", [P, KD, T])
        slot = sb("slot", [P, RING, KD * CW])
        mem = sb("mem", [P, NPROJ * T + NXBC * TPAD + 7808])
        sq = sb("sq", [P, 2, 2 * T])
        rinv = sb("rinv", [P, T])
        ident = sb("ident", [P, P])
        ones = sb("ones", [P, P])
        rmask = sb("rmask", [P, T])
        lmask = sb("lmask", [P, len(LEVELS), CH])
        causal = sb("causal", [P, CH])
        parT = sb("parT", [P, 3 * P])
        modT = sb("modT", [P, 6 * KD, 2])
        rows = sb("rows", [P, 2 * CW])
        modrow = rows[:, :].rearrange("p (j n) -> p j n", j=2)
        cT = sb("cT", [P, KD, 2])
        sm = sb("sm", [P, 18, 16])
        BDT = sb("BDT", [P, 2, 4, P])
        dt_raw = BDT[0:NH, 0, :, :].rearrange("p u n -> p (u n)")[:, 0:T]
        CT = sb("CT", [P, 2, 4, P])
        ab1 = sb("ab1", [P, KD, 2])
        small = sb("small", [P, 96])
        sel = small[:, 92:94]
        s5fin = sb("s5fin", [P, 4, 16])

        proj = mem[:, 0:NPROJ * T].rearrange("p (n t) -> p n t", n=NPROJ)
        XB0 = NPROJ * T
        xbcp = mem[:, XB0:XB0 + NXBC * TPAD].rearrange("p (n t) -> p n t", n=NXBC)
        A0 = XB0 + NXBC * TPAD

        def ar(off, n):
            return mem[:, A0 + off:A0 + off + n]

        flat = mem[:, :]
        xnat = ar(0, 3 * D).rearrange("p (j d) -> p j d", j=3)
        prow = flat[:, 0:384].rearrange("p (j d) -> p j d", j=3)
        crow = flat[0:2, 384:384 + D]
        BR = flat[:, 2432:2688].rearrange("p (i j) -> p i j", i=16)
        BI = flat[:, 2688:2944].rearrange("p (i j) -> p i j", i=16)
        CR = flat[:, 2944:3456].rearrange("p (w u q) -> p w u q", w=2, u=4)
        bdp = flat[:, 3456:4480].rearrange("p (w i g j) -> p w i g j", w=2, i=16, g=2)
        cpad = flat[:, 4480:5504].rearrange("p (w u g q) -> p w u g q", w=2, u=4, g=2)
        btmp = flat[:, 5504:5760].rearrange("p (i j) -> p i j", i=16)
        cvrow = flat[0:3, 5760:7040]
        ldrow = flat[0:48, 7040:7042]
        s5b = [ar(640 * i, 640) for i in range(9)]
        wglu = ar(5760, 2048).rearrange("p (k m) -> p k m", k=4)
        hb, hE, hq_, hk_ = (ar(640 * i, 640) for i in range(4))
        htmp = ar(2560, 384)
        kdn = ar(1920, 768).rearrange("p (h q k) -> p h q k", h=2, q=3)
        hAT = ar(2944, 384)
        vn = ar(3328, 768).rearrange("p (h q k) -> p h q k", h=2, q=3)
        hS = ar(4096, 3072).rearrange("p (s h v) -> p s h v", s=6, h=4)
        dg = ar(0, 1024)
        W = ar(1024, 1024)
        v_ = ar(2048, 1024)
        vd = ar(3072, 1024)
        ctil = ar(4096, 1024)
        EB = ar(5120, 512)
        bn = ar(5632, 128)
        ytmp = ar(5760, 512)
        gtm = ar(6272, 128)
        cvout = ar(6400, 60).rearrange("p (i c) -> p i c", i=NXBC)
        cvst = ar(0, NXBC * P)
        aS = flat[:, HQ * T:HQ * T + 3072].rearrange("p (s n) -> p s n", s=6)
        hflat = hT[:, :, :].rearrange("p k t -> p (k t)")
        xbcT = hflat[:, 0:NXBC * T].rearrange("p (n t) -> p n t", n=NXBC)
        dtw = hflat[0:NH, 3200:3200 + 5 * T].rearrange("p (w t) -> p w t", w=5)
        bnat = hflat[:, 4800:4896].rearrange("p (q w h) -> p q w h", q=3, w=2)
        U32 = mybir.dt.uint32
        idx_ = sb("idx", [P, 40], U32)
        pos_scatter, pos_gather, tokid = idx_[:, 0:6], idx_[:, 6:12], idx_[:, 12:15]
        spill = idx_[:, 15:16].bitcast(I32)
        slot_tok = idx_[:, 16:32]
        gu = [slot[:, 2 * h:2 * h + 2, :].rearrange("p s n -> p (s n)").rearrange("p (k n) -> p k n", k=KD)
              for h in range(2)]
        dn = [flat[:, 4096 * h:4096 * h + 4096].rearrange("p (f n) -> p f n", f=2) for h in range(2)]
        hn = flat[:, 8192:8192 + 3 * D].rearrange("p (j d) -> p j d", j=3)
        xe = [flat[:, 8192 + 2048 * i:10240 + 2048 * i].rearrange("p (k t) -> p k t", k=KD) for i in range(2)]
        ys = flat[:, 12288:12288 + D]
        xg = [flat[:, 14336 + 2048 * i:16384 + 2048 * i] for i in range(2)]
        r1 = flat[:, 0:3 * D].rearrange("p (j d) -> p j d", j=3)
        r2 = flat[:, 3 * D:6 * D].rearrange("p (j d) -> p j d", j=3)
        ynat = r1
        tri = flat[:, 18432:18560]
        e64i = flat[:, 18560:18592].bitcast(I32)
        e64 = flat[:, 18592:18624]
        eTi = flat[:, 18624:18656].bitcast(I32)
        eT = tri[:, 0:32]
        wr = flat[:, 18684:18684 + KD * 36].rearrange("p (k e) -> p k e", k=KD)
        brow = flat[0:1, 19260:19260 + 36]
        rt = flat[:, 19296:19296 + 512]
        comb = flat[:, 19808:19808 + 96].rearrange("p (j e) -> p j e", j=3)
        A1, A2, Mk, rk, ge, am = (sq[:, 0, 96 * i:96 * i + 96].rearrange("p (j e) -> p j e", j=3) for i in range(6))
        sg = sq[:, 1, 0:256]
        asb = sq[:, 1, 256:512]
        aTT = sq[:, 0, 0:4 * CAP].rearrange("p (h f t) -> p h f t", h=2, f=2)
        acc = flat[:, 0:KD * T].rearrange("p (k t) -> p k t", k=KD)
        combB = flat[:, 5120:5120 + NE * T]
        combT = flat[0:NE, 15360:15360 + T]
        sgc = flat[:, 15680:15680 + 640]
        act_ = flat[:, 16320:16320 + 640]
        tok_dram = nc.dram_tensor("token_of_slot", [NE * CAP, 1], U32, kind="Internal").ap()
        h2_dram = nc.dram_tensor("moe_input", [T, D], F32, kind="Internal").ap()
        y_dram = nc.dram_tensor("moe_output", [NE * CAP, D], F32, kind="Internal").ap()
        comb_dram = nc.dram_tensor("comb_scratch", [NE, T], F32, kind="Internal").ap()

        b_ada, g_mix, g_ffn = parT[:, 0:96], parT[:, 96:112], parT[:, 112:128]
        p2 = parT[:, P:2 * P]
        conv_w = p2[:, 0:40].rearrange("p (j i) -> p j i", j=4)
        conv_b, ssd_g, lb_raw, hg_g, s5_d, s5_bg = (p2[:, x:y] for x, y in
                                                    ((40, 50), (50, 58), (58, 62), (62, 66), (66, 70), (70, 74)))
        g_fin, lam_re, lam_im = p2[:, 74:90], p2[:, 90:106], p2[:, 106:122]
        p3 = parT[:, 2 * P:3 * P]
        log_dt, ssd_D, x0re, x0im = p3[:, 0:16], p3[:, 32:40], p3[:, 64:80], p3[:, 80:96]

        def seg(i):
            return modT[:, KD * i:KD * (i + 1), :]

        def bc(ap, shape):
            return ap.broadcast_to(shape)

        def turned_at(i):
            return 64 + 4 * (i if i < 16 else i % 4)

        def ring_chunk(item):
            return MIDDLE + CHUNKS.index(item)

        def chunk_groups(n):
            return n + 1 if n < MIDDLE else DONE[n - MIDDLE]

        def in_group(n):
            return GROUP["in", n, 0]

        def ada_group(i):
            return i if i < 16 else GROUP["ada", i]

        all_in = GROUP["in", len(IN_CHUNKS) - 1, 1] + 1

        class Steps:

            def __init__(self, eng, name):
                self.eng, self.name, self.n = eng, name, {}

            def __call__(self, ins, sem=None, wait=True):
                sem = sem or self.name
                ins.then_inc(S(sem), 1)
                self.n[sem] = self.n.get(sem, 0) + 1
                if wait:
                    self.eng.wait_ge(S(sem), self.n[sem])

        def states_stored(eng):
            eng.wait_ge(S("s5_stored"), 16 * 4)
            eng.wait_ge(S("hg_state_stored"), 16 * 2)
            eng.wait_ge(S("cv_saved"), 16 * 2)
            eng.wait_ge(S("ssd_stored"), 16 * 4)

        block = ctx.enter_context(nc.Block())

        @block.sync
        def _(sp):
            w_ada = a["w_ada"][0].rearrange("(k p) n -> p k n", p=P)
            w_in = a["w_in"][0].rearrange("(k p) n -> p k n", p=P)
            w_out = a["w_out"][0].rearrange("(k p) n -> p k n", p=P)

            def dst(s, w=CW):
                return slot[:, s, 0:KD * w].rearrange("p (k n) -> p k n", k=KD)

            for j in range(RING):
                sp.dma_start(dst(j), w_ada[:, :, j * CW:(j + 1) * CW]).then_inc(S(f"w_landed{j}"), 16)
            with sp.Fori(1, 4) as i:
                for j in range(RING):
                    sp.wait_ge(S("bulk_done"), 4 * i + (j - 3))
                    sp.dma_start(dst(j), w_ada[:, :, bass.ds(i * (4 * CW) + j * CW, CW)])\
                      .then_inc(S(f"w_landed{j}"), 16)
            for n in range(MIDDLE, PRE):
                s = n % RING
                sp.wait_ge(S("bulk_done"), chunk_groups(n - RING))
                if n < OUTP and CHUNKS[n - MIDDLE][0] == "in":
                    col = IN_CHUNKS[CHUNKS[n - MIDDLE][1]][0]
                    w = 16 if col == COL_DT else CW
                    sp.dma_start(dst(s, w), w_in[:, :, col:col + w]).then_inc(S(f"w_landed{s}"), 16)
                elif n >= OUTP or CHUNKS[n - MIDDLE][0] == "out":
                    k0, i = (0, n - OUTP) if n >= OUTP else (8, CHUNKS[n - MIDDLE][1])
                    sp.dma_start(slot[:, s, :].rearrange("p (k n) -> p k n", k=8),
                                 w_out[:, k0:k0 + 8, 512 * i:512 * i + 512]).then_inc(S(f"w_landed{s}"), 16)
                else:
                    i = CHUNKS[n - MIDDLE][1]
                    sp.dma_start(dst(s), w_ada[:, :, i * CW:(i + 1) * CW]).then_inc(S(f"w_landed{s}"), 16)
            gate = a["w_exp_gate"][0].rearrange("e (k p) n -> e p k n", p=P)
            up = a["w_exp_up"][0].rearrange("e (k p) n -> e p k n", p=P)
            down = a["w_exp_down"][0].rearrange("e (k p) n -> e p k n", p=P)

            def one(w, e):
                return w[e] if isinstance(e, int) else w[bass.ds(e, 1)].rearrange("e p k n -> (e p) k n")

            def load_gu(h, e):
                sp.dma_start(gu[h][:, :, 0:CW], one(gate, e)).then_inc(S(f"gu_landed{h}"), 16)
                sp.dma_start(gu[h][:, :, CW:2 * CW], one(up, e)).then_inc(S(f"gu_landed{h}"), 16)

            def load_dn(h, e):
                sp.dma_start(dn[h], one(down, e)).then_inc(S(f"dn_landed{h}"), 16)

            sp.wait_ge(S("out_done"), 8)
            load_gu(0, 0)
            sp.wait_ge(S("out_done"), 16)
            load_gu(1, 1)
            load_dn(0, 0)
            sp.wait_ge(S("gu_done"), 1)
            load_gu(0, 2)
            load_dn(1, 1)
            sp.wait_ge(S("gu_done"), 2)
            load_gu(1, 3)
            sp.wait_ge(S("down_done"), 1)
            load_dn(0, 2)
            with sp.Fori(2, NPAIR) as i:
                sp.wait_ge(S("gu_done"), 2 * i - 1)
                load_gu(0, 2 * i)
                sp.wait_ge(S("down_done"), 2 * i - 2)
                load_dn(1, 2 * i - 1)
                sp.wait_ge(S("gu_done"), 2 * i)
                load_gu(1, 2 * i + 1)
                sp.wait_ge(S("down_done"), 2 * i - 1)
                load_dn(0, 2 * i)
            sp.wait_ge(S("down_done"), NE - 2)
            load_dn(1, NE - 1)
            sp.wait_ge(S("routed"), 5)
            with sp.If(sp.value_load(spill[0:1, :], min_val=0, max_val=2 * T) > 0):
                with sp.Fori(1, NE + 1) as e:
                    sp.wait_ge(S("fb_free"), e)
                    for j, (w, d_) in enumerate(((gate, dst(0)), (up, dst(1)),
                                                 (down, slot[:, 2, :].rearrange("p (k n) -> p k n", k=2)))):
                        sp.dma_start(d_, w[bass.ds(e - 1, 1)].rearrange("e p k n -> (e p) k n"))\
                          .then_inc(S("fb_landed"), 16)
            for j in range(2):
                sp.wait_ge(S("y_rows"), 4 * (j + 1))
                sp.dma_start(o["y_prompt"][0, j * P:j * P + P], ynat[:, j, :]).then_inc(S("stores"), 16)
            sp.wait_ge(S("y_rows"), 12)
            sp.dma_start(o["y_sample"][0], ynat[0:TS, 2, :]).then_inc(S("stores"), 16)
            sp.wait_ge(S("stores"), 16 * 3)
            states_stored(sp)

        @block.gpsimd
        def _(pool):
            pl = Steps(pool, "pool_step")
            g = nc.gpsimd
            pl(g.memset(ident[:, :], 0.0))
            pl(g.affine_select(out=ident[:, :], in_=ident[:, :], compare_op=ALU.not_equal, fill=1.0, base=0,
                               pattern=[[-1, P]], channel_multiplier=1))
            pl(g.memset(prow[:, 2, :], 0.0))
            pl(g.tensor_tensor(sel, ident[:, 0:2], ident[:, 32:34], ALU.add))
            pl(g.tensor_tensor(sel, sel, ident[:, 64:66], ALU.add))
            pl(g.tensor_tensor(sel, sel, ident[:, 96:98], ALU.add))
            pl(g.memset(modrow, 0.0))
            pl(g.memset(ones[:, :], 1.0), "consts_a")
            pl(g.memset(rmask[:, :], 1.0))
            pl(g.memset(rmask[:, :].rearrange("p (c t) -> p c t", c=NCH)[:, :, 0:1], 0.0))
            pl(g.memset(lmask[:, :, :], 0.0))
            pl(g.memset(causal[:, :], 1.0))
            for half in range(2):
                lo = CH * half
                rows = slice(lo, lo + CH)
                pl(g.affine_select(out=lmask[rows, 0, :], in_=lmask[rows, 0, :], compare_op=ALU.not_equal,
                                   fill=1.0, base=0, pattern=[[-1, CH]], channel_multiplier=1))
                pl(g.affine_select(out=causal[rows, :], in_=causal[rows, :], compare_op=ALU.is_ge,
                                   fill=0.0, base=0, pattern=[[1, CH]], channel_multiplier=-1))
                for lv, m in enumerate(LEVELS[1:], 1):
                    sub = lmask[rows, lv, :].rearrange("p (b r) -> p b r", r=2 * m)[:, :, m:2 * m]
                    pl(g.memset(sub, 1.0))
                    pl(g.affine_select(out=sub, in_=sub, compare_op=ALU.is_ge, fill=0.0, base=0,
                                       pattern=[[-2 * m, CH // (2 * m)], [0, m]], channel_multiplier=1))
                    pl(g.affine_select(out=sub, in_=sub, compare_op=ALU.is_ge, fill=0.0, base=m - 1,
                                       pattern=[[2 * m, CH // (2 * m)], [0, m]], channel_multiplier=-1))
            par = small[:, 4:8]
            pl(g.memset(par, 1.0))
            pl(g.affine_select(out=par, in_=par, compare_op=ALU.is_ge, fill=0.0, base=-16,
                               pattern=[[-32, 4]], channel_multiplier=1))
            pl(g.affine_select(out=par, in_=par, compare_op=ALU.is_ge, fill=0.0, base=31,
                               pattern=[[32, 4]], channel_multiplier=-1))
            pl(g.tensor_tensor(small[:, 8:9], small[:, 4:5], small[:, 5:6], ALU.add))
            pl(g.tensor_tensor(small[:, 9:10], small[:, 6:7], small[:, 7:8], ALU.add))
            pl(g.tensor_tensor(small[:, 1:2], small[:, 8:9], small[:, 9:10], ALU.add))
            pl(g.tensor_scalar(small[:, 0:1], small[:, 1:2], -1.0, 1.0, ALU.mult, ALU.add))
            for j in range(8):
                pl(g.memset(small[:, 16 + j:17 + j], float(j - 99)))
            pl(g.memset(bdp, 0.0), "consts_b")
            pool.wait_ge(S("setup_act"), 5)
            pool.wait_ge(S("x_transposed"), 12)
            pool.dma_start(wglu, a["s5_w_glu"][0].rearrange("(k p) m -> p k m", p=P)).then_inc(S("wglu_loaded"), 16)
            for b in range(8):
                if b >= 2:
                    pool.wait_ge(S("s5_turned"), b - 1)
                pc, ps = (s5b[5 + 2 * (b % 2) + i].rearrange("p (i t) -> p i t", i=2) for i in range(2))
                tt, t2 = (sq[:, 0, 320 * i:320 * i + 256].rearrange("p (i t) -> p i t", i=2) for i in range(2))
                if b == 0:
                    pool.wait_ge(S("squares_used"), 8)
                cs = sm[:, 0, 2 * b:2 * b + 2].unsqueeze(2)
                sn = sm[:, 1, 2 * b:2 * b + 2].unsqueeze(2)
                pl(g.tensor_copy(pc[:, :, 0:1], cs))
                pl(g.tensor_copy(ps[:, :, 0:1], sn))
                m = 1
                while m < TP:
                    cm, sn_ = (bc(t[:, :, m - 1:m], [P, 2, m]) for t in (pc, ps))
                    pl(g.tensor_tensor(tt[:, :, 0:m], pc[:, :, 0:m], cm, ALU.mult))
                    pl(g.tensor_tensor(t2[:, :, 0:m], ps[:, :, 0:m], sn_, ALU.mult))
                    pl(g.tensor_tensor(pc[:, :, m:2 * m], tt[:, :, 0:m], t2[:, :, 0:m], ALU.subtract))
                    pl(g.tensor_tensor(tt[:, :, 0:m], pc[:, :, 0:m], sn_, ALU.mult))
                    pl(g.tensor_tensor(t2[:, :, 0:m], ps[:, :, 0:m], cm, ALU.mult))
                    pl(g.tensor_tensor(ps[:, :, m:2 * m], tt[:, :, 0:m], t2[:, :, 0:m], ALU.add))
                    m *= 2
                pl(g.tensor_copy(pc[:, :, TP:T], pc[:, :, 0:TS]))
                pl(g.tensor_copy(ps[:, :, TP:T], ps[:, :, 0:TS]), "s5_table")
            pool.wait_ge(S("s5_fin_rows"), 1)
            for w, name in enumerate(("s5re_p", "s5im_p", "s5re_s", "s5im_s")):
                pool.dma_start(o[name][0, 0].rearrange("(i g) q -> i (g q)", g=2), sq[0:16, 1, w * P:(w + 1) * P])\
                    .then_inc(S("s5_stored"), 16)
            pool.wait_ge(S("glu_used"), 4)
            pool.dma_start(hS[:, 4, :, :], a["state_hgrn"][0, 0].rearrange("h k v -> k h v"))\
                .then_inc(S("hg_in_loaded"), 16)
            pool.wait_ge(S("hg_S"), 2 * NCH)
            for sl, name in ((3, "hgrn_p"), (5, "hgrn_s")):
                pool.dma_start(o[name][0, 0].rearrange("h k v -> k h v"), hS[:, sl, :, :])\
                    .then_inc(S("hg_state_stored"), 16)
            pool.wait_ge(S("hg_normed"), 4)
            for g_ in range(2):
                pool.dma_start(aS[64 * g_:64 * g_ + 64, 4, :].rearrange("k (j v) -> k j v", j=8),
                               a["state_ssd"][0, 0, 8 * g_:8 * g_ + 8].rearrange("j k v -> k j v"))\
                    .then_inc(S("ssd_in_loaded"), 16)
            def add_pieces(pieces):
                for item in pieces:
                    m = 4 * item[1] + item[2]
                    pool.wait_ge(S("bulk_evac"), GROUP[item] + 1)
                    g.tensor_tensor(xT[:, m, :], xT[:, m, :], sq[:, OUT_PIECES.index(item) % 2, 0:T], ALU.add)\
                        .then_inc(S("x_part"), 1)

            early = [item for item in OUT_PIECES if PLAN.index(item) < PLAN.index(("ssd_gamma", 0))]
            add_pieces(early)
            pool.wait_ge(S("cv_stored"), 1)
            for s_, name in ((0, "conv_p"), (3, "conv_s")):
                pool.dma_start(o[name][0, 0], cvst[s_:s_ + 3, :]).then_inc(S("cv_saved"), 16)
            pool.dma_start(wr[:, :, 0:4], a["w_router_group"][0].rearrange("(k p) e -> p k e", p=P))\
                .then_inc(S("router_loaded"), 16)
            pool.dma_start(wr[:, :, 4:36], a["w_router_expert"][0].rearrange("(k p) e -> p k e", p=P))\
                .then_inc(S("router_loaded"), 16)
            pool.dma_start(brow[:, 0:4], a["b_router_group"]).then_inc(S("router_loaded"), 16)
            pool.dma_start(brow[:, 4:36], a["b_router_expert"]).then_inc(S("router_loaded"), 16)
            add_pieces(OUT_PIECES[len(early):])
            pool.wait_ge(S("ssd_done"), NCH)
            pl(g.memset(tri, 1.0))
            pl(g.affine_select(out=tri, in_=tri, compare_op=ALU.is_ge, fill=0.0, base=-1, pattern=[[1, P]],
                               channel_multiplier=-1))
            pl(g.iota(e64i, pattern=[[CAP, NE]], base=0, channel_multiplier=0))
            pl(g.iota(eTi, pattern=[[1, NPAIR], [CAP * NPAIR, 2]], base=0, channel_multiplier=0))
            pl(g.iota(tokid, pattern=[[P, 3]], base=0, channel_multiplier=1))
            pl(g.memset(slot_tok, 0), "slot_consts")
            pool.dma_start(tok_dram.rearrange("(p i) u -> p (i u)", p=P), slot_tok).then_inc(S("tokens_moved"), 16)
            pool.wait_ge(S("tokens_moved"), 16)
            pool.wait_ge(S("ssd_S"), NCH)
            for sl, name in ((3, "ssd_p"), (5, "ssd_s")):
                for g_ in range(2):
                    pool.dma_start(o[name][0, 0, 8 * g_:8 * g_ + 8].rearrange("j k v -> k j v"),
                                   aS[64 * g_:64 * g_ + 64, sl, :].rearrange("k (j v) -> k j v", j=8))\
                        .then_inc(S("ssd_stored"), 16)
            pool.wait_ge(S("routed"), 3)
            for c in range(2):
                for j in range(3):
                    n = P if j < 2 else TS
                    pool.indirect_dma_start(tok_dram, bass.IndirectOffsetOnAxis(ap=pos_scatter[0:n, 3 * c + j:3 * c + j + 1], axis=0),
                                            tokid[0:n, j:j + 1], None, bounds_check=NE * CAP - 1, oob_is_err=False)\
                        .then_inc(S("tokens_moved"), 16)
            pool.wait_ge(S("tokens_moved"), 16 * 7)
            pool.dma_start(slot_tok, tok_dram.rearrange("(p i) u -> p (i u)", p=P)).then_inc(S("tokens_moved"), 16)
            pool.wait_ge(S("tokens_moved"), 16 * 8)
            pool.wait_ge(S("h2_stored"), 32)
            states_stored(pool)
            for i in range(NPAIR):
                if i >= 2:
                    pool.wait_ge(S("xe_turned"), 4 * (i - 1))
                pool.indirect_dma_start(xg[i % 2], None, h2_dram, bass.IndirectOffsetOnAxis(ap=slot_tok[:, i:i + 1], axis=0))\
                    .then_inc(S(f"xg_landed{i % 2}"), 16)
            pool.wait_ge(S("y_stored0"), 16 * NPAIR)
            pool.wait_ge(S("y_stored1"), 16 * NPAIR)
            pool.wait_ge(S("down_done"), NE)
            for j in range(3):
                n = P if j < 2 else TS
                for c, r_ in ((0, r1), (1, r2)):
                    pool.indirect_dma_start(r_[0:n, j, :], None, y_dram,
                                            bass.IndirectOffsetOnAxis(ap=pos_gather[0:n, 3 * c + j:3 * c + j + 1], axis=0))\
                        .then_inc(S(f"rows_landed{j}"), 16)

        @block.scalar
        def _(act):
            s = nc.scalar
            st = Steps(act, "act_step")

            def load(dst, src, sem):
                act.dma_start(dst, src).then_inc(S(sem), 16)

            load(crow[0:1, :], a["c_prompt"], "c_loaded")
            load(crow[1:2, :], a["c_sample"], "c_loaded")
            act.wait_ge(S("c_loaded"), 32)
            st(s.activation(crow, crow, ACT.Silu), "setup_act")
            load(xnat[:, 0:2, :], a["x_prompt"][0].rearrange("(j p) d -> p j d", p=P), "x_loaded")
            load(xnat[0:TS, 2, :], a["x_sample"][0], "x_loaded")
            r = lambda ap: ap.rearrange("(n q) -> n q", q=P)
            load(prow[0:96, 0, :], r(a["b_ada"][0]), "par_loaded")
            load(prow[96:112, 0, :], r(a["g_mix"][0]), "par_loaded")
            load(prow[112:128, 0, :], r(a["g_ffn"][0]), "par_loaded")
            load(prow[0:40, 1, :], a["conv_w"][0].rearrange("j (n q) -> (j n) q", q=P), "par_loaded")
            for lo, hi, name in ((40, 50, "conv_b"), (50, 58, "ssd_norm_g"), (58, 62, "hgrn_lb_raw"),
                                 (66, 70, "s5_d"), (70, 74, "s5_b_glu")):
                load(prow[lo:hi, 1, :], r(a[name][0]), "par_loaded")
            load(prow[62:66, 1, :], a["hgrn_norm_g"][0], "par_loaded")
            load(prow[74:90, 1, :], r(a["g_final"]), "par_loaded")
            two = lambda ap: ap.rearrange("(i g) q -> i (g q)", g=2)
            load(prow[90:106, 1, :], two(a["s5_lam_re"][0]), "par_loaded")
            load(prow[106:122, 1, :], two(a["s5_lam_im"][0]), "par_loaded")
            load(ldrow[0:16, :], a["s5_log_dt"][0].rearrange("(i g) -> i g", g=2), "ld_loaded")
            load(ldrow[32:40, :], a["ssd_d"][0].rearrange("(i g) -> i g", g=2), "ld_loaded")
            act.wait_ge(S("consts_a"), 1)
            load(prow[64:80, 2, :], two(a["state_s5_re"][0, 0]), "par_loaded")
            load(prow[80:96, 2, :], two(a["state_s5_im"][0, 0]), "par_loaded")
            gp = lambda ap: ap.rearrange("(i g) q j -> (g q) i j", g=2)
            load(BR, gp(a["s5_b_re"][0]), "s5_loaded")
            load(BI, gp(a["s5_b_im"][0]), "s5_loaded")
            load(CR[:, 0], a["s5_c_re"][0].rearrange("(u g) j q -> (g j) u q", u=4), "s5_loaded")
            load(CR[:, 1], a["s5_c_im"][0].rearrange("(u g) j q -> (g j) u q", u=4), "s5_loaded")
            load(cvrow, a["state_conv"][0, 0], "cv_loaded")
            load(small[0:NH, 32:33], a["ssd_dt_bias"][0].rearrange("(h u) -> h u", u=1), "hd_loaded")
            load(small[0:NH, 33:34], a["ssd_a_log"][0].rearrange("(h u) -> h u", u=1), "hd_loaded")

            def squares(src, i, tag):
                if i >= 2:
                    act.wait_ge(S("squares_used"), NORM[tag] + i - 1)
                st(s.activation(sq[:, i % 2, :].rearrange("p (k t) -> p k t", k=2), src, ACT.Square), "squares")

            def take_rows(j, b):
                for c in range(4):
                    last = s.activation(modrow[32 * c:32 * c + 2, j, :], psum[32 * c:32 * c + 2, b, 0:CW], ACT.Copy)
                last.then_inc(S("bulk_evac"), 1)

            def ada_evac(n):
                act.wait_ge(S("bulk_done"), ada_group(n) + 1)
                if n >= 2:
                    act.wait_ge(S("mod_turned"), n - 1)
                take_rows(n % 2, ada_group(n) % 2)

            for step in START:
                if isinstance(step, int):
                    ada_evac(step)
                elif step == "s5":
                    act.wait_ge(S("setup_taken"), 3)
                    st(s.activation(sm[:, 2, :], log_dt, ACT.Exp), "setup_act")
                    act.wait_ge(S("setup_dve"), 1)
                    st(s.activation(sm[:, 4, :], sm[:, 3, :], ACT.Exp), "setup_act")
                    act.wait_ge(S("hd_loaded"), 32)
                    st(s.activation(small[0:NH, 34:35], small[0:NH, 33:34], ACT.Exp), "setup_act")
                    act.wait_ge(S("setup_dve"), 2)
                    st(s.activation(sm[:, 0, :], sm[:, 7, :], ACT.Sin))
                    st(s.activation(sm[:, 1, :], sm[:, 6, :], ACT.Sin), "setup_act")
                elif step == "norm":
                    for i in range(8):
                        act.wait_ge(S("x_transposed"), 12)
                        squares(xT[:, 2 * i:2 * i + 2, :], i, "n1")
                    act.wait_ge(S("mean_square"), 1)
                    st(s.activation(rinv[:, :], rinv[:, :], ACT.Sqrt), "root")

            for k in range(KD):
                act.wait_ge(S("h_scaled"), k // 4 + 1)
                s.activation(hT[:, k, 0:TP], hT[:, k, 0:TP], ACT.Identity, bias=seg(0)[:, k, 0:1],
                             scale=ab1[:, k, 0:1]).then_inc(S("h_prompt"), 1)

            def evac_in(n, q):
                tile, grp = IN_CHUNKS[n][1], GROUP["in", n, q]
                act.wait_ge(S("bulk_done"), grp + 1)
                src = psum[:, grp % 2, 0:T]
                if tile is None:
                    s.activation(dt_raw, psum[0:NH, grp % 2, 0:T], ACT.Copy).then_inc(S("bulk_evac"), 1)
                elif tile >= 100:
                    i = tile - 100 + q
                    st(s.activation(xbcp[:, i, PADP:PADP + TP], src[:, 0:TP], ACT.Copy))
                    s.activation(xbcp[:, i, PADS:PADS + TS], src[:, TP:T], ACT.Copy).then_inc(S("bulk_evac"), 1)
                else:
                    s.activation(proj[:, tile + q, :], src, ACT.Copy).then_inc(S("bulk_evac"), 1)

            def s5_in(b):
                act.wait_ge(S("s5_bu"), b + 1)
                if b:
                    act.wait_ge(S("s5_turned"), b)
                    act.wait_ge(S("s5_y"), b)
                for w in range(2):
                    src = psum[:, 4 + 2 * w:6 + 2 * w, 0:T]
                    st(s.activation(s5b[w].rearrange("p (i t) -> p i t", i=2), src, ACT.Copy), "s5_bu_sb")

            def s5_out(b):
                if b % 2:
                    act.wait_ge(S("s5_gelu_arg"), b // 2 + 1)
                    st(s.activation(sq[:, 1, 0:T], sq[:, 1, 0:T], ACT.Sigmoid), "s5_gelu_sig")

            def s5_glu():
                for m in range(4):
                    act.wait_ge(S("glu_mm"), m + 1)
                    if m >= 1:
                        act.wait_ge(S("glu_used"), m)
                    st(s.activation(rinv[:, :], psum[:, 4 + m, 0:T], ACT.Sigmoid, bias=s5_bg[:, m:m + 1]), "glu_sig")

            def hg_prep(hp):
                hf = flat[:, (HF + 2 * hp) * T:(HF + 2 * hp + 2) * T]
                if hp == 0:
                    act.wait_ge(S("glu_used"), 4)
                act.wait_ge(S("bulk_evac"), GROUP["in", AFTER_HG - 1, 1] + 1)
                if hp:
                    act.wait_ge(S("hg_kd_turned"), 2 * hp)
                    act.wait_ge(S("hg_kdn"), hp)
                st(s.activation(hE, hf, ACT.Sigmoid))
                st(s.activation(hf, hf, ACT.Sigmoid, scale=-1.0), "hg_sig")
                act.wait_ge(S("hg_f"), hp + 1)
                st(s.activation(hE, hE, ACT.Ln), "hg_ln")

            def hg_level(hp, lv):
                if lv:
                    act.wait_ge(S("hg_expo"), 6 * hp + lv)
                    st(s.activation(hE, hE, ACT.Exp), "hg_exp")

            def hg_kd(hp):
                act.wait_ge(S("hg_expo2"), 2 * hp + 1)
                st(s.activation(hE, hb, ACT.Exp), "hg_exp2")
                act.wait_ge(S("hg_expo2"), 2 * hp + 2)
                st(s.activation(hE, hE, ACT.Exp), "hg_exp2")

            def hg_out(hp):
                gate = flat[:, (HG + 2 * hp) * T:(HG + 2 * hp + 2) * T]
                st(s.activation(gate, gate, ACT.Silu), "hg_gate")
                for h in range(2):
                    act.wait_ge(S("hg_o"), 2 * hp + 2)
                    st(s.activation(sq[:, 0, h * T:h * T + T], psum[:, 4 + h, 0:T], ACT.Square), "hg_sq")
                for h in range(2):
                    act.wait_ge(S("hg_var"), 2 * hp + h + 1)
                    st(s.activation(rinv[:, :], rinv[:, :], ACT.Sqrt), "hg_root")

            def ssd_dt():
                act.wait_ge(S("dt_arg"), 1)
                st(s.activation(dtw[:, 1, :], dtw[:, 0, :], ACT.Exp), "dt_func")
                act.wait_ge(S("dt_arg"), 2)
                st(s.activation(dtw[:, 3, :], dtw[:, 2, :], ACT.Ln), "dt_func")

            def conv_silu(i):
                act.wait_ge(S("conv_out"), i + 1)
                for n in (2 * i, 2 * i + 1):
                    st(s.activation(xbcT[:, n, :], xbcT[:, n, :], ACT.Silu), "conv_silu")

            def ssd_conv(i):
                if i:
                    conv_silu(i - 1)
                else:
                    st(s.activation(flat[:, 0:8 * T], flat[:, 0:8 * T], ACT.Silu), "z_silu")

            def out_evac(n, q):
                i = OUT_PIECES.index(("out", n, q))
                act.wait_ge(S("bulk_done"), GROUP["out", n, q] + 1)
                if i == 0:
                    act.wait_ge(S("mod_ready"), 24)
                    act.wait_ge(S("s5_stored"), 64)
                else:
                    if i >= 2:
                        act.wait_ge(S("x_part"), i - 1)
                for s_, (lo, hi) in enumerate(STREAMS):
                    last = s.activation(sq[:, i % 2, lo:hi], psum[:, GROUP["out", n, q] % 2, lo:hi], ACT.Identity,
                                        scale=seg(2)[:, 4 * n + q, s_:s_ + 1])
                last.then_inc(S("bulk_evac"), 1)

            def ssd_decay(c):
                half = slice(CH * (c % 2), CH * (c % 2) + CH)
                act.wait_ge(S("ssd_diff"), 2 * c + 1)
                st(s.activation(small[half, 64:80], small[half, 64:80], ACT.Exp), "ssd_exp")
                for g in range(2):
                    rows = slice(64 * g, 64 * g + 64)
                    st(s.activation(EB[rows, :], psum[rows, 4 + g, :], ACT.Exp), "ssd_EB")
                act.wait_ge(S("ssd_diff"), 2 * c + 2)
                st(s.activation(W[half, :], W[half, :], ACT.Exp), "ssd_exp")

            def ssd_norm():
                act.wait_ge(S("ssd_done"), NCH)
                act.wait_ge(S("x_part"), 16)
                for i in range(4):
                    squares(proj[:, 2 * i:2 * i + 2, :], i, "ssd")
                act.wait_ge(S("mean_square"), 2)
                st(s.activation(rinv[:, :], rinv[:, :], ACT.Sqrt), "root")

            order, late = [], []
            for item in PLAN:
                if item[0] in ("in", "ada"):
                    late.append(item)
                elif item[0] in ("hg_level", "hg_kd"):
                    order += [item] + late
                    late = []
                else:
                    order += late + [item]
                    late = []
            for item in order:
                kind = item[0]
                if kind == "in":
                    evac_in(item[1], item[2])
                elif kind == "ada":
                    ada_evac(item[1])
                elif kind == "out":
                    out_evac(item[1], item[2])
                elif kind == "s5_in":
                    s5_in(item[1])
                elif kind == "s5_out":
                    s5_out(item[1])
                elif kind == "s5_glu":
                    s5_glu()
                elif kind == "hg_prep":
                    hg_prep(item[1])
                elif kind == "hg_level":
                    hg_level(item[1], item[2])
                elif kind == "hg_kd":
                    hg_kd(item[1])
                elif kind == "hg_out":
                    hg_out(item[1])
                elif kind == "ssd_dt":
                    ssd_dt()
                elif kind == "ssd_conv":
                    ssd_conv(item[1])
                elif kind == "ssd_gamma":
                    conv_silu(NXBC // 2 - 1)
                elif kind == "ssd_decay":
                    ssd_decay(item[1])
                elif kind == "ssd_norm":
                    ssd_norm()

            for i in range(8):
                act.wait_ge(S("x_mixed"), 4 * (i + 1))
                squares(xT[:, 2 * i:2 * i + 2, :], i, "n2")
            act.wait_ge(S("mean_square"), 3)
            st(s.activation(rinv[:, :], rinv[:, :], ACT.Sqrt), "root")
            for k in range(KD):
                act.wait_ge(S("h_scaled"), 4 + k // 4 + 1)
                s.activation(hT[:, k, 0:TP], hT[:, k, 0:TP], ACT.Identity, bias=seg(3)[:, k, 0:1],
                             scale=ab1[:, k, 0:1]).then_inc(S("h_prompt"), 1)
            act.wait_ge(S("rt_expo"), 1)
            st(s.activation(rt[:, 16:28], rt[:, 16:28], ACT.Exp))
            st(s.activation(rt[:, 240:243], rt[:, 240:243], ACT.Exp), "rt_exp")
            for g_ in range(12):
                j, kg = g_ // 4, g_ % 4
                n = P if j < 2 else TS
                act.wait_ge(S("hn_turned"), g_ + 1)
                s.activation(hn[0:n, j, 512 * kg:512 * kg + 512], bank(4 + g_ % 4, 512, n), ACT.Copy)\
                 .then_inc(S("act_rows"), 1)
            act.wait_ge(S("act_rows"), 12)
            act.dma_start(h2_dram[0:TP].rearrange("(j p) d -> p j d", p=P), hn[:, 0:2, :]).then_inc(S("h2_stored"), 16)
            act.dma_start(h2_dram[TP:T], hn[0:TS, 2, :]).then_inc(S("h2_stored"), 16)

            def silu_gate(h, e):
                rows_ = slice(CAP * h, CAP * h + CAP)
                act.wait_ge(S("gu_done"), e + 1)
                if not (isinstance(e, int) and e < 2):
                    act.wait_ge(S("act_ready"), e - 1)
                s.activation(sg[rows_, :], psum[rows_, 0, 0:CW], ACT.Silu).then_inc(S("gate_silu"), 1)

            def store_y(h, e):
                act.wait_ge(S("y_rows_sb"), e + 1)
                where = y_dram[e * CAP:(e + 1) * CAP] if isinstance(e, int) else y_dram[bass.ds(e * CAP, CAP)]
                act.dma_start(where, ys[CAP * h:CAP * h + CAP, :]).then_inc(S(f"y_stored{h}"), 16)

            silu_gate(0, 0)
            silu_gate(1, 1)
            store_y(0, 0)
            with act.Fori(1, NPAIR) as i:
                silu_gate(0, 2 * i)
                store_y(1, 2 * i - 1)
                silu_gate(1, 2 * i + 1)
                store_y(0, 2 * i)
            store_y(1, NE - 1)
            act.wait_ge(S("routed"), 5)
            for j in range(3):
                n = P if j < 2 else TS
                act.wait_ge(S(f"rows_landed{j}"), 32)
                s.activation(r1[0:n, j, :], r1[0:n, j, :], ACT.Copy, scale=rt[0:n, 506 + j:507 + j])\
                 .then_inc(S("act_rows"), 1)
            act.wait_ge(S("routed"), 5)
            with act.If(act.value_load(spill[0:1, :], min_val=0, max_val=2 * T) > 0):
                act.wait_ge(S("fb_dve"), 2)
                act.dma_start(comb_dram, combT).then_inc(S("fb_rows"), 16)
                act.wait_ge(S("fb_rows"), 16)
                act.dma_start(combB, comb_dram.rearrange("e t -> (e t)").unsqueeze(0).broadcast_to([P, NE * T]))\
                   .then_inc(S("fb_rows"), 16)
                with act.Fori(1, NE + 1) as e:
                    act.wait_ge(S("fb_hidden"), e)
                    s.activation(sgc.rearrange("p (f t) -> p f t", f=2), psum[:, 0:2, 0:T], ACT.Silu)\
                     .then_inc(S("fb_silu"), 1)
            for i in range(8):
                act.wait_ge(S("x_final"), 1)
                squares(xT[:, 2 * i:2 * i + 2, :], i, "n3")
            act.wait_ge(S("mean_square"), 4)
            st(s.activation(rinv[:, :], rinv[:, :], ACT.Sqrt), "root")

        @block.tensor
        def _(pe):
            mm, tr = nc.tensor.matmul, nc.tensor.transpose
            pe.wait_ge(S("consts_a"), 1)
            pe.wait_ge(S("setup_act"), 1)
            for k in range(KD):
                last = tr(bank(3, 2, lo=384 + 2 * k), crow[:, k * P:(k + 1) * P], ident[0:2, 0:2])
            last.then_inc(S("setup_turned"), 1)
            pe.wait_ge(S("setup_taken"), 1)
            def sum_squares(b, count, tag):
                for i in range(count):
                    pe.wait_ge(S("squares"), NORM[tag] + i + 1)
                    for q in range(2):
                        last = mm(bank(b, T), ones[:, :], sq[:, i % 2, q * T:q * T + T],
                                  start=(i == 0 and q == 0), stop=(i == count - 1 and q == 1))
                    last.then_inc(S("squares_used"), 1)

            def ada_mm(s_, b):
                w = slot[:, s_, :].rearrange("p (k n) -> p k n", k=KD)
                for k in range(KD):
                    c = k % 4
                    last = mm(psum[32 * c:32 * c + 2, b, 0:CW], cT[:, k, :], w[:, k, :], start=(k < 4), stop=(k >= KD - 4))
                last.then_inc(S("bulk_done"), 1)

            def ada_turn(j):
                for q in range(2):
                    last = mm(bank(2, 2, lo=turned_at(j) + 2 * q), modrow[:, j % 2, q * P:(q + 1) * P],
                              sel, start=True, stop=True)
                last.then_inc(S("mod_turned"), 1)

            for step in START:
                if isinstance(step, int):
                    j = step
                    pe.wait_ge(S(f"w_landed{j % RING}"), 16 * (j // RING + 1))
                    if j >= 2:
                        pe.wait_ge(S("bulk_evac"), j - 1)
                    ada_mm(j % RING, j % 2)
                    if j >= 1:
                        pe.wait_ge(S("bulk_evac"), j)
                        ada_turn(j - 1)
                elif step == "x":
                    pe.wait_ge(S("x_loaded"), 32)
                    for g in range(12):
                        j, kg = g // 4, g % 4
                        n = P if j < 2 else TS
                        if g >= 4:
                            pe.wait_ge(S("x_transposed"), g - 3)
                        for q in range(4):
                            k = 4 * kg + q
                            last = tr(bank(4 + g % 4, n, lo=q * n), xnat[0:n, j, k * P:(k + 1) * P], ident[0:n, 0:n])
                        last.then_inc(S("x_turned"), 1)
                elif step == "parameters":
                    pe.wait_ge(S("setup_taken"), 2)
                    pe.wait_ge(S("par_loaded"), 16 * 15)
                    tr(bank(3, P, lo=0), prow[:, 0, :], ident[:, :])
                    tr(bank(3, 122, lo=P), prow[0:122, 1, :], ident[0:122, 0:122])
                    tr(bank(3, 96, lo=2 * P), prow[0:96, 2, :], ident[0:96, 0:96]).then_inc(S("setup_turned"), 1)
                elif step == "s5":
                    pe.wait_ge(S("cv_loaded"), 16)
                    pe.wait_ge(S("setup_taken"), 3)
                    for i in range(NXBC):
                        last = tr(bank(3, 3, lo=416 + 4 * i), cvrow[:, i * P:(i + 1) * P], ident[0:3, 0:3])
                    last.then_inc(S("setup_turned"), 1)
                elif step == "norm":
                    pe.wait_ge(S("setup_taken"), 4)
                    sum_squares(3, 8, "n1")
                elif step == "s5_matrices":
                    pe.wait_ge(S("s5_mats"), 1)
                    for w in range(2):
                        for u in range(4):
                            tr(bank(4 + w, P, lo=u * P),
                               bdp[:, w, 4 * u:4 * u + 4].rearrange("p i g j -> p (i g j)"), ident[:, :])
                            last = tr(bank(6 + w, P, lo=u * P), cpad[:, w, u].rearrange("p g q -> p (g q)"), ident[:, :])
                    last.then_inc(S("setup_turned"), 1)
            pe.wait_ge(S("bulk_evac"), 16)
            ada_turn(15)

            def in_mm(n, q):
                tile = IN_CHUNKS[n][1]
                r = ring_chunk(("in", n))
                pe.wait_ge(S(f"w_landed{r % RING}"), 16 * (r // RING + 1))
                wd = NH if tile is None else P
                w = slot[:, r % RING, 0:KD * (NH if tile is None else CW)].rearrange("p (k n) -> p k n", k=KD)
                grp = GROUP["in", n, q]
                pe.wait_ge(S("bulk_evac"), grp - 1)
                for k in range(KD):
                    if n == 0 and q == 0:
                        pe.wait_ge(S("h_prompt"), k + 1)
                        pe.wait_ge(S("h_sample"), k + 1)
                    last = mm(psum[0:wd, grp % 2, 0:T], w[:, k, q * P:q * P + wd], hT[:, k, :],
                              start=(k == 0), stop=(k == KD - 1))
                last.then_inc(S("bulk_done"), 1)

            def ada(i):
                r = ring_chunk(("ada", i))
                grp = ada_group(i)
                pe.wait_ge(S(f"w_landed{r % RING}"), 16 * (r // RING + 1))
                pe.wait_ge(S("bulk_evac"), grp - 1)
                ada_mm(r % RING, grp % 2)
                if i > 16:
                    pe.wait_ge(S("bulk_evac"), ada_group(i - 1) + 1)
                    if (i - 1) % 4 == 0:
                        pe.wait_ge(S("mod_ready"), i - 1)
                    ada_turn(i - 1)

            mixed = [proj[:, Z + i, :] for i in range(8)] + [proj[:, HG + i, :] for i in range(4)] \
                + [proj[:, U + i, :] for i in range(4)]

            def out_piece(n, q):
                r, grp = ring_chunk(("out", n)), GROUP["out", n, q]
                if n == 0 and q == 0:
                    pe.wait_ge(S("hg_normed"), 4)
                pe.wait_ge(S(f"w_landed{r % RING}"), 16 * (r // RING + 1))
                pe.wait_ge(S("bulk_evac"), grp - 1)
                w = slot[:, r % RING, :].rearrange("p (k n) -> p k n", k=8)
                for k in range(8):
                    last = mm(bank(grp % 2, T), w[:, k, q * P:(q + 1) * P], mixed[8 + k], start=(k == 0), stop=(k == 7))
                last.then_inc(S("bulk_done"), 1)

            def s5_in(b):
                if b == 0:
                    pe.wait_ge(S("bulk_evac"), in_group(2))
                    pe.wait_ge(S("s5_mats_ready"), 1)
                if b:
                    pe.wait_ge(S("s5_bu_sb"), 2 * b)
                u = b // 2
                for i in range(2):
                    rows = slice(32 * (2 * (b % 2) + i), 32 * (2 * (b % 2) + i) + 32)
                    for w in range(2):
                        last = mm(psum[:, 4 + 2 * w + i, 0:T], BDT[rows, w, u, :], proj[rows, U + u, :],
                                  start=True, stop=True)
                last.then_inc(S("s5_bu"), 1)

            def s5_out(b):
                pe.wait_ge(S("s5_turned"), b + 1)
                if b % 2 == 0 and b:
                    pe.wait_ge(S("s5_g"), b // 2)
                u = b // 2
                for i in range(2):
                    c0 = 32 * (2 * (b % 2) + i)
                    for w in range(2):
                        last = mm(psum[c0:c0 + 32, 3, 0:T], CT[:, w, u, c0:c0 + 32],
                                  s5b[2 + w][:, i * T:i * T + T], start=(w == 0), stop=(w == 1))
                last.then_inc(S("s5_y"), 1)

            def s5_glu():
                pe.wait_ge(S("s5_g"), 4)
                pe.wait_ge(S("wglu_loaded"), 16)
                pe.wait_ge(S("s5_bu_sb"), 16)
                for m in range(4):
                    for k in range(4):
                        last = mm(bank(4 + m, T), wglu[:, k, m * P:(m + 1) * P], proj[:, U + k, :],
                                  start=(k == 0), stop=(k == 3))
                    last.then_inc(S("glu_mm"), 1)
                for w in range(4):
                    last = tr(bank(3, P, 16, lo=w * P), s5fin[:, w, :], ident[:, :])
                last.then_inc(S("s5_fin_turned"), 1)

            def hg_prep(hp):
                if hp == 0:
                    pe.wait_ge(S("bulk_evac"), GROUP["in", AFTER_HG - 1, 1] + 1)
                    pe.wait_ge(S("glu_used"), 4)
                else:
                    pe.wait_ge(S("hg_normed"), 2)
                for h in range(2):
                    src = proj[:, HI + 2 * hp + h, :]
                    for q in range(3):
                        n = P if q < 2 else TS
                        last = tr(bank(6 + h, P, n, lo=q * P), src[:, q * P:q * P + n], ident[:, :])
                last.then_inc(S("hg_v"), 1)

            def hg_level(hp, lv):
                it = 7 * hp + lv
                if lv == 0:
                    pe.wait_ge(S("hg_k"), hp + 1)
                    q_, k_ = (flat[:, (x + 2 * hp) * T:(x + 2 * hp + 2) * T] for x in (HQ, HF))
                else:
                    pe.wait_ge(S("hg_qk"), 6 * hp + lv)
                    q_, k_ = hq_, hk_
                if it >= 2:
                    pe.wait_ge(S("hg_sc_used"), it - 1)
                for h in range(2):
                    for c in range(6):
                        cc = min(c, NCH - 1)
                        col = h * T + cc * CH
                        last = mm(psum[CH * (c % 2):CH * (c % 2) + CH, 4 + it % 2,
                                       (h * 3 + c // 2) * CH:(h * 3 + c // 2) * CH + CH],
                                  k_[:, col:col + CH], q_[:, col:col + CH], start=True, stop=True)
                last.then_inc(S("hg_sc"), 1)

            def hg_kd(hp):
                pe.wait_ge(S("hg_kd"), hp + 1)
                pe.wait_ge(S("hg_vn"), hp + 1)
                for h in range(2):
                    for q in range(3):
                        n = P if q < 2 else TS
                        last = tr(bank(6 + h, P, n, lo=q * P), hE[:, h * T + q * P:h * T + q * P + n], ident[:, :])
                    last.then_inc(S("hg_kd_turned"), 1)

            def hg_state(hp):
                pe.wait_ge(S("hg_kdn"), hp + 1)
                for c in range(NCH):
                    half = slice(CH * (c % 2), CH * (c % 2) + CH)
                    if c >= 2:
                        pe.wait_ge(S("hg_S"), NCH * hp + c - 1)
                    for h in range(2):
                        last = mm(bank(6 + c % 2, P, lo=h * P), kdn[half, h, c // 2, :], vn[half, h, c // 2, :],
                                  start=True, stop=True)
                    last.then_inc(S("hg_dS"), 1)

            def hg_out(hp):
                pe.wait_ge(S("hg_S"), NCH * (hp + 1))
                pe.wait_ge(S("hg_sc_used"), 7 * (hp + 1))
                for parity in range(2):
                    for h in range(2):
                        for c in range(parity, NCH, 2):
                            half = slice(CH * parity, CH * parity + CH)
                            out = bank(4 + h, CH, lo=c * CH)
                            pair = (h * 3 + c // 2) * CH
                            last = mm(out, vn[half, h, c // 2, :], hAT[half, pair:pair + CH], start=True, stop=(c == 0))
                            if c:
                                sl = c - 1 if c < 4 else 4
                                last = mm(out, hS[:, sl, 2 * hp + h, :], hq_[:, h * T + c * CH:h * T + c * CH + CH],
                                          start=False, stop=True)
                    last.then_inc(S("hg_o"), 1)
                    pe.wait_ge(S("hg_o"), 2 * hp + parity + 1)
                for h in range(2):
                    pe.wait_ge(S("hg_sq"), 2 * hp + h + 1)
                    mm(bank(6 + h, T), ones[:, :], sq[:, 0, h * T:h * T + T], start=True, stop=True)\
                        .then_inc(S("hg_ss"), 1)

            def ssd_gamma():
                pe.wait_ge(S("dt_done"), 1)
                pe.wait_ge(S("cv_new"), 1)
                pe.wait_ge(S("hg_normed"), 4)
                for q in range(3):
                    n = P if q < 2 else TS
                    for w in range(2):
                        last = tr(bank(6, NH, n, lo=(2 * q + w) * NH), dtw[:, w, q * P:q * P + n],
                                  ident[0:NH, 0:NH])
                last.then_inc(S("bdt_turned"), 1)
                for i in range(NXBC):
                    last = tr(psum[0:6, 3 + i // 4, (i % 4) * P:(i % 4) * P + P], cvout[:, i, :], ident[:, :])
                last.then_inc(S("cv_new_turned"), 1)

            def ssd_nat(q):
                n = P if q < 2 else TS
                pe.wait_ge(S("conv_silu"), NXBC)
                if q == 0:
                    pe.wait_ge(S("cv_stored"), 1)
                    pe.wait_ge(S("bdt_taken"), 1)
                else:
                    pe.wait_ge(S("ssd_done"), 2 * q)
                cols = slice(q * P, q * P + n)
                for i in range(8):
                    tr(bank(4 + i // 4, P, n, lo=(i % 4) * P), xbcT[:, i, cols], ident[:, :])
                tr(bank(6, P, n, lo=0), xbcT[:, 8, cols], ident[:, :])
                for g in range(2):
                    rows = slice(64 * g, 64 * g + 64)
                    for c in range(2 * q, min(2 * q + 2, NCH)):
                        c2 = c % 2
                        last = mm(psum[CH * c2:CH * c2 + CH, 6 + g, P:P + CH],
                                  xbcT[rows, 8, c * CH:c * CH + CH], xbcT[rows, 9, c * CH:c * CH + CH],
                                  start=True, stop=True)
                last.then_inc(S("ssd_nat"), 1)

            def ssd_decay(c):
                pe.wait_ge(S("ssd_diag"), c + 1)
                for g in range(2):
                    last = mm(bank(4 + g), ones[0:NH, :], dg[0:NH, 512 * g:512 * g + 512], start=True, stop=True)
                last.then_inc(S("ssd_b"), 1)

            def ssd_y(c):
                half = slice(CH * (c % 2), CH * (c % 2) + CH)
                pe.wait_ge(S("ssd_vd"), c + 1)
                for g in range(2):
                    rows = slice(64 * g, 64 * g + 64)
                    last = mm(psum[rows, 7, :], bn[half, 64 * g:64 * g + 64], vd[half, 512 * g:512 * g + 512],
                              start=True, stop=True)
                last.then_inc(S("ssd_dS"), 1)
                pe.wait_ge(S("ssd_W"), c + 1)
                if c == 4:
                    pe.wait_ge(S("ssd_in_loaded"), 32)
                def head_out(h):
                    return psum[64 * (h % 2):64 * (h % 2) + 64, 3, (h // 2) * CH:(h // 2) * CH + CH]

                for h in range(NH):
                    last = mm(head_out(h), v_[half, h * 64:h * 64 + 64], W[half, h * CH:h * CH + CH],
                              start=(h < 2), stop=(c == 0 and h >= NH - 2), skip_group_check=True)
                if c:
                    sl = c - 1 if c < 4 else 4
                    for h in range(NH):
                        last = mm(head_out(h), aS[:, sl, (h % 8) * 64:(h % 8) * 64 + 64], ctil[:, h * CH:h * CH + CH],
                                  start=False, stop=(h >= NH - 2), skip_group_check=True)
                last.then_inc(S("ssd_y"), 1)

            for item in PLAN:
                kind = item[0]
                if kind == "in":
                    in_mm(item[1], item[2])
                elif kind == "ada":
                    ada(item[1])
                elif kind == "out":
                    out_piece(item[1], item[2])
                elif kind == "s5_in":
                    s5_in(item[1])
                elif kind == "s5_out":
                    s5_out(item[1])
                elif kind == "s5_glu":
                    s5_glu()
                elif kind == "hg_prep":
                    hg_prep(item[1])
                elif kind == "hg_level":
                    hg_level(item[1], item[2])
                elif kind == "hg_kd":
                    hg_kd(item[1])
                elif kind == "hg_state":
                    hg_state(item[1])
                elif kind == "hg_out":
                    hg_out(item[1])
                elif kind == "ssd_gamma":
                    ssd_gamma()
                elif kind == "ssd_nat":
                    ssd_nat(item[1])
                elif kind == "ssd_decay":
                    ssd_decay(item[1])
                elif kind == "ssd_y":
                    ssd_y(item[1])
                elif kind == "ssd_norm":
                    sum_squares(3, 4, "ssd")
            pe.wait_ge(S("bulk_evac"), ALL_GROUPS)
            ada_turn(47)

            for n in range(4):
                r = OUTP + n
                pe.wait_ge(S(f"w_landed{r % RING}"), 16 * (r // RING + 1))
                w = slot[:, r % RING, :].rearrange("p (k n) -> p k n", k=8)
                for q in range(4):
                    m = 4 * n + q
                    if m >= 4:
                        pe.wait_ge(S("x_mixed"), 2 * (m - 3))
                    for k in range(8):
                        if m == 0:
                            pe.wait_ge(S("merged"), k + 1)
                        last = mm(bank(4 + m % 4, T), w[:, k, q * P:(q + 1) * P], mixed[k], start=(k == 0), stop=(k == 7))
                    last.then_inc(S("out_done"), 1)
            sum_squares(3, 8, "n2")
            pe.wait_ge(S("router_loaded"), 64)
            tiles = [(j, P if j < 2 else TS) for j in range(3)]
            for k in range(KD):
                pe.wait_ge(S("h_prompt"), KD + k + 1)
                pe.wait_ge(S("h_sample"), KD + k + 1)
                for j, n in tiles:
                    mm(bank(j, 36, n), hT[:, k, j * P:j * P + n], wr[:, k, :], start=(k == 0), stop=False)
            for j, n in tiles:
                last = mm(bank(j, 36, n), ones[0:1, 0:n], brow, start=False, stop=True)
            last.then_inc(S("logits"), 1)
            for g in range(12):
                j, kg = g // 4, g % 4
                n = P if j < 2 else TS
                pe.wait_ge(S("x_mixed"), 32)
                if g >= 4:
                    pe.wait_ge(S("act_rows"), g - 3)
                for q in range(4):
                    last = tr(bank(4 + g % 4, P, n, lo=q * P), hT[:, 4 * kg + q, j * P:j * P + n], ident[:, :])
                last.then_inc(S("hn_turned"), 1)
            pe.wait_ge(S("routed"), 1)
            pe.wait_ge(S("slot_consts"), 1)
            for j in range(3):
                n = P if j < 2 else TS
                for jj in range(j + 1):
                    last = mm(bank(3, NE, n, lo=NE * j), tri[:, 0:n] if jj == j else ones[:, 0:n], Mk[:, jj, :],
                              start=(jj == 0), stop=(jj == j))
            last.then_inc(S("rank"), 1)
            pe.wait_ge(S("routed"), 2)
            mm(bank(3, 3), ones[:, :], rt[:, 496:499], start=True, stop=True).then_inc(S("rank"), 1)

            def turn_x(i, g_, par):
                pe.wait_ge(S(f"xg_landed{par}"), 8 * (i - par) + 16)
                if not (isinstance(i, int) and 4 * i + g_ < 2):
                    pe.wait_ge(S("xe_ready"), 4 * i + (g_ - 1))
                for q in range(4):
                    last = tr(bank(6 + g_ % 2, P, lo=q * P), xg[par][:, (4 * g_ + q) * P:(4 * g_ + q + 1) * P], ident[:, :])
                last.then_inc(S("xe_turned"), 1)

            def act_turn(h, e):
                rows_ = slice(CAP * h, CAP * h + CAP)
                pe.wait_ge(S("act_ready"), e + 1)
                if not (isinstance(e, int) and e < 1):
                    pe.wait_ge(S("actT_ready"), e)
                for f in range(2):
                    last = mm(bank(5, CAP, lo=f * CAP), asb[rows_, f * P:(f + 1) * P], ident[rows_, rows_],
                              start=True, stop=True)
                last.then_inc(S("act_turned"), 1)

            def expert_gu(i, h, par, prev):
                e = 2 * i + h
                rows_ = slice(CAP * h, CAP * h + CAP)
                pe.wait_ge(S(f"gu_landed{h}"), 32 * i + 32)
                pe.wait_ge(S("xe_ready"), 4 * i + 4)
                if not (isinstance(e, int) and e < 2):
                    pe.wait_ge(S("act_ready"), e - 1)
                for k in range(KD):
                    last = mm(psum[rows_, 0, :], xe[par][:, k, CAP * h:CAP * h + CAP], gu[h][:, k, :],
                              start=(k == 0), stop=(k == KD - 1))
                    if k == 11 and prev:
                        act_turn(1 - h, e - 1)
                last.then_inc(S("gu_done"), 1)

            def expert_down(i, h):
                e = 2 * i + h
                rows_ = slice(CAP * h, CAP * h + CAP)
                pe.wait_ge(S(f"dn_landed{h}"), 16 * i + 16)
                pe.wait_ge(S("actT_ready"), e + 1)
                if not (isinstance(e, int) and e < 2):
                    pe.wait_ge(S("y_rows_sb"), e - 1)
                for n in range(4):
                    for f in range(2):
                        last = mm(psum[rows_, 1 + n, :], aTT[:, h, f, :], dn[h][:, f, 512 * n:512 * n + 512],
                                  start=(f == 0), stop=(f == 1))
                last.then_inc(S("down_done"), 1)

            def pair(i, par, more):
                expert_gu(i, 0, par, not (isinstance(i, int) and i == 0))
                if not (isinstance(i, int) and i == 0):
                    expert_down(i - 1, 1)
                if more:
                    turn_x(i + 1, 0, 1 - par)
                    turn_x(i + 1, 1, 1 - par)
                expert_gu(i, 1, par, True)
                expert_down(i, 0)
                if more:
                    turn_x(i + 1, 2, 1 - par)
                    turn_x(i + 1, 3, 1 - par)

            pe.wait_ge(S("act_rows"), 12)
            pe.wait_ge(S("routed"), 5)
            for g_ in range(4):
                turn_x(0, g_, 0)
            pair(0, 0, True)
            pair(1, 1, True)
            with pe.Fori(1, QUADS - 1) as q:
                pair(2 * q, 0, True)
                pair(2 * q + 1, 1, True)
            pair(NPAIR - 2, 0, True)
            pair(NPAIR - 1, 1, False)
            act_turn(1, NE - 1)
            expert_down(NPAIR - 1, 1)
            for g in range(12):
                j, kg = g // 4, g % 4
                n = P if j < 2 else TS
                if kg == 0:
                    pe.wait_ge(S("rows_summed"), j + 1)
                    pe.wait_ge(S("xe_ready"), 4 * NPAIR)
                if g >= 2:
                    pe.wait_ge(S("m_added"), g - 1)
                for q in range(4):
                    last = tr(bank(6 + g % 2, n, lo=q * n), r1[0:n, j, (4 * kg + q) * P:(4 * kg + q + 1) * P], ident[0:n, 0:n])
                last.then_inc(S("m_turned"), 1)
            with pe.If(pe.value_load(spill[0:1, :], min_val=0, max_val=2 * T) > 0):
                pe.wait_ge(S("m_added"), 12)
                for j in range(3):
                    n = P if j < 2 else TS
                    last = tr(psum[0:NE, 3, j * P:j * P + n], comb[0:n, j, :], ident[0:n, 0:n])
                last.then_inc(S("fb_comb_turned"), 1)
                pe.wait_ge(S("fb_dve"), 2)
                pe.sem_inc(S("fb_free"), 1)
                w0, w1 = (slot[:, j, :].rearrange("p (k n) -> p k n", k=KD) for j in range(2))
                w2 = slot[:, 2, :].rearrange("p (k n) -> p k n", k=2)
                with pe.Fori(1, NE + 1) as e:
                    pe.wait_ge(S("fb_landed"), 48 * e)
                    pe.wait_ge(S("fb_added"), 4 * e - 3)
                    for b, w in ((0, w0), (2, w1)):
                        for f in range(2):
                            for k in range(KD):
                                last = mm(bank(b + f, T), w[:, k, f * P:(f + 1) * P], hT[:, k, :],
                                          start=(k == 0), stop=(k == KD - 1))
                    last.then_inc(S("fb_hidden"), 1)
                    pe.wait_ge(S("fb_act"), e)
                    for g in range(4):
                        pe.wait_ge(S("fb_added"), 4 * e + (g - 3))
                        for m in range(4 * g, 4 * g + 4):
                            for f in range(2):
                                last = mm(bank(4 + m % 4, T), w2[:, f, m * P:(m + 1) * P], act_[:, f * T:f * T + T],
                                          start=(f == 0), stop=(f == 1))
                        last.then_inc(S("fb_down"), 1)
                    pe.wait_ge(S("fb_down"), 4 * e)
                    pe.sem_inc(S("fb_free"), 1)
            sum_squares(3, 8, "n3")
            for g in range(12):
                j, kg = g // 4, g % 4
                pe.wait_ge(S("y_ready"), 4 * kg + 4 if j == 0 else KD)
                n = P if j < 2 else TS
                if g >= 4:
                    pe.wait_ge(S("y_rows"), g - 3)
                for q in range(4):
                    last = tr(bank(4 + g % 4, P, n, lo=q * P), xT[:, 4 * kg + q, j * P:j * P + n], ident[:, :])
                last.then_inc(S("y_turned"), 1)

        @block.vector
        def _(dve):
            v = nc.vector
            st = Steps(dve, "dve_step")
            tt, ts, stt = v.tensor_tensor, v.tensor_scalar, v.scalar_tensor_tensor
            MUL, ADD, SUB = ALU.mult, ALU.add, ALU.subtract

            dve.wait_ge(S("setup_turned"), 1)
            st(v.tensor_copy(cT[:, :, :], bank(3, 32, lo=384).rearrange("p (k c) -> p k c", k=KD)), "setup_taken")
            for g in range(12):
                j, kg = g // 4, g % 4
                n = P if j < 2 else TS
                dve.wait_ge(S("x_turned"), g + 1)
                st(v.tensor_copy(xT[:, 4 * kg:4 * kg + 4, j * P:j * P + n],
                                 bank(4 + g % 4, 4 * n).rearrange("p (q t) -> p q t", q=4)), "x_transposed", wait=False)
            dve.wait_ge(S("ld_loaded"), 32)
            dve.wait_ge(S("consts_a"), 1)
            for lo, n in ((0, 16), (32, 8)):
                last = v.tensor_copy(prow[lo:lo + n, 2, :].rearrange("p (g q) -> p g q", g=2),
                                     bc(ldrow[lo:lo + n, :].unsqueeze(2), [n, 2, 64]))
                st(last, "setup_taken" if lo else None)
            dve.wait_ge(S("setup_turned"), 2)
            st(v.tensor_copy(parT[:, 0:250], bank(3, 250)))
            st(v.tensor_copy(parT[:, 256:352], bank(3, 96, lo=256)), "setup_taken")
            dve.wait_ge(S("setup_turned"), 3)
            st(v.tensor_copy(xbcp[:, :, PADS - 3:PADS],
                             bank(3, 40, lo=416).rearrange("p (i c) -> p i c", i=NXBC)[:, :, 0:3]), "setup_taken")
            st(v.memset(xbcp[:, :, 0:3], 0.0))
            cos_, sin_, dt_, ex, mag, th, wr_, wc, k_, lr, aR, aI, den, nr, cr, ci, t1, t2 = \
                (sm[:, i, :] for i in range(18))
            st(ts(lr, lam_re, -1e-4, None, ALU.min))
            dve.wait_ge(S("setup_act"), 2)
            st(tt(ex, lr, dt_, MUL), "setup_dve")
            st(tt(th, lam_im, dt_, MUL))
            magic = 12582912.0
            st(ts(k_, th, 0.15915494309189535, magic, MUL, ADD))
            st(ts(k_, k_, magic, None, SUB))
            st(stt(t1, k_, -6.28125, th, MUL, ADD))
            st(stt(t2, k_, -0.0019350051879882812, t1, MUL, ADD))
            st(stt(t1, k_, -3.0199159819e-07, t2, MUL, ADD))
            pi = 3.1415925
            st(ts(wr_, t1, pi, -pi, ALU.min, ALU.max))
            st(stt(t2, wr_, -1.0, wr_, MUL, ALU.max))
            st(ts(wc, t2, -1.0, 1.5707963267948966, MUL, ADD), "setup_dve")
            dve.wait_ge(S("setup_act"), 5)
            dve.wait_ge(S("setup_act"), 3)
            st(tt(aR, mag, cos_, MUL))
            st(tt(aI, mag, sin_, MUL))
            st(tt(t1, lr, lr, MUL))
            st(tt(t2, lam_im, lam_im, MUL))
            st(tt(den, t1, t2, ADD))
            st(v.reciprocal(den, den))
            st(ts(nr, aR, -1.0, None, ADD))
            st(tt(t1, nr, lr, MUL))
            st(tt(t2, aI, lam_im, MUL))
            st(tt(cr, t1, t2, ADD))
            st(tt(cr, cr, den, MUL))
            st(tt(t1, aI, lr, MUL))
            st(tt(t2, nr, lam_im, MUL))
            st(tt(ci, t1, t2, SUB))
            st(tt(ci, ci, den, MUL))
            dve.wait_ge(S("s5_loaded"), 64)
            dve.wait_ge(S("consts_b"), 1)
            for w in range(2):
                b0, b1 = (BR, BI) if w == 0 else (BI, BR)
                for g in range(2):
                    rows = slice(64 * g, 64 * g + 64)
                    crb, cib = (bc(x[rows, :].unsqueeze(2), [64, 16, 16]) for x in (cr, ci))
                    st(tt(btmp[rows], b1[rows], cib, MUL))
                    st(tt(bdp[rows, w, :, g, :], b0[rows], crb, MUL))
                    st(tt(bdp[rows, w, :, g, :], bdp[rows, w, :, g, :], btmp[rows], SUB if w == 0 else ADD))
            for w in range(2):
                for g in range(2):
                    last = st(ts(cpad[:, w, :, g, :], CR[:, w], small[:, g:g + 1], 1.0 if w == 0 else -1.0, MUL, MUL),
                              "s5_mats" if w and g else None)
            dve.wait_ge(S("squares_used"), 8)

            def mean_square(b, width):
                st(ts(rinv[:, :], bank(b, T), 1.0 / width, EPS, MUL, ADD), "mean_square")

            def invert(sem):
                dve.wait_ge(S(sem[0]), sem[1])
                st(v.reciprocal(rinv[:, :], rinv[:, :]))

            def modulate(g, sc):
                for s_ in range(2):
                    st(ts(ab1[:, :, s_], seg(sc)[:, :, s_], 1.0, None, ADD))
                    st(tt(ab1[:, :, s_], ab1[:, :, s_], g, MUL))
                dve.wait_ge(S("x_transposed"), 12)
                for k in range(0, KD, 4):
                    st(tt(hT[:, k:k + 4, :], xT[:, k:k + 4, :], bc(rinv[:, :].unsqueeze(1), [P, 4, T]), MUL),
                       "h_scaled")

            def shift_sample(sh):
                for k in range(KD):
                    st(ts(hT[:, k, TP:T], hT[:, k, TP:T], ab1[:, k, 1:2], seg(sh)[:, k, 1:2], MUL, ADD),
                       "h_sample", wait=False)

            mean_square(3, D)
            invert(("root", 1))
            dve.wait_ge(S("setup_turned"), 4)
            for w in range(2):
                st(v.tensor_copy(BDT[:, w], bank(4 + w).rearrange("p (u n) -> p u n", u=4)))
                st(v.tensor_copy(CT[:, w], bank(6 + w).rearrange("p (u n) -> p u n", u=4)),
                   "s5_mats_ready" if w else None)
            lb, omlb, e_, r_ = (small[:, 40 + 4 * i:44 + 4 * i] for i in range(4))
            st(tt(e_, lb_raw, lb_raw, SUB))
            st(ts(e_, e_, 1.0, None, ADD))
            st(v.reciprocal(r_, e_))
            st(tt(e_, e_, r_, MUL))
            st(tt(lb, e_, e_, SUB))
            st(ts(omlb, lb, -1.0, 1.0, MUL, ADD))

            def mod_take(i, n):
                tiles = slice(2 * i, 2 * (i + n))
                src = bank(2, 4 * n, lo=turned_at(i)).rearrange("p (q c) -> p q c", c=2)
                tt(modT[:, tiles, :], src, bc(b_ada[:, tiles].unsqueeze(2), [P, 2 * n, 2]), ADD)\
                    .then_inc(S("mod_ready"), n)

            dve.wait_ge(S("mod_turned"), 16)
            mod_take(0, 16)
            dve.wait_ge(S("mod_ready"), 16)
            modulate(g_mix, 1)
            shift_sample(0)

            def ada(i):
                if i > 20 and i % 4 == 1:
                    take(i - 5)

            def take(i):
                dve.wait_ge(S("mod_turned"), i + 4)
                mod_take(i, 4)

            def s5_in(b):
                br, bi, yr, yi, tm = s5b[0:5]
                pc, ps = s5b[5 + 2 * (b % 2)], s5b[6 + 2 * (b % 2)]
                dve.wait_ge(S("s5_bu_sb"), 2 * b + 2)
                dve.wait_ge(S("s5_table"), b + 1)
                if b:
                    dve.wait_ge(S("s5_y"), b)
                st(tt(yr, br, pc, MUL))
                st(tt(tm, bi, ps, MUL))
                st(tt(yr, yr, tm, ADD))
                st(tt(yi, bi, pc, MUL))
                st(tt(tm, br, ps, MUL))
                st(tt(yi, yi, tm, SUB))
                for i in range(2):
                    n = 2 * b + i
                    for lo, hi in STREAMS:
                        for src, dst, x0 in ((yr, br, x0re), (yi, bi, x0im)):
                            last = v.tensor_tensor_scan(
                                dst[:, i * T + lo:i * T + hi], bc(mag[:, n:n + 1], [P, hi - lo]),
                                src[:, i * T + lo:i * T + hi], x0[:, n:n + 1] if lo else 0.0, MUL, ADD)
                            st(last, wait=False)
                dve.wait_ge(S("dve_step"), st.n["dve_step"])
                st(tt(yr, br, pc, MUL))
                st(tt(tm, bi, ps, MUL))
                st(tt(yr, yr, tm, SUB))
                st(tt(yi, br, ps, MUL))
                st(tt(tm, bi, pc, MUL))
                st(tt(yi, yi, tm, ADD))
                for k, (src, col) in enumerate(((yr, TP - 1), (yi, TP - 1), (yr, T - 1), (yi, T - 1))):
                    st(v.tensor_copy(s5fin[:, k, 2 * b:2 * b + 2].unsqueeze(2),
                                     src.rearrange("p (i t) -> p i t", i=2)[:, :, col:col + 1]),
                       "s5_turned" if k == 3 else None)

            def s5_out(b):
                if b % 2 == 0:
                    return
                u = b // 2
                y, y3 = sq[:, 1, T:2 * T], sq[:, 1, 0:T]
                dve.wait_ge(S("s5_y"), b + 1)
                st(stt(y, proj[:, U + u, :], s5_d[:, u:u + 1], bank(3, T), MUL, ADD))
                st(tt(y3, y, y, MUL))
                st(ts(y3, y3, 0.044715, 1.0, MUL, ADD))
                st(tt(y3, y3, y, MUL))
                st(ts(y3, y3, 1.5957691216057308, None, MUL), "s5_gelu_arg")
                dve.wait_ge(S("s5_gelu_sig"), u + 1)
                st(tt(proj[:, U + u, :], y, y3, MUL), "s5_g")

            def s5_glu():
                dve.wait_ge(S("glu_mm"), 4)
                for m in range(4):
                    dve.wait_ge(S("glu_sig"), m + 1)
                    st(tt(proj[:, U + m, :], proj[:, U + m, :], rinv[:, :], MUL), "glu_used")
                dve.wait_ge(S("s5_fin_turned"), 1)
                st(v.tensor_copy(sq[0:16, 1, 0:512], psum[0:16, 3, :]), "s5_fin_rows")

            hb3 = lambda t, m: t.rearrange("p (n r) -> p n r", r=2 * m)

            def hg_prep(hp):
                hf = flat[:, (HF + 2 * hp) * T:(HF + 2 * hp + 2) * T]
                dve.wait_ge(S("hg_sig"), hp + 1)
                for h in range(2):
                    c = slice(h * T, h * T + T)
                    n = 2 * hp + h
                    st(ts(hE[:, c], hE[:, c], omlb[:, n:n + 1], lb[:, n:n + 1], MUL, ADD))
                    st(ts(hf[:, c], hf[:, c], omlb[:, n:n + 1], None, MUL), "hg_k" if h else None)
                if hp:
                    dve.wait_ge(S("hg_o"), 2)
                st(ts(hE, hE, 1e-30, None, ALU.max))
                st(ts(hq_, hE, 2.0 ** -40, None, ALU.is_lt))
                st(ts(hb, hq_, 2.0 ** 50, 1.0, MUL, ADD))
                st(tt(hE, hE, hb, MUL), "hg_f")
                dve.wait_ge(S("hg_ln"), hp + 1)
                st(stt(hE, hq_, -34.657359, hE, MUL, ADD))
                for h in range(2):
                    c = slice(h * T, h * T + T)
                    st(v.tensor_tensor_scan(hb[:, c], rmask[:, :], hE[:, c], 0.0, MUL, ADD))
                dve.wait_ge(S("hg_v"), hp + 1)
                for h in range(2):
                    b3 = bank(6 + h, 384).rearrange("p (q k) -> p q k", q=3)
                    st(v.tensor_copy(vn[:, h, 0:2, :], b3[:, 0:2, :]))
                    st(v.tensor_copy(vn[0:64, h, 2, :], b3[0:64, 2, :]), "hg_vn" if h else None)

            def hg_take(hp, lv):
                it = 7 * hp + lv
                dve.wait_ge(S("hg_sc"), it + 1)
                src = bank(4 + it % 2, 384).rearrange("p (n t) -> p n t", n=6)
                dst = (hAT if lv == 0 else htmp).rearrange("p (n t) -> p n t", n=6)
                mask = bc(lmask[:, lv, :].unsqueeze(1), [P, 6, CH])
                st(tt(dst, src, mask, MUL), "hg_sc_used")
                if lv:
                    st(tt(hAT, hAT, htmp, ADD))

            def hg_level(hp, lv):
                q_, k_ = (flat[:, (x + 2 * hp) * T:(x + 2 * hp + 2) * T] for x in (HQ, HF))
                if lv == 0:
                    return
                m = LEVELS[lv]
                b3 = hb3(hb, m)
                st(tt(hb3(hE, m), b3, bc(b3[:, :, m - 1:m], [P, 640 // (2 * m), 2 * m]), SUB))
                st(stt(hE, hE, -1.0, hE, MUL, ALU.min), "hg_expo")
                hg_take(hp, lv - 1)
                dve.wait_ge(S("hg_exp"), 6 * hp + lv)
                st(tt(hq_, q_, hE, MUL))
                st(tt(hk_, k_, hE, MUL), "hg_qk")

            def hg_kd(hp):
                q_, k_ = (flat[:, (x + 2 * hp) * T:(x + 2 * hp + 2) * T] for x in (HQ, HF))
                hg_take(hp, 6)
                st(v.memset(small[:, 60:61], 0.0), "hg_expo2")
                dve.wait_ge(S("hg_exp2"), 2 * hp + 1)
                st(tt(hq_, q_, hE, MUL))
                e3, b3 = (t.rearrange("p (n r) -> p n r", r=CH) for t in (hE, hb))
                st(v.tensor_copy(small[:, 80:90].unsqueeze(2), e3[:, :, CH - 1:CH]))
                st(tt(e3, bc(b3[:, :, CH - 1:CH], [P, 10, CH]), b3, SUB), "hg_expo2")
                dve.wait_ge(S("hg_exp2"), 2 * hp + 2)
                st(tt(hE, k_, hE, MUL), "hg_kd")
                for h in range(2):
                    dve.wait_ge(S("hg_kd_turned"), 2 * hp + h + 1)
                    b4 = bank(6 + h, 384).rearrange("p (q k) -> p q k", q=3)
                    st(v.tensor_copy(kdn[:, h, 0:2, :], b4[:, 0:2, :]))
                    st(v.tensor_copy(kdn[0:64, h, 2, :], b4[0:64, 2, :]), "hg_kdn" if h else None)

            def hg_state(hp):
                for c in range(NCH):
                    dve.wait_ge(S("hg_dS"), NCH * hp + c + 1)
                    if c == 4:
                        dve.wait_ge(S("hg_in_loaded"), 16)
                    into = (0, 1, 2, 3, 5)[c]
                    frm = (None, 0, 1, 2, 4)[c]
                    for h in range(2):
                        add = bank(6 + c % 2, P, lo=h * P)
                        dst = hS[:, into, 2 * hp + h, :]
                        if frm is None:
                            last = v.tensor_copy(dst, add)
                        else:
                            last = stt(dst, hS[:, frm, 2 * hp + h, :], small[:, 80 + 5 * h + c:81 + 5 * h + c],
                                       add, MUL, ADD)
                        st(last, "hg_S" if h else None)

            def hg_out(hp):
                for h in range(2):
                    n = 2 * hp + h
                    dve.wait_ge(S("hg_ss"), n + 1)
                    st(ts(rinv[:, :], bank(6 + h, T), 1.0 / P, EPS, MUL, ADD), "hg_var")
                    invert(("hg_root", n + 1))
                    st(stt(hb[:, 0:T], bank(4 + h, T), hg_g[:, n:n + 1], rinv[:, :], MUL, MUL))
                    dve.wait_ge(S("hg_gate"), hp + 1)
                    st(tt(proj[:, HG + n, :], proj[:, HG + n, :], hb[:, 0:T], MUL), "hg_normed")

            def ssd_dt():
                dve.wait_ge(S("bulk_evac"), all_in)
                dve.wait_ge(S("bulk_done"), all_in)
                dve.wait_ge(S("hg_state_stored"), 32)
                st(v.memset(ctil, 0.0))
                bias, alog = small[0:NH, 32:33], small[0:NH, 34:35]
                x_, e_, u_, l_, raw = (dtw[:, i, :] for i in range(5))
                st(v.tensor_copy(raw, dt_raw))
                st(ts(raw, raw, bias, None, ADD))
                st(stt(x_, raw, -1.0, raw, MUL, ALU.min), "dt_arg")
                dve.wait_ge(S("dt_func"), 1)
                st(ts(u_, e_, 1.0, None, ADD), "dt_arg")
                dve.wait_ge(S("dt_func"), 2)
                st(ts(u_, u_, -1.0, None, ADD))
                st(ts(x_, u_, 0.0, None, ALU.is_equal))
                st(tt(u_, u_, x_, ADD))
                st(tt(l_, l_, x_, ADD))
                st(v.reciprocal(u_, u_))
                st(tt(l_, l_, e_, MUL))
                st(tt(l_, l_, u_, MUL))
                st(ts(x_, raw, 0.0, None, ALU.max))
                st(tt(dtw[:, 1, :], x_, l_, ADD))
                dve.wait_ge(S("setup_act"), 4)
                st(ts(l_, dtw[:, 1, :], alog, -1.0, MUL, MUL))
                st(v.tensor_tensor_scan(dtw[:, 0, :], rmask[0:NH, :], l_, 0.0, MUL, ADD), "dt_done")
                for s_, c0 in ((0, PADP + TP - 3), (1, PADS + TS - 3)):
                    st(v.tensor_copy(cvout[:, :, 3 * s_:3 * s_ + 3], xbcp[:, :, c0:c0 + 3]), "cv_new" if s_ else None)

            def ssd_conv(i):
                for j in range(4):
                    for n in (2 * i, 2 * i + 1):
                        for lo, hi in STREAMS:
                            p0 = (PADP if lo == 0 else PADS) - 3 + j
                            dst, src = xbcT[:, n, lo:hi], xbcp[:, n, p0:p0 + hi - lo]
                            last = n % 2 and lo
                            if j == 0:
                                ins = ts(dst, src, conv_w[:, 0, n:n + 1], conv_b[:, n:n + 1], MUL, ADD)
                            else:
                                ins = stt(dst, src, conv_w[:, j, n:n + 1], dst, MUL, ADD)
                            st(ins, "conv_out" if last and j == 3 else None, wait=bool(last))

            def ssd_gamma():
                dve.wait_ge(S("bdt_turned"), 1)
                src = bank(6, 96).rearrange("p (q w h) -> p q w h", q=3, w=2)
                st(v.tensor_copy(bnat[:, 0:2].rearrange("p q w h -> p (q w h)"), bank(6, 64)))
                st(v.tensor_copy(bnat[0:64, 2].rearrange("p w h -> p (w h)"), bank(6, 32, 64, lo=64)), "bdt_taken")
                dve.wait_ge(S("cv_new_turned"), 1)
                st(v.tensor_copy(cvst[0:6, :], psum[0:6, 3:6, :].rearrange("p b n -> p (b n)")[:, 0:NXBC * P]),
                   "cv_stored")

            def ssd_nat(q):
                n = P if q < 2 else TS
                if q == 0:
                    dve.wait_ge(S("cv_saved"), 32)
                dve.wait_ge(S("ssd_nat"), q + 1)
                st(tt(v_[0:n, :].rearrange("p (h n) -> p h n", h=NH),
                      psum[0:n, 4:6, :].rearrange("p b n -> p (b n)").rearrange("p (h n) -> p h n", h=NH),
                      bc(bnat[0:n, q, 1, :].unsqueeze(2), [n, NH, 64]), MUL))
                st(v.tensor_copy(bn[0:n, :], bank(6, P, n)))
                st(tt(gtm[0:n, :].rearrange("p (g t) -> p g t", g=2), psum[0:n, 6:8, P:P + CH],
                      bc(causal[0:n, :].unsqueeze(1), [n, 2, CH]), MUL))

            def ssd_diag(c):
                cols = slice(c * CH, c * CH + CH)
                st(tt(dg[0:NH, :].rearrange("p (h t) -> p h t", h=NH),
                      bc(dtw[:, 0, cols].unsqueeze(1), [NH, NH, CH]),
                      bc(ident[0:NH, 0:NH].unsqueeze(2), [NH, NH, CH]), MUL), "ssd_diag")

            def ssd_decay(c):
                half = slice(CH * (c % 2), CH * (c % 2) + CH)
                cols = slice(c * CH, c * CH + CH)
                q = c // 2
                if c % 2 == 0:
                    ssd_diag(c)
                dve.wait_ge(S("ssd_b"), c + 1)
                bB = psum[half, 4:6, :].rearrange("p b n -> p (b n)").rearrange("p (h t) -> p h t", h=NH)
                dl = small[half, 64:80]
                st(tt(dl, bB[:, :, CH - 1], bnat[half, q, 0, :], SUB))
                w3 = W[half, :].rearrange("p (h t) -> p h t", h=NH)
                st(tt(w3, bB, bc(bnat[half, q, 0, :].unsqueeze(2), [CH, NH, CH]), SUB), "ssd_diff")
                st(ts(W[half, :], W[half, :], 0.0, None, ALU.min), "ssd_diff")
                dve.wait_ge(S("ssd_exp"), 2 * c + 1)
                st(tt(vd[half, :].rearrange("p (h n) -> p h n", h=NH), v_[half, :].rearrange("p (h n) -> p h n", h=NH),
                      bc(dl.unsqueeze(2), [CH, NH, 64]), MUL), "ssd_vd")
                dve.wait_ge(S("ssd_EB"), 2 * c + 2)
                e3 = EB.rearrange("p (j t) -> p j t", j=8)
                for g in range(2):
                    rows = slice(64 * g, 64 * g + 64)
                    st(tt(ctil[rows, 512 * g:512 * g + 512].rearrange("p (j t) -> p j t", j=8), e3[rows],
                          bc(xbcT[rows, 9, cols].unsqueeze(1), [64, 8, CH]), MUL))
                dve.wait_ge(S("ssd_exp"), 2 * c + 2)
                for g in range(2):
                    st(tt(W[half, 512 * g:512 * g + 512].rearrange("p (h t) -> p h t", h=8),
                          W[half, 512 * g:512 * g + 512].rearrange("p (h t) -> p h t", h=8),
                          bc(gtm[half, g * CH:g * CH + CH].unsqueeze(1), [CH, 8, CH]), MUL), "ssd_W" if g else None)

            def ssd_y(c):
                cols = slice(c * CH, c * CH + CH)
                e3 = EB.rearrange("p (j t) -> p j t", j=8)
                into = (0, 1, 2, 3, 5)[c]
                frm = (None, 0, 1, 2, 4)[c]
                dve.wait_ge(S("ssd_dS"), c + 1)
                if frm is None:
                    st(v.tensor_copy(aS[:, into, :], bank(7)))
                else:
                    if c == 4:
                        dve.wait_ge(S("ssd_in_loaded"), 32)
                    st(tt(aS[:, into, :].rearrange("p (j n) -> p j n", j=8),
                          aS[:, frm, :].rearrange("p (j n) -> p j n", j=8),
                          bc(e3[:, :, CH - 1:CH], [P, 8, 64]), MUL))
                    st(tt(aS[:, into, :], aS[:, into, :], bank(7), ADD))
                st(v.memset(small[:, 61:62], 0.0), "ssd_S")
                y3 = ytmp.rearrange("p (i t) -> p i t", i=8)
                st(tt(y3, xbcT[:, 0:8, cols], bc(ssd_D.unsqueeze(2), [P, 8, CH]), MUL))
                if c % 2 == 0 and c + 1 < NCH:
                    ssd_diag(c + 1)
                dve.wait_ge(S("ssd_y"), c + 1)
                st(tt(ytmp, ytmp, bank(3), ADD))
                dve.wait_ge(S("z_silu"), 1)
                st(tt(proj[:, 0:8, cols], proj[:, 0:8, cols], y3, MUL), "ssd_done")

            def ssd_norm():
                dve.wait_ge(S("squares_used"), NORM["ssd"] + 4)
                mean_square(3, 1024)
                invert(("root", 2))
                for i in range(8):
                    st(stt(proj[:, i, :], proj[:, i, :], ssd_g[:, i:i + 1], rinv[:, :], MUL, MUL), "merged", wait=False)

            for item in PLAN:
                kind = item[0]
                if kind == "ada":
                    ada(item[1])
                elif kind == "s5_in":
                    s5_in(item[1])
                elif kind == "s5_out":
                    s5_out(item[1])
                elif kind == "s5_glu":
                    s5_glu()
                elif kind == "hg_prep":
                    hg_prep(item[1])
                elif kind == "hg_level":
                    hg_level(item[1], item[2])
                elif kind == "hg_kd":
                    hg_kd(item[1])
                elif kind == "hg_state":
                    hg_state(item[1])
                elif kind == "hg_out":
                    hg_out(item[1])
                elif kind == "ssd_dt":
                    ssd_dt()
                elif kind == "ssd_conv":
                    ssd_conv(item[1])
                elif kind == "ssd_gamma":
                    ssd_gamma()
                elif kind == "ssd_nat":
                    ssd_nat(item[1])
                elif kind == "ssd_decay":
                    ssd_decay(item[1])
                elif kind == "ssd_y":
                    ssd_y(item[1])
                elif kind == "ssd_norm":
                    ssd_norm()
            take(44)
            dve.wait_ge(S("mod_ready"), 48)

            dve.wait_ge(S("x_part"), 16)
            for m in range(KD):
                dve.wait_ge(S("out_done"), m + 1)
                for s_, (lo, hi) in enumerate(STREAMS):
                    st(stt(xT[:, m, lo:hi], bank(4 + m % 4, T)[:, lo:hi], seg(2)[:, m, s_:s_ + 1],
                           xT[:, m, lo:hi], MUL, ADD), "x_mixed", wait=False)
            dve.wait_ge(S("x_mixed"), 32)
            dve.wait_ge(S("squares_used"), NORM["n2"] + 8)
            mean_square(3, D)
            invert(("root", 3))
            modulate(g_ffn, 4)
            shift_sample(3)

            lg = rt[:, 400:508].rearrange("p (j e) -> p j e", j=3)
            states_stored(dve)
            st(v.memset(rt, 0.0))
            dve.wait_ge(S("logits"), 1)
            st(v.tensor_copy(lg[:, 0:2, :], psum[:, 0:2, 0:36]), wait=False)
            st(v.tensor_copy(lg[0:TS, 2, :], bank(2, 36, TS)))
            G = lg[:, :, 0:4]
            ex4 = rt[:, 16:28].rearrange("p (j e) -> p j e", j=3)
            m3 = rt[:, 0:3].unsqueeze(2)
            st(v.tensor_reduce(m3, G, AX.X, ALU.max))
            st(tt(ex4, G, bc(m3, [P, 3, 4]), SUB))

            def first_max(dst, src, mx, n, tmp, idx):
                c = bc(small[:, 16:16 + n].unsqueeze(1), [P, 3, n])
                st(tt(dst, src, bc(mx, [P, 3, n]), ALU.is_equal))
                st(tt(tmp, dst, c, MUL))
                st(v.tensor_reduce(idx, tmp, AX.X, ALU.min))
                st(tt(dst, c, bc(idx, [P, 3, n]), ALU.is_equal))

            f3 = lambda off, n: rt[:, off:off + 3 * n].rearrange("p (j e) -> p j e", j=3)
            idx = rt[:, 4:7].unsqueeze(2)
            oh4 = f3(32, 4)
            first_max(oh4, G, m3, 4, f3(48, 4), idx)
            le4 = rt[:, 128:224].rearrange("p (j e) -> p j e", j=3)
            for g in range(4):
                st(tt(le4[:, :, 8 * g:8 * g + 8], lg[:, :, 4 + 8 * g:12 + 8 * g], bc(oh4[:, :, g:g + 1], [P, 3, 8]), MUL))
            le = f3(64, 8)
            st(tt(le, le4[:, :, 0:8], le4[:, :, 8:16], ADD))
            st(tt(le, le, le4[:, :, 16:24], ADD))
            st(tt(le, le, le4[:, :, 24:32], ADD))
            v1, v2 = rt[:, 8:11].unsqueeze(2), rt[:, 12:15].unsqueeze(2)
            oh1, oh2, tmp8, le2 = f3(96, 8), f3(256, 8), f3(288, 8), f3(320, 8)
            st(v.tensor_reduce(v1, le, AX.X, ALU.max))
            first_max(oh1, le, v1, 8, tmp8, idx)
            st(stt(le2.rearrange("p j e -> p (j e)"), oh1.rearrange("p j e -> p (j e)"), -3e38,
                   le.rearrange("p j e -> p (j e)"), MUL, ADD))
            st(v.tensor_reduce(v2, le2, AX.X, ALU.max))
            first_max(oh2, le2, v2, 8, tmp8, idx)
            st(tt(rt[:, 240:243].unsqueeze(2), v2, v1, SUB), "rt_expo")
            dve.wait_ge(S("rt_exp"), 1)
            e2, den, w1, w2 = (rt[:, 240 + 3 * i:243 + 3 * i].unsqueeze(2) for i in range(4))
            st(v.tensor_reduce(den, ex4, AX.X, ALU.add))
            st(v.reciprocal(den, den))
            st(ts(w1, e2, 1.0, None, ADD))
            st(v.reciprocal(w1, w1))
            st(tt(w1, w1, den, MUL))
            st(tt(w2, w1, e2, MUL))
            for g in range(4):
                for A_, oh_ in ((A1, oh1), (A2, oh2)):
                    st(tt(A_[:, :, 8 * g:8 * g + 8], oh_, bc(oh4[:, :, g:g + 1], [P, 3, 8]), MUL))
            st(v.memset(A1[64:P, 2, :], 0.0))
            st(v.memset(A2[64:P, 2, :], 0.0))
            st(tt(Mk, A1, A2, ADD), "routed")
            dve.wait_ge(S("slot_consts"), 1)
            st(v.tensor_copy(e64, e64i))
            dve.wait_ge(S("rank"), 1)
            st(v.tensor_copy(eT, eTi))
            st(v.memset(rk, 0.0))
            st(v.tensor_copy(rk[:, 0:2, :], bank(3, 64).rearrange("p (j e) -> p j e", j=2)))
            st(v.tensor_copy(rk[0:64, 2, :], bank(3, NE, 64, lo=64)))
            st(ts(ge, rk, float(CAP), None, ALU.is_ge))
            st(ts(Mk, rk, float(NPAIR), None, MUL))
            st(tt(Mk, Mk, bc(eT.unsqueeze(1), [P, 3, NE]), ADD))
            st(tt(rk, rk, bc(e64.unsqueeze(1), [P, 3, NE]), ADD))
            over, sl_, keep = rt[:, 484:490], rt[:, 490:496], rt[:, 500:506]
            for c, (A_, w_) in enumerate(((A1, w1), (A2, w2))):
                cc = slice(3 * c, 3 * c + 3)
                st(tt(am, A_, ge, MUL))
                st(v.tensor_reduce(over[:, cc].unsqueeze(2), am, AX.X, ADD))
                st(tt(am, A_, rk, MUL))
                st(v.tensor_reduce(sl_[:, cc].unsqueeze(2), am, AX.X, ADD))
                st(tt(am, A_, Mk, MUL))
                st(v.tensor_reduce(rt[:, 472 + 3 * c:475 + 3 * c].unsqueeze(2), am, AX.X, ADD))
            st(tt(rt[:, 496:499], over[:, 0:3], over[:, 3:6], ADD), "routed")
            st(ts(keep, over, -1.0, 1.0, MUL, ADD))
            st(stt(rt[:, 472:478], over, 1.0e6, rt[:, 472:478], MUL, ADD))
            st(v.tensor_copy(pos_scatter, rt[:, 472:478]), "routed")
            st(tt(rt[:, 478:484], sl_, keep, MUL))
            st(v.tensor_copy(pos_gather, rt[:, 478:484]), "routed")
            for c, (A_, w_) in enumerate(((A1, w1), (A2, w2))):
                st(tt(A_, A_, bc(w_, [P, 3, NE]), MUL))
            st(tt(comb, A1, A2, ADD))
            st(tt(comb, comb, ge, MUL))
            wk = rt[:, 506:512]
            st(tt(wk[:, 0:3].unsqueeze(2), w1, keep[:, 0:3].unsqueeze(2), MUL))
            st(tt(wk[:, 3:6].unsqueeze(2), w2, keep[:, 3:6].unsqueeze(2), MUL))
            dve.wait_ge(S("rank"), 2)
            st(v.tensor_reduce(rt[:, 499:500], bank(3, 3), AX.X, ADD))
            st(v.tensor_copy(spill, rt[:, 499:500]), "routed")

            def take_x(i, g_, par):
                dve.wait_ge(S("xe_turned"), 4 * i + (g_ + 1))
                v.tensor_copy(xe[par][:, 4 * g_:4 * g_ + 4, :], bank(6 + g_ % 2).rearrange("p (k t) -> p k t", k=4))\
                    .then_inc(S("xe_ready"), 1)

            def activate(h, e):
                rows_ = slice(CAP * h, CAP * h + CAP)
                dve.wait_ge(S("gate_silu"), e + 1)
                if not (isinstance(e, int) and e < 2):
                    dve.wait_ge(S("act_turned"), e - 1)
                tt(asb[rows_, :], sg[rows_, :], psum[rows_, 0, CW:2 * CW], MUL).then_inc(S("act_ready"), 1)

            def take_act(h, e):
                dve.wait_ge(S("act_turned"), e + 1)
                if not (isinstance(e, int) and e < 2):
                    dve.wait_ge(S("down_done"), e - 1)
                v.tensor_copy(aTT[:, h], bank(5, 2 * CAP).rearrange("p (f t) -> p f t", f=2)).then_inc(S("actT_ready"), 1)

            def take_y(h, e):
                rows_ = slice(CAP * h, CAP * h + CAP)
                dve.wait_ge(S("down_done"), e + 1)
                if not (isinstance(e, int) and e < 2):
                    dve.wait_ge(S(f"y_stored{h}"), 8 * (e - h))
                v.tensor_copy(ys[rows_, :], psum[rows_, 1:5, :].rearrange("p b n -> p (b n)")).then_inc(S("y_rows_sb"), 1)

            def pair(i, par, more):
                first = isinstance(i, int) and i == 0
                if not first:
                    take_act(1, 2 * i - 1)
                activate(0, 2 * i)
                if not first:
                    take_y(1, 2 * i - 1)
                if more:
                    take_x(i + 1, 0, 1 - par)
                    take_x(i + 1, 1, 1 - par)
                take_act(0, 2 * i)
                activate(1, 2 * i + 1)
                take_y(0, 2 * i)
                if more:
                    take_x(i + 1, 2, 1 - par)
                    take_x(i + 1, 3, 1 - par)

            dve.wait_ge(S("h2_stored"), 32)
            for g_ in range(4):
                take_x(0, g_, 0)
            pair(0, 0, True)
            pair(1, 1, True)
            with dve.Fori(1, QUADS - 1) as q:
                pair(2 * q, 0, True)
                pair(2 * q + 1, 1, True)
            pair(NPAIR - 2, 0, True)
            pair(NPAIR - 1, 1, False)
            take_act(1, NE - 1)
            take_y(1, NE - 1)
            for j in range(3):
                n = P if j < 2 else TS
                dve.wait_ge(S(f"rows_landed{j}"), 32)
                dve.wait_ge(S("act_rows"), 12 + j + 1)
                st(stt(r1[0:n, j, :], r2[0:n, j, :], wk[0:n, 3 + j:4 + j], r1[0:n, j, :], MUL, ADD), "rows_summed")
            for g in range(12):
                j, kg = g // 4, g % 4
                n = P if j < 2 else TS
                dve.wait_ge(S("m_turned"), g + 1)
                for q in range(4):
                    k = 4 * kg + q
                    cols = slice(j * P, j * P + n)
                    st(stt(xT[:, k, cols], bank(6 + g % 2, n, lo=q * n), seg(5)[:, k, j // 2:j // 2 + 1],
                           xT[:, k, cols], MUL, ADD), "m_added" if q == 3 else None, wait=False)
            dve.wait_ge(S("m_added"), 12)
            dve.wait_ge(S("dve_step"), st.n["dve_step"])
            with dve.If(dve.value_load(spill[0:1, :], min_val=0, max_val=2 * T) > 0):
                dve.wait_ge(S("fb_comb_turned"), 1)
                v.memset(acc, 0.0).then_inc(S("fb_dve"), 1)
                dve.wait_ge(S("fb_dve"), 1)
                v.tensor_copy(combT, psum[0:NE, 3, 0:T]).then_inc(S("fb_dve"), 1)
                v.memset(small[:, 62:63], 0.0).then_inc(S("fb_added"), 1)
                dve.wait_ge(S("fb_rows"), 32)
                s3 = sgc.rearrange("p (f t) -> p f t", f=2)
                a3 = act_.rearrange("p (f t) -> p f t", f=2)
                with dve.Fori(1, NE + 1) as e:
                    dve.wait_ge(S("fb_silu"), e)
                    cb = combB[:, bass.ds((e - 1) * T, T)]
                    tt(s3, s3, bc(cb.unsqueeze(1), [P, 2, T]), MUL).then_inc(S("fb_weighted"), 1)
                    dve.wait_ge(S("fb_weighted"), e)
                    tt(a3, s3, psum[:, 2:4, 0:T], MUL).then_inc(S("fb_act"), 1)
                    for g in range(4):
                        dve.wait_ge(S("fb_down"), 4 * e + (g - 3))
                        tt(acc[:, 4 * g:4 * g + 4, :], acc[:, 4 * g:4 * g + 4, :], psum[:, 4:8, 0:T], ADD)\
                            .then_inc(S("fb_added"), 1)
                dve.wait_ge(S("fb_added"), 4 * NE + 1)
                for m in range(KD):
                    for s_, (lo, hi) in enumerate(STREAMS):
                        last = stt(xT[:, m, lo:hi], acc[:, m, lo:hi], seg(5)[:, m, s_:s_ + 1], xT[:, m, lo:hi], MUL, ADD)
                last.then_inc(S("fb_dve"), 1)
                dve.wait_ge(S("fb_dve"), 3)
            st(v.memset(small[:, 63:64], 0.0), "x_final")
            dve.wait_ge(S("squares_used"), NORM["n3"] + 8)
            mean_square(3, D)
            invert(("root", 4))
            for k in range(KD):
                st(stt(xT[:, k, :], xT[:, k, :], g_fin[:, k:k + 1], rinv[:, :], MUL, MUL), "y_ready", wait=False)
            for g in range(12):
                j, kg = g // 4, g % 4
                n = P if j < 2 else TS
                dve.wait_ge(S("y_turned"), g + 1)
                st(v.tensor_copy(ynat[0:n, j, kg * 512:kg * 512 + 512], bank(4 + g % 4, 512, n)), "y_rows", wait=False)


_INS = ["x_prompt", "x_sample", "c_prompt", "c_sample", "state_conv", "state_ssd", "state_hgrn", "state_s5_re",
        "state_s5_im", "w_ada", "b_ada", "g_mix", "g_ffn", "w_in", "conv_w", "conv_b", "ssd_dt_bias", "ssd_a_log",
        "ssd_d", "ssd_norm_g", "hgrn_lb_raw", "hgrn_norm_g", "s5_lam_re", "s5_lam_im", "s5_log_dt", "s5_b_re",
        "s5_b_im", "s5_c_re", "s5_c_im", "s5_d", "s5_w_glu", "s5_b_glu", "w_out", "w_router_group",
        "b_router_group", "w_router_expert", "b_router_expert", "w_exp_gate", "w_exp_up", "w_exp_down", "g_final"]
_STATES = [("conv", (1, 1, 3, 1280)), ("ssd", (1, 1, 16, 64, 64)), ("hgrn", (1, 1, 4, 128, 128)),
           ("s5re", (1, 1, 32, 64)), ("s5im", (1, 1, 32, 64))]
_OUTS = [("y_prompt", (1, TP, D)), ("y_sample", (1, TS, D))] \
    + [(f"{n}_{s}", shape) for s in "ps" for n, shape in _STATES]


def kernel(**inputs):
    import numpy as _np
    import concourse.bacc as _bacc
    from concourse.bass_utils import run_bass_kernel_spmd as _run

    nc = _bacc.Bacc("TRN2", target_bir_lowering=False, num_devices=1)
    arrays, ins, outs = {}, {}, {}
    for name in _INS:
        x = _np.ascontiguousarray(inputs[name])
        arrays[f"in_{name}"] = x
        ins[name] = nc.dram_tensor(f"in_{name}", x.shape, mybir.dt.from_np(x.dtype), kind="ExternalInput").ap()
    for name, shape in _OUTS:
        outs[name] = nc.dram_tensor(f"out_{name}", shape, F32, kind="ExternalOutput").ap()
    build(nc, ins, outs)
    r = _run(nc, [arrays], core_ids=[0])
    return tuple(r.results[0][f"out_{name}"] for name, _ in _OUTS)
```
